# Optimizing a Trainium2 kernel written in Bass

```python
import jax, jax.numpy as jnp
from jax import lax
import numpy as np
import functools

D_MODEL = 1024
BATCH = 1
SEQ = 256
DEPTH = 1

GRID_W = 64
CTX_LEN = 256
DN_HEADS = 8
DN_HEAD_DIM = 128
DN_WIDTH = DN_HEADS * DN_HEAD_DIM
SHORT_CONV = 5
CHUNK = 64
POOL_GROUPS = 4
POOL_WINDOWS = (2, 4, 8, 16)
POOL_WIDTH = D_MODEL
POOL_GROUP_DIM = POOL_WIDTH // POOL_GROUPS
D_MIX = DN_WIDTH + POOL_WIDTH
PROJ_SIZES = (3 * DN_WIDTH, 4 * DN_HEADS, DN_WIDTH, POOL_WIDTH, POOL_WIDTH)
D_PROJ = sum(PROJ_SIZES)
PROJ_SPLITS = tuple(int(s) for s in np.cumsum(PROJ_SIZES)[:-1])
EPS = 1e-6


def _rms_norm(h, gain):
    hf = h.astype(jnp.float32)
    hf = hf * lax.rsqrt(jnp.mean(hf * hf, axis=-1, keepdims=True) + EPS)
    return hf.astype(h.dtype) * gain

def _l2_norm(h):
    hf = h.astype(jnp.float32)
    hf = hf * lax.rsqrt(jnp.sum(hf * hf, axis=-1, keepdims=True) + EPS)
    return hf.astype(h.dtype)

def _short_conv(u, w):
    k = w.shape[0]
    return lax.conv_general_dilated(
        u, w[:, None, :], window_strides=(1,), padding=[(k // 2, k // 2)],
        dimension_numbers=('NWC', 'WIO', 'NWC'), feature_group_count=u.shape[-1])

def _gated_delta_rule(q, k, v, g, beta, s0):
    out_dtype = v.dtype
    q, k, v, g, beta = (t.astype(jnp.float32) for t in (q, k, v, g, beta))
    bsz, nh, length, dk = q.shape
    dv = v.shape[-1]
    n = length // CHUNK
    q = q * dk ** -0.5
    q, k, v = (t.reshape(bsz, nh, n, CHUNK, -1) for t in (q, k, v))
    g = jnp.cumsum(g.reshape(bsz, nh, n, CHUNK), axis=-1)
    beta = beta.reshape(bsz, nh, n, CHUNK, 1)
    incl = jnp.tril(jnp.ones((CHUNK, CHUNK), bool))
    strict = jnp.tril(jnp.ones((CHUNK, CHUNK), bool), -1)
    decay = jnp.exp(jnp.where(incl, g[..., :, None] - g[..., None, :], -jnp.inf))
    kb = k * beta
    a_mat = jnp.where(strict, jnp.einsum('bhncd,bhnsd->bhncs', kb, k) * decay, 0.0)
    eye = jnp.eye(CHUNK, dtype=jnp.float32)
    rhs = jnp.concatenate([v * beta, kb * jnp.exp(g)[..., None]], axis=-1)
    sol = lax.linalg.triangular_solve(eye + a_mat, rhs, left_side=True, lower=True,
                                      unit_diagonal=True)
    u_c, w_c = sol[..., :dv], sol[..., dv:]
    qk = jnp.einsum('bhncd,bhnsd->bhncs', q, k) * decay
    q_dec = q * jnp.exp(g)[..., None]
    g_last = g[..., -1]
    k_tail = k * jnp.exp(g_last[..., None] - g)[..., None]
    xs = tuple(jnp.moveaxis(t, 2, 0) for t in (u_c, w_c, qk, q_dec, k_tail, g_last))

    def step(state, inp):
        u_i, w_i, qk_i, q_i, k_i, gl_i = inp
        v_new = u_i - jnp.einsum('bhcd,bhdv->bhcv', w_i, state)
        o_i = (jnp.einsum('bhcd,bhdv->bhcv', q_i, state)
               + jnp.einsum('bhcs,bhsv->bhcv', qk_i, v_new))
        state = state * jnp.exp(gl_i)[..., None, None] + jnp.einsum('bhcd,bhcv->bhdv', k_i, v_new)
        return state, o_i

    s_final, o = lax.scan(step, s0.astype(jnp.float32), xs)
    o = jnp.moveaxis(o, 0, 2).reshape(bsz, nh, length, dv)
    return o.astype(out_dtype), s_final

def _window_bounds(n, w):
    idx = jnp.arange(n)
    lo = jnp.clip(idx - w // 2, 0, n)
    hi = jnp.clip(idx - w // 2 + w, 0, n)
    return lo, hi

def _pool_grid(u, w):
    bsz, length, ch = u.shape
    rows = length // GRID_W
    grid = u.reshape(bsz, rows, GRID_W, ch)
    sat = jnp.pad(jnp.cumsum(jnp.cumsum(grid, axis=1), axis=2), ((0, 0), (1, 0), (1, 0), (0, 0)))
    lr, hr = _window_bounds(rows, w)
    lc, hc = _window_bounds(GRID_W, w)
    s_hr, s_lr = sat[:, hr], sat[:, lr]
    box = s_hr[:, :, hc] - s_lr[:, :, hc] - s_hr[:, :, lc] + s_lr[:, :, lc]
    cnt = ((hr - lr)[:, None] * (hc - lc)[None, :]).astype(u.dtype)
    return (box / cnt[None, :, :, None]).reshape(bsz, length, ch)

def _pool_seq(u, w):
    length = u.shape[1]
    cs = jnp.pad(jnp.cumsum(u, axis=1), ((0, 0), (1, 0), (0, 0)))
    lo, hi = _window_bounds(length, w)
    return (cs[:, hi] - cs[:, lo]) / (hi - lo).astype(u.dtype)[None, :, None]

def _pool_mixer(u, grid, pool_w, pool_scale):
    bsz, length, _ = u.shape
    pool = _pool_grid if grid else _pool_seq
    groups = jnp.split(u.astype(jnp.float32), POOL_GROUPS, axis=-1)
    d = jnp.stack([pool(gu, w) - gu for gu, w in zip(groups, POOL_WINDOWS)], axis=2)
    y = jnp.einsum('blgc,gce->blge', d.astype(u.dtype), pool_w).reshape(bsz, length, POOL_WIDTH)
    return y * pool_scale

def _mix(h, shift, scale, grid, s0_f, s0_b, gain, w_in, conv_w, a_log, dt_bias, dn_gain,
         pool_w, pool_scale):
    bsz, length, _ = h.shape
    hn = _rms_norm(h, gain) * (1 + scale) + shift
    proj = jnp.einsum('bld,dp->blp', hn, w_in)
    qkv, ab, z_dn, u_pool, z_pool = jnp.split(proj, PROJ_SPLITS, axis=-1)
    qkv = jax.nn.silu(_short_conv(qkv, conv_w))
    q, k, v = (t.reshape(bsz, length, DN_HEADS, DN_HEAD_DIM).transpose(0, 2, 1, 3)
               for t in jnp.split(qkv, 3, axis=-1))
    q, k = _l2_norm(q), _l2_norm(k)
    ab = ab.astype(jnp.float32).reshape(bsz, length, 2, 2, DN_HEADS).transpose(2, 3, 0, 4, 1)
    g = -jnp.exp(a_log.astype(jnp.float32))[:, None, :, None] * jax.nn.softplus(
        ab[0] + dt_bias.astype(jnp.float32)[:, None, :, None])
    beta = jax.nn.sigmoid(ab[1])
    o_f, s_f = _gated_delta_rule(q, k, v, g[0], beta[0], s0_f)
    o_b, s_b = _gated_delta_rule(jnp.flip(q, 2), jnp.flip(k, 2), jnp.flip(v, 2),
                                 jnp.flip(g[1], -1), jnp.flip(beta[1], -1), s0_b)
    o = _rms_norm(o_f + jnp.flip(o_b, 2), dn_gain)
    o = o.transpose(0, 2, 1, 3).reshape(bsz, length, DN_WIDTH) * jax.nn.silu(z_dn)
    y_pool = _pool_mixer(u_pool, grid, pool_w, pool_scale) * jax.nn.silu(z_pool)
    return jnp.concatenate([o, y_pool], axis=-1), s_f, s_b

def first_inputs(seed: int = 0) -> dict:
    key = jax.random.key(seed)
    ks = jax.random.split(key, 20)
    f32 = jnp.float32
    nrm = lambda k, shape, s: jax.random.normal(k, shape, f32) * s
    a_init = jnp.log(jax.random.uniform(ks[10], (DEPTH, 2, DN_HEADS), f32, 1.0, 16.0))
    dt = jnp.exp(jax.random.uniform(ks[11], (DEPTH, 2, DN_HEADS), f32,
                                    float(np.log(1e-3)), float(np.log(1e-1))))
    dt_bias = dt + jnp.log(-jnp.expm1(-dt))
    return {
        "x": nrm(ks[0], (BATCH, SEQ, D_MODEL), 1.0),
        "c": nrm(ks[1], (BATCH, D_MODEL), 1.0),
        "ctx": nrm(ks[2], (BATCH, CTX_LEN, D_MODEL), 1.0),
        "c_ctx": nrm(ks[3], (D_MODEL,), 1.0),
        "w_mod": nrm(ks[4], (DEPTH, D_MODEL, 3 * D_MODEL), D_MODEL ** -0.5),
        "b_mod": nrm(ks[5], (DEPTH, 3 * D_MODEL), 0.01),
        "norm_gain": 1.0 + nrm(ks[6], (DEPTH, D_MODEL), 0.1),
        "w_in": nrm(ks[7], (DEPTH, D_MODEL, D_PROJ), D_MODEL ** -0.5),
        "conv_w": nrm(ks[8], (DEPTH, SHORT_CONV, 3 * DN_WIDTH), SHORT_CONV ** -0.5),
        "a_log": a_init,
        "dt_bias": dt_bias,
        "dn_norm_gain": 1.0 + nrm(ks[12], (DEPTH, DN_HEAD_DIM), 0.1),
        "pool_w": nrm(ks[13], (DEPTH, POOL_GROUPS, POOL_GROUP_DIM, POOL_GROUP_DIM),
                       POOL_GROUP_DIM ** -0.5),
        "pool_scale": 1.0 + nrm(ks[14], (DEPTH, POOL_WIDTH), 0.1),
        "w_out": nrm(ks[15], (DEPTH, D_MIX, D_MODEL), D_MIX ** -0.5),
        "final_gain": 1.0 + nrm(ks[16], (D_MODEL,), 0.1),
    }

def first_block(x, c, ctx, c_ctx, w_mod, b_mod, norm_gain, w_in, conv_w, a_log, dt_bias,
              dn_norm_gain, pool_w, pool_scale, w_out, final_gain):
    bsz = x.shape[0]
    silu_c = jax.nn.silu(c)
    silu_cc = jax.nn.silu(c_ctx)
    s_zero = jnp.zeros((bsz, DN_HEADS, DN_HEAD_DIM, DN_HEAD_DIM), jnp.float32)
    for layer in range(DEPTH):
        mod_x = (silu_c @ w_mod[layer] + b_mod[layer])[:, None, :]
        shift_x, scale_x, gate_x = jnp.split(mod_x, 3, axis=-1)
        mod_c = silu_cc @ w_mod[layer] + b_mod[layer]
        shift_c, scale_c, gate_c = jnp.split(mod_c, 3, axis=-1)
        params = (norm_gain[layer], w_in[layer], conv_w[layer], a_log[layer], dt_bias[layer],
                  dn_norm_gain[layer], pool_w[layer], pool_scale[layer])
        y_ctx, s_f, s_b = _mix(ctx, shift_c, scale_c, False, s_zero, s_zero, *params)
        y_x, _, _ = _mix(x, shift_x, scale_x, True, s_f, s_b, *params)
        x = x + gate_x * jnp.einsum('blm,md->bld', y_x, w_out[layer])
        if layer < DEPTH - 1:
            ctx = ctx + gate_c * jnp.einsum('blm,md->bld', y_ctx, w_out[layer])
    return _rms_norm(x, final_gain)


DEPTH_2 = 2

N_MIXERS = 2
N_A = (DEPTH_2 + 1) // 2
N_B = DEPTH_2 // 2
N_MOD = 9
D_FF = 2816
CONV_DIM = D_MODEL
CONV_W = 3
MLA_HEADS = 8
QK_NOPE = 128
QK_ROPE = 64
QK_HEAD = QK_NOPE + QK_ROPE
V_HEAD = 128
Q_LORA = 256
KV_LORA = 128
ROPE_BASE = 10000.0
QK_SCALE = QK_HEAD ** -0.5
Q_BLOCK = 128


def rms_norm(x, g):
    xf = x.astype(jnp.float32)
    y = xf * lax.rsqrt(jnp.mean(xf * xf, axis=-1, keepdims=True) + EPS)
    return (y * g.astype(jnp.float32)).astype(x.dtype)

def adaln_chunks(cond, w_mod, b_mod):
    m = jax.nn.silu(cond) @ w_mod + b_mod
    return jnp.split(m[:, None, :], N_MOD, axis=-1)

def pre(h, g, shift, scale):
    return rms_norm(h, g) * (1 + scale) + shift

def swiglu(h, w1, w3, w2):
    return (jax.nn.silu(h @ w1) * (h @ w3)) @ w2

def conv3_centred(u, w):
    return lax.conv_general_dilated(
        u, w[:, None, :].astype(u.dtype), window_strides=(1,), padding=((1, 1),),
        dimension_numbers=("NWC", "WIO", "NWC"), feature_group_count=u.shape[-1])

def short_conv_mixer(h, w_in, conv_w, w_out):
    b_gate, c_gate, u = jnp.split(h @ w_in, 3, axis=-1)
    return (b_gate * conv3_centred(c_gate * u, conv_w)) @ w_out

def axial_rope_tables(n):
    rows = n // GRID_W
    r = jnp.broadcast_to(jnp.arange(rows)[:, None], (rows, GRID_W)).reshape(n).astype(jnp.float32)
    col = jnp.broadcast_to(jnp.arange(GRID_W)[None, :], (rows, GRID_W)).reshape(n).astype(jnp.float32)
    n_freq = QK_ROPE // 4
    inv = ROPE_BASE ** (-jnp.arange(n_freq, dtype=jnp.float32) / n_freq)
    ang = jnp.stack([r[:, None] * inv, col[:, None] * inv], axis=1)
    return jnp.cos(ang), jnp.sin(ang)

def apply_axial_rope(t, cos, sin):
    ts = t.reshape(t.shape[:-1] + (2, 2, QK_ROPE // 4))
    x1, x2 = ts[..., 0, :], ts[..., 1, :]
    cos = cos.astype(t.dtype)
    sin = sin.astype(t.dtype)
    y = jnp.stack([x1 * cos - x2 * sin, x1 * sin + x2 * cos], axis=-2)
    return y.reshape(t.shape)

def rope_tail(t, cos, sin):
    return jnp.concatenate([t[..., :QK_NOPE], apply_axial_rope(t[..., QK_NOPE:], cos, sin)], axis=-1)

def mla_down(h, w_a):
    return jnp.split(h @ w_a, [Q_LORA, Q_LORA + KV_LORA], axis=-1)

def mla_queries(cq, g_qa, w_uq, g_q):
    b, n, _ = cq.shape
    q = (rms_norm(cq, g_qa) @ w_uq).reshape(b, n, MLA_HEADS, QK_HEAD)
    return rms_norm(q, g_q).transpose(0, 2, 1, 3)

def mla_keys_values(ckv, k_rope, g_kva, w_ukv, g_k):
    b, n, _ = ckv.shape
    kv = (rms_norm(ckv, g_kva) @ w_ukv).reshape(b, n, MLA_HEADS, QK_NOPE + V_HEAD)
    k_nope, v = jnp.split(kv, [QK_NOPE], axis=-1)
    k_r = jnp.broadcast_to(k_rope[:, :, None, :], (b, n, MLA_HEADS, QK_ROPE))
    k = rms_norm(jnp.concatenate([k_nope, k_r], axis=-1), g_k)
    return k.transpose(0, 2, 1, 3), v.transpose(0, 2, 1, 3)

def softmax_attend(q, k, v):
    s = jnp.einsum("bhqd,bhkd->bhqk", q, k).astype(jnp.float32) * QK_SCALE
    p = jax.nn.softmax(s, axis=-1).astype(v.dtype)
    return jnp.einsum("bhqk,bhkd->bhqd", p, v)

def merge_heads(o):
    b, h, n, d = o.shape
    return o.transpose(0, 2, 1, 3).reshape(b, n, h * d)

def latent_attention(q, k_all, v_all):
    b, h, n, dq = q.shape
    nb = n // Q_BLOCK
    qb = q.reshape(b, h, nb, Q_BLOCK, dq).transpose(2, 0, 1, 3, 4)
    o = lax.map(lambda qblk: softmax_attend(qblk, k_all, v_all), qb)
    return o.transpose(1, 0, 3, 2, 4).reshape(b, n, h * V_HEAD)

def second_inputs(seed: int = 0) -> dict:
    key = jax.random.key(seed)
    ks = jax.random.split(key, 24)
    f32 = jnp.float32

    def nrm(k, shape, scale):
        return jax.random.normal(k, shape, f32) * scale

    def gain(k, shape):
        return 1.0 + 0.1 * jax.random.normal(k, shape, f32)

    D = D_MODEL
    return {
        "x": nrm(ks[0], (BATCH, SEQ, D), 1.0),
        "c": nrm(ks[1], (BATCH, D), 1.0),
        "ctx": nrm(ks[2], (BATCH, CTX_LEN, D), 1.0),
        "c_ctx": nrm(ks[3], (D,), 1.0),
        "w_mod": nrm(ks[4], (DEPTH_2, D, N_MOD * D), 0.5 * D ** -0.5),
        "b_mod": nrm(ks[5], (DEPTH_2, N_MOD * D), 0.02),
        "g_norm": gain(ks[6], (DEPTH_2, 3, D)),
        "ffn_w1": nrm(ks[7], (DEPTH_2, 2, D, D_FF), D ** -0.5),
        "ffn_w3": nrm(ks[8], (DEPTH_2, 2, D, D_FF), D ** -0.5),
        "ffn_w2": nrm(ks[9], (DEPTH_2, 2, D_FF, D), D_FF ** -0.5),
        "sc_w_in": nrm(ks[10], (N_A, D, 3 * CONV_DIM), D ** -0.5),
        "sc_conv": nrm(ks[11], (N_A, CONV_W, CONV_DIM), CONV_W ** -0.5),
        "sc_w_out": nrm(ks[12], (N_A, CONV_DIM, D), CONV_DIM ** -0.5),
        "mla_w_a": nrm(ks[13], (N_B, D, Q_LORA + KV_LORA + QK_ROPE), D ** -0.5),
        "mla_g_qa": gain(ks[14], (N_B, Q_LORA)),
        "mla_w_uq": nrm(ks[15], (N_B, Q_LORA, MLA_HEADS * QK_HEAD), Q_LORA ** -0.5),
        "mla_g_kva": gain(ks[16], (N_B, KV_LORA)),
        "mla_w_ukv": nrm(ks[17], (N_B, KV_LORA, MLA_HEADS * (QK_NOPE + V_HEAD)), KV_LORA ** -0.5),
        "mla_g_q": gain(ks[18], (N_B, QK_HEAD)),
        "mla_g_k": gain(ks[19], (N_B, QK_HEAD)),
        "mla_w_o": nrm(ks[20], (N_B, MLA_HEADS * V_HEAD, D), (MLA_HEADS * V_HEAD) ** -0.5),
    }

def second_block(x, c, ctx, c_ctx, w_mod, b_mod, g_norm, ffn_w1, ffn_w3, ffn_w2,
              sc_w_in, sc_conv, sc_w_out, mla_w_a, mla_g_qa, mla_w_uq, mla_g_kva,
              mla_w_ukv, mla_g_q, mla_g_k, mla_w_o):
    n = x.shape[1]
    cos, sin = axial_rope_tables(n)
    h_x, h_c = x, ctx
    for i in range(DEPTH_2):
        kind, j = i % N_MIXERS, i // N_MIXERS
        last = i == DEPTH_2 - 1
        run_ctx_in = (not last) or kind == 1
        run_ctx_out = not last

        mx = adaln_chunks(c, w_mod[i], b_mod[i])
        mc = adaln_chunks(c_ctx[None], w_mod[i], b_mod[i])
        ffn1 = functools.partial(swiglu, w1=ffn_w1[i, 0], w3=ffn_w3[i, 0], w2=ffn_w2[i, 0])
        ffn2 = functools.partial(swiglu, w1=ffn_w1[i, 1], w3=ffn_w3[i, 1], w2=ffn_w2[i, 1])

        h_x = h_x + 0.5 * mx[2] * ffn1(pre(h_x, g_norm[i, 0], mx[0], mx[1]))
        if run_ctx_in:
            h_c = h_c + 0.5 * mc[2] * ffn1(pre(h_c, g_norm[i, 0], mc[0], mc[1]))

        nx = pre(h_x, g_norm[i, 1], mx[3], mx[4])
        if kind == 0:
            ox = short_conv_mixer(nx, sc_w_in[j], sc_conv[j], sc_w_out[j])
            if run_ctx_out:
                nc = pre(h_c, g_norm[i, 1], mc[3], mc[4])
                oc = short_conv_mixer(nc, sc_w_in[j], sc_conv[j], sc_w_out[j])
        else:
            nc = pre(h_c, g_norm[i, 1], mc[3], mc[4])
            cq_c, ckv_c, kr_c = mla_down(nc, mla_w_a[j])
            k_c, v_c = mla_keys_values(ckv_c, kr_c, mla_g_kva[j], mla_w_ukv[j], mla_g_k[j])
            cq_x, ckv_x, kr_x = mla_down(nx, mla_w_a[j])
            k_x, v_x = mla_keys_values(ckv_x, kr_x, mla_g_kva[j], mla_w_ukv[j], mla_g_k[j])
            k_x = rope_tail(k_x, cos, sin)
            q_x = rope_tail(mla_queries(cq_x, mla_g_qa[j], mla_w_uq[j], mla_g_q[j]), cos, sin)
            k_all = jnp.concatenate([k_c, k_x], axis=2)
            v_all = jnp.concatenate([v_c, v_x], axis=2)
            ox = latent_attention(q_x, k_all, v_all) @ mla_w_o[j]
            if run_ctx_out:
                q_c = mla_queries(cq_c, mla_g_qa[j], mla_w_uq[j], mla_g_q[j])
                oc = merge_heads(softmax_attend(q_c, k_c, v_c)) @ mla_w_o[j]
        h_x = h_x + mx[5] * ox
        if run_ctx_out:
            h_c = h_c + mc[5] * oc

        h_x = h_x + 0.5 * mx[8] * ffn2(pre(h_x, g_norm[i, 2], mx[6], mx[7]))
        if run_ctx_out:
            h_c = h_c + 0.5 * mc[8] * ffn2(pre(h_c, g_norm[i, 2], mc[6], mc[7]))
    return h_x


def setup_inputs(seed=0):
    out = dict(first_inputs(seed))
    for name, value in second_inputs(seed + 1).items():
        if name != "x":
            out[name + "_2"] = value
    return out


def reference(
    x, c, ctx, c_ctx, w_mod, b_mod, norm_gain, w_in, conv_w, a_log, dt_bias, dn_norm_gain,
    pool_w, pool_scale, w_out, final_gain, c_2, ctx_2, c_ctx_2, w_mod_2, b_mod_2, g_norm_2,
    ffn_w1_2, ffn_w3_2, ffn_w2_2, sc_w_in_2, sc_conv_2, sc_w_out_2, mla_w_a_2, mla_g_qa_2,
    mla_w_uq_2, mla_g_kva_2, mla_w_ukv_2, mla_g_q_2, mla_g_k_2, mla_w_o_2,
):
    x = first_block(
        x, c, ctx, c_ctx, w_mod, b_mod, norm_gain, w_in, conv_w, a_log, dt_bias, dn_norm_gain,
        pool_w, pool_scale, w_out, final_gain,
    )
    return second_block(
        x, c_2, ctx_2, c_ctx_2, w_mod_2, b_mod_2, g_norm_2, ffn_w1_2, ffn_w3_2, ffn_w2_2,
        sc_w_in_2, sc_conv_2, sc_w_out_2, mla_w_a_2, mla_g_qa_2, mla_w_uq_2, mla_g_kva_2,
        mla_w_ukv_2, mla_g_q_2, mla_g_k_2, mla_w_o_2,
    )


_drawn_inputs = setup_inputs


def setup_inputs(seed=0):
    import zlib

    import numpy as np

    out = dict(_drawn_inputs(seed))
    spreads = {}
    factors = {'b_mod': 4.547,
     'ctx_2': 4.112,
     'mla_g_qa_2': 8.0,
     'mla_g_kva_2': 6.451,
     'mla_g_q_2': 8.0,
     'mla_g_k_2': 8.0}
    for name, (base, spread) in spreads.items():
        noise = np.random.default_rng([zlib.crc32(name.encode()), seed]).standard_normal(out[name].shape)
        drawn = base * np.exp(spread * noise) if base else spread * noise
        out[name] = __import__('jax').numpy.asarray(drawn.astype(out[name].dtype))
    for name, factor in factors.items():
        out[name] = (out[name] * factor).astype(out[name].dtype)
    return out
```

```python
from contextlib import ExitStack

import numpy as np

import concourse.bass as bass
from concourse import mybir

F32 = mybir.dt.float32
F32R = mybir.dt.float32r
ACT = mybir.ActivationFunctionType
ALU = mybir.AluOpType
AX_X = mybir.AxisListType.X

P = 128
D = 1024
KT = D // P
L = 256
T = 2 * L
HEADS = 8
FF = 2816
FT = FF // P
HALF = FT // 2
EPS = 1e-6
CONV = 5
GRID_W = 64
ROWS = L // GRID_W
WINDOWS = (2, 4, 8, 16)
NOPE, ROPE = 128, 64
QK_HEAD = NOPE + ROPE
TILES_PER_CHUNK = 8
CHUNK = TILES_PER_CHUNK * P
RING = 3
BANKS = 6
MOD_BANK, MISC_BANK = 6, 7

CH_IN = 0
N_IN = 51
CH_OUT = CH_IN + N_IN
N_OUT = 16
N_FFN = 2 * (2 * HALF + HALF * KT // TILES_PER_CHUNK)
CH_FFN = [CH_OUT + N_OUT, 0, 0, 0]
CH_SC = CH_FFN[0] + N_FFN
N_SC = 32
CH_FFN[1] = CH_SC + N_SC
CH_FFN[2] = CH_FFN[1] + N_FFN
CH_MLA = CH_FFN[2] + N_FFN
N_MLA = 17
CH_FFN[3] = CH_MLA + N_MLA
N_CHUNKS = CH_FFN[3] + N_FFN
AHEAD = 2
N_STREAM = N_CHUNKS + AHEAD

OUT_ORDER = list(range(8, 16)) + list(range(8))

MOD_COLS = 2048
MOD_GROUPS = 11
MOD_TILES = MOD_COLS // P
MOD_PARTS = 2 * KT
M_SHIFT, M_SCALE, M_GATE = 0, 8, 16


def mod2(layer, vector):
    return 24 + 72 * layer + 8 * vector


class Cols:
    NORM_GAIN = 0
    FINAL_GAIN = 8
    G_NORM = 16
    POOL_SCALE = 64
    DN_GAIN = 72
    CONV = 73
    SC_CONV = 193
    G_QA = 217
    G_KVA = 219
    G_Q = 220
    G_K = 222
    A_LOG = 224
    DT_BIAS = 225
    BIAS = 226
    SEL = 226 + MOD_GROUPS * MOD_TILES
    N = SEL + 15


class Const:
    IDENT, ONES = range(2)
    INCL = (2, 3)
    STRICT = (4, 5)
    LEVEL = (6, 13)
    N = 20


class Rope:
    COS, SIN, ONES_LO, ONES_HI, PERM, N = 0, L, 2 * L, 2 * L + P, 2 * L + 2 * P, 2 * L + 3 * P


LEVELS = (1, 2, 4, 8, 16, 32, 64)
FWD, BWD = 0, 1


MOVING_CHUNK = "moving"


def mark_plan():
    stages = {}
    before = [0] * (N_CHUNKS + 1)
    groups_before = {}
    count = groups = 0

    def stage(name, first_chunk, sizes):
        nonlocal count, groups
        groups_before[name] = groups
        done = []
        tile = first_chunk * TILES_PER_CHUNK
        for n in sizes:
            if n == MOVING_CHUNK:
                before[tile // TILES_PER_CHUNK] = count
                tile += TILES_PER_CHUNK
                for _ in range(8):
                    count += 1
                    done.append(count)
                groups += 7
                continue
            for j in range(n):
                if tile % TILES_PER_CHUNK == 0:
                    before[tile // TILES_PER_CHUNK] = count
                tile += 1
                if tile % TILES_PER_CHUNK == 0 or j == n - 1:
                    count += 1
            done.append(count)
        groups += len(sizes)
        stages[name] = done

    stage("in", CH_IN, [8] * 25 + [8] * 4 + [2] * 4 + [8] * 4 + [2] * 4 + [8] * 16)
    stage("out", CH_OUT, [16] * 8)
    for n in range(4):
        if n == 1:
            stage("sc", CH_SC, [8] * 32)
        if n == 3:
            stage("mla", CH_MLA, [8] * 4 + [2] * 12 + [1] * 8 + [MOVING_CHUNK] + [8] * 8)
        for half in range(2):
            stage(("ffn", n, half), CH_FFN[n] + half * N_FFN // 2, [8] * (2 * HALF) + [HALF] * KT)
    before[N_CHUNKS] = count
    return before, stages, groups_before


CHUNK_BEFORE, GROUP_DONE, GROUPS_BEFORE = mark_plan()


def two_block_kernel(nc, stream, modstream, tokens, ctx2, conds, cols_in, consts_in, rope_tab, count_in, out):
    ctx = ExitStack()

    def sem(name):
        return ctx.enter_context(nc.semaphore(name))

    class Scope:

        def __enter__(self):
            self.stack = ExitStack()
            return self

        def __exit__(self, *_):
            self.stack.close()

        def __call__(self, name, shape, dt=F32):
            return self.stack.enter_context(nc.sbuf_tensor(name, shape, dt))

    def sb(name, shape, dt=F32):
        return ctx.enter_context(nc.sbuf_tensor(name, shape, dt))

    h = sb("h", [P, KT, T])
    w_raw = sb("w_raw", [P, RING, CHUNK])
    w_hi = sb("w_hi", [P, RING, CHUNK], F32R)
    w_lo = sb("w_lo", [P, RING, CHUNK], F32R)
    cols = sb("cols", [P, Cols.N])
    mods = sb("mods", [P, MOD_GROUPS * MOD_TILES, 2])
    consts = sb("consts", [P, Const.N, P])
    gains = sb("gains", [P, 7, KT, 2])
    gates = sb("gates", [P, 6, KT, 2])

    with Scope() as s:
        n_hi = s("n_hi", [P, KT, T], F32R)
        n_lo = s("n_lo", [P, KT, T], F32R)
    gdn_names = ["diff", "dec", "a", "at", "xm", "xt", "t1", "rhs", "vnew", "pt", "qdec", "ktok"]
    W = [{}, {}]
    with Scope() as s:
        for d in (FWD, BWD):
            for name in gdn_names[:8]:
                W[d][name] = s(f"gdn_{name}{d}", [P, 4, P])
    sb("n_space", [P, 2, KT, T])

    with Scope() as s:
        kT = s("kT", [P, HEADS, T])
        qT = s("qT", [P, HEADS, L])
        v_tok = s("v_tok", [P, 4, HEADS, P])
        z_dn = s("z_dn", [P, HEADS, L])
        y_pool = s("y_pool", [P, KT, L])
        mod_raw = s("mod_raw", [P, 3, CHUNK])
        mod_row = s("mod_row", [P, 512])
        cond = s("cond", [P, 2, KT, 32])
        gb = s("gb", [64, T])
        gb_tok = s("gb_tok", [P, 4, 64])
        cum = s("cum", [P, 4, 16])
        e_cum = s("e_cum", [P, 4, 16])
        be_cum = s("be_cum", [P, 4, 16])
        tot = s("tot", [P, 4, 16])
        e_tot = s("e_tot", [P, 4, 16])
        e_tail = s("e_tail", [P, 4, 16])
        log_a = s("log_a", [16, 1])
        with Scope() as s2:
            pad = s2("pad", [P, 2, 2, L + CONV - 1])
            conv = s2("conv", [P, 2, T])
            act_out = s2("act_out", [P, 2, T])
            upad = s2("upad", [P, 2, ROWS, GRID_W + 16])
            box = s2("box", [P, 2, ROWS, GRID_W + 16])
            boxr = s2("boxr", [P, 2, ROWS, GRID_W])
            u_hi = s2("u_hi", [P, 4, L], F32R)
            u_lo = s2("u_lo", [P, 4, L], F32R)
            inv_cnt = s2("inv_cnt", [P, 4, GRID_W])
            rk = s2("rk", [HEADS, T])
            rq = s2("rq", [HEADS, L])
        with Scope() as s2:
            for d in (FWD, BWD):
                for name in gdn_names[8:]:
                    W[d][name] = s2(f"gdn_{name}{d}", [P, 4, P])
            state = s2("state", [P, 2, HEADS, P])
            o_sum = s2("o_sum", [P, HEADS, L])
    with Scope() as s:
        nt = s("nt", [P, 2, T])
        sq_acc = s("sq_acc", [P, T])
        rstd = s("rstd", [P, T])
        with Scope() as s2:
            g_hi = s2("g_hi", [P, HALF, T], F32R)
            g_lo = s2("g_lo", [P, HALF, T], F32R)
            silu = s2("silu", [P, 2, T])
            prod = s2("prod", [P, 2, T])
            sc_pad = s2("sc_pad", [P, 2, 2, L + 2])
            sc_conv = s2("sc_conv", [P, T])
        with Scope() as s2:
            cq = s2("cq", [P, 2, L])
            ckv = s2("ckv", [P, T])
            kr = s2("kr", [P, T])
            kr_rot = s2("kr_rot", [P, T])
            a_sq = s2("a_sq", [P, 3, T])
            a_rstd = s2("a_rstd", [P, 2, T])
            c_hi = s2("c_hi", [P, 3, T], F32R)
            c_lo = s2("c_lo", [P, 3, T], F32R)
            q_nope = s2("q_nope", [P, HEADS, L])
            q_rope = s2("q_rope", [P, HEADS, L])
            k_nope = s2("k_nope", [P, HEADS, T])
            k_rope = s2("k_rope", [P, HEADS // 2, T])
            v_att = s2("v_att", [P, 4, HEADS, P])
            probs = s2("probs", [P, 2, T])
            probs_t = s2("probs_t", [P, 4, L])
            rot = s2("rot", [P, 2, L])
            smax = s2("smax", [P, 2])
            ssum = s2("ssum", [P, 2])
            rope = s2("rope", [P, Rope.N])

    bank = [ctx.enter_context(nc.psum_tensor(f"bank{b}", [P, 512], F32)) for b in range(8)]

    raw_full = [sem(f"raw_full{i}") for i in range(RING)]
    mod_full = [sem(f"mod_full{i}") for i in range(3)]
    const_in = sem("const_in")
    tokens_in = sem("tokens_in")
    ctx2_in = sem("ctx2_in")
    rope_in_sem = sem("rope_in")
    out_done = sem("out_done")
    w_hi_ready = sem("w_hi_ready")
    w_lo_ready = sem("w_lo_ready")
    linear_done = sem("linear_done")
    groups_read = sem("groups_read")
    cond_ready = sem("cond_ready")
    mod_used = sem("mod_used")
    mod_copied = sem("mod_copied")
    mod_turned = sem("mod_turned")
    mod_ready = sem("mod_ready")
    gains_ready = sem("gains_ready")
    sq_ready = sem("sq_ready")
    sum_ready = sem("sum_ready")
    ms_ready = sem("ms_ready")
    rstd_ready = sem("rstd_ready")
    scaled = sem("scaled")
    norm_hi = sem("norm_hi")
    normed = sem("normed")
    gate_ready = sem("gate_ready")
    hid_hi = sem("hid_hi")
    hid_lo = sem("hid_lo")
    dve_step = sem("dve_step")
    dve_count = [0]
    dve_loop = [0]

    def C(i, rows=P):
        return consts[0:rows, i, :]

    def col(i, n=1):
        return cols[:, i:i + n]

    def step(ins):
        dve_count[0] += 1
        ins.then_inc(dve_step, 1)
        nc.vector.wait_ge(dve_step, dve_loop[0] + dve_count[0])

    def load_chunk(sp, i, slot):
        sp.dma_start(w_raw[:, slot, :], stream[i]).then_inc(raw_full[slot], 16)

    def load_mod(sp, m, slot):
        sp.dma_start(mod_raw[:, slot, :], modstream[m]).then_inc(mod_full[slot], 16)

    def stream_loads(sp, first, last):
        while first < last and first % RING:
            sp.wait_ge(w_lo_ready, first - RING + 1)
            load_chunk(sp, first, first % RING)
            first += 1
        rounds = (last - first) // RING
        if rounds > 0:
            with sp.Fori(0, rounds) as r:
                for s_ in range(RING):
                    sp.wait_ge(w_lo_ready, r * RING + (first + s_ - RING + 1))
                    load_chunk(sp, r * RING + (first + s_), s_)
            first += rounds * RING
        while first < last:
            sp.wait_ge(w_lo_ready, first - RING + 1)
            load_chunk(sp, first, first % RING)
            first += 1

    MOD_EARLY = 2 * MOD_PARTS
    MOD_ALL = MOD_GROUPS * MOD_PARTS
    AFTER_IN = N_IN + AHEAD + RING

    def sp_program(sp):
        sp.dma_start(cols[:], cols_in[:]).then_inc(const_in, 16)
        sp.dma_start(cond[:], conds[:]).then_inc(const_in, 16)
        for m in range(3):
            load_mod(sp, m, m)
        sp.dma_start(consts[:], consts_in[:]).then_inc(const_in, 16)
        sp.dma_start(inv_cnt[:], count_in[:]).then_inc(const_in, 16)
        sp.dma_start(h[:], tokens[:]).then_inc(tokens_in, 16)
        for m in range(3, MOD_EARLY):
            sp.wait_ge(mod_used, m - 2)
            load_mod(sp, m, m % 3)
        for i in range(RING):
            load_chunk(sp, i, i)
        stream_loads(sp, RING, AFTER_IN)
        sp.wait_ge(normed, KT)
        sp.dma_start(h[:, :, L:T], ctx2[:]).then_inc(ctx2_in, 16)
        with sp.Fori(0, (MOD_ALL - MOD_EARLY) // 3) as r:
            for s_ in range(3):
                sp.wait_ge(mod_used, r * 3 + (MOD_EARLY + s_ - 2))
                load_mod(sp, r * 3 + (MOD_EARLY + s_), (MOD_EARLY + s_) % 3)
        stream_loads(sp, AFTER_IN, N_STREAM)

    def low_half(pool, i, slot):
        pool.wait_ge(w_hi_ready, i + 1)
        nc.gpsimd.tensor_tensor(w_lo[:, slot, :], w_raw[:, slot, :], w_hi[:, slot, :].bitcast(F32),
                                ALU.subtract).then_inc(w_lo_ready, 1)

    def pool_program(pool):
        with pool.Fori(0, N_STREAM // RING) as r:
            for s_ in range(RING):
                low_half(pool, r * RING + s_, s_)
        for i in range(N_STREAM - N_STREAM % RING, N_STREAM):
            low_half(pool, i, i % RING)

    def product3(pe, out_ap, tile, hi, lo, start, stop):
        slot, j = tile // TILES_PER_CHUNK % RING, tile % TILES_PER_CHUNK
        wh, wl = w_hi[:, slot, j * P:(j + 1) * P], w_lo[:, slot, j * P:(j + 1) * P]
        nc.tensor.matmul(out_ap, wl, hi, start=start, stop=False)
        nc.tensor.matmul(out_ap, wh, lo, start=False, stop=False)
        return nc.tensor.matmul(out_ap, wh, hi, start=False, stop=stop)

    def linear(pe, key, sizes, first_chunk, rhs, width, group0=0, chunk_off=0, group_off=0,
               before=None, after=None):
        tile = first_chunk * TILES_PER_CHUNK
        for gi, n in enumerate(sizes):
            g = GROUPS_BEFORE[key] + group0 + gi
            if g >= BANKS:
                pe.wait_ge(groups_read, g - BANKS + 1 + group_off)
            out_ap = bank[g % BANKS][:, 0:width]
            for k in range(n):
                if tile % TILES_PER_CHUNK == 0:
                    pe.wait_ge(w_lo_ready, tile // TILES_PER_CHUNK + 1 + chunk_off)
                if before is not None:
                    before(group0 + gi, k)
                hi, lo = rhs(group0 + gi, k)
                last = product3(pe, out_ap, tile, hi, lo, k == 0, k == n - 1)
                tile += 1
                if tile % TILES_PER_CHUNK == 0 or k == n - 1:
                    last.then_inc(linear_done, 1)
            if after is not None:
                after(group0 + gi)

    def mod_part(pe, m):
        g, q = m // MOD_PARTS, m % MOD_PARTS
        k, half = q // 2, q % 2
        pe.wait_ge(mod_full[m % 3], 16 * (m // 3 + 1))
        if q == 0 and g:
            pe.wait_ge(mod_copied, g)
        for jj in range(2):
            j = 2 * half + jj
            which = 0 if g * MOD_COLS + j * 512 < 3 * D else 1
            last = nc.tensor.matmul(bank[MOD_BANK][32 * j:32 * j + 32, :], cond[:, which, k, :],
                                    mod_raw[:, m % 3, jj * 512:(jj + 1) * 512],
                                    start=(k == 0), stop=(k == KT - 1))
        last.then_inc(mod_used, 1)

    def mod_turn(pe, g, free=None):
        pe.wait_ge(mod_copied, g + 1)
        if g:
            pe.wait_ge(mod_ready, g)
        for b in range(4):
            last = nc.tensor.transpose(bank[MISC_BANK][:, b * P:(b + 1) * P], mod_row[:, b * P:(b + 1) * P],
                                       C(Const.IDENT))
        last.then_inc(mod_turned, 1)

    def act_mod_copy(act, g):
        act.wait_ge(mod_used, MOD_PARTS * (g + 1))
        if g:
            act.wait_ge(mod_turned, g)
        nc.scalar.copy(mod_row[:], bank[MOD_BANK][:]).then_inc(mod_copied, 1)

    def dve_mod_bias(dve, g):
        dve.wait_ge(mod_turned, g + 1)
        turned = bank[MISC_BANK][:].rearrange("p (b j c) -> p j b c", b=4, j=4)[:, :, :, 0:2]
        t0 = g * MOD_TILES
        bias = col(Cols.BIAS + t0, MOD_TILES).rearrange("p (j b) -> p j b", j=4)
        for c in range(2):
            ins = nc.vector.tensor_tensor(
                mods[:, t0:t0 + MOD_TILES, c].rearrange("p (j b) -> p j b", j=4),
                turned[:, :, :, c], bias, ALU.add)
            if c:
                ins.then_inc(mod_ready, 1)

    NORMS = [(Cols.NORM_GAIN, M_SHIFT, M_SCALE)]
    for layer in range(2):
        for v in range(3):
            NORMS.append((Cols.G_NORM + 24 * layer + 8 * v, mod2(layer, 3 * v), mod2(layer, 3 * v + 1)))
    GATES = [(mod2(0, 2), 0.5), (mod2(0, 5), 1.0), (mod2(0, 8), 0.5),
             (mod2(1, 2), 0.5), (mod2(1, 5), 1.0), (mod2(1, 8), 0.5)]

    def dve_gain(dve, i):
        gain, _, scale = NORMS[i]
        for c in range(2):
            last = nc.vector.scalar_tensor_tensor(gains[:, i, :, c], mods[:, scale:scale + KT, c], 1.0,
                                                  col(gain, KT), ALU.add, ALU.mult)
        return last

    def norm_sum(pe, m, width):
        pe.wait_ge(sq_ready, SQ_COUNT[m])
        nc.tensor.matmul(bank[MISC_BANK][:, 0:width], C(Const.ONES), sq_acc[:, 0:width],
                         start=True, stop=True).then_inc(sum_ready, 1)

    def dve_mean_square(dve, m, width):
        dve.wait_ge(sum_ready, m + 1)
        step(nc.vector.tensor_scalar(rstd[:, 0:width], bank[MISC_BANK][:, 0:width], 1.0 / D, EPS,
                                     ALU.mult, ALU.add))
        nc.vector.reciprocal(rstd[:, 0:width], rstd[:, 0:width]).then_inc(ms_ready, 1)

    def act_rstd(act, m, width):
        act.wait_ge(ms_ready, m + 1)
        nc.scalar.activation(rstd[:, 0:width], rstd[:, 0:width], ACT.Sqrt).then_inc(rstd_ready, 1)

    def sides(width):
        return [(0, slice(0, L)), (1, slice(L, T))][:width // L]

    def dve_norm(dve, i, m, width):
        if m:
            dve_mean_square(dve, m, width)
        dve.wait_ge(rstd_ready, m + 1)

        def low(k):
            dve.wait_ge(norm_hi, KT * i + k + 1)
            shift = NORMS[i][1]
            for c, s_ in sides(width):
                last = nc.vector.scalar_tensor_tensor(n_lo[:, k, s_], nt[:, k % 2, s_],
                                                      mods[:, shift + k, c:c + 1],
                                                      n_hi[:, k, s_].bitcast(F32), ALU.add, ALU.subtract)
            last.then_inc(normed, 1)

        for k in range(KT):
            if k >= 2:
                dve.wait_ge(normed, KT * i + k - 1)
            for c, s_ in sides(width):
                last = nc.vector.scalar_tensor_tensor(nt[:, k % 2, s_], h[:, k, s_],
                                                      gains[:, i, k, c:c + 1], rstd[:, s_],
                                                      ALU.mult, ALU.mult)
            last.then_inc(scaled, 1)
            if k:
                low(k - 1)
        low(KT - 1)

    def act_norm(act, i, m, width):
        if m:
            act_rstd(act, m, width)
        shift = NORMS[i][1]
        for k in range(KT):
            act.wait_ge(scaled, KT * i + k + 1)
            for c, s_ in sides(width):
                last = nc.scalar.activation(n_hi[:, k, s_], nt[:, k % 2, s_], ACT.Identity,
                                            bias=mods[:, shift + k, c:c + 1])
            last.then_inc(norm_hi, 1)

    def dve_square(dve, k, width, last_k):
        if k == 0:
            step(nc.vector.tensor_tensor(sq_acc[:, 0:width], h[:, 0, 0:width], h[:, 0, 0:width], ALU.mult))
            return
        step(nc.vector.tensor_tensor(nt[:, 0, 0:width], h[:, k, 0:width], h[:, k, 0:width], ALU.mult))
        ins = nc.vector.tensor_tensor(sq_acc[:, 0:width], sq_acc[:, 0:width], nt[:, 0, 0:width], ALU.add)
        if k == last_k:
            ins.then_inc(sq_ready, 1)
        else:
            step(ins)

    SQ_COUNT = {0: 1}

    def split_ahead(act, i, chunk_off=0, mark_off=0, turn_off=0):
        c = i + AHEAD
        act.wait_ge(raw_full[c % RING], 16 * (c // RING + 1) + turn_off)
        if i >= 1:
            act.wait_ge(linear_done, CHUNK_BEFORE[i] + mark_off)
        nc.scalar.copy(w_hi[:, c % RING, :], w_raw[:, c % RING, :]).then_inc(w_hi_ready, 1)

    def pe_start(pe):
        pe.wait_ge(const_in, 16 * 4)
        norm_sum(pe, 0, T)
        pe.wait_ge(cond_ready, 1)
        for g in range(2):
            for q in range(MOD_PARTS):
                mod_part(pe, g * MOD_PARTS + q)
            if g == 0:
                pe.wait_ge(ms_ready, 1)
            mod_turn(pe, g)

    def act_start(act):
        act.wait_ge(const_in, 16 * 4)
        nc.scalar.activation(cond[:], cond[:], ACT.Silu).then_inc(cond_ready, 1)
        act_rstd(act, 0, T)
        act_mod_copy(act, 0)
        act_mod_copy(act, 1)
        for i in (-2, -1):
            split_ahead(act, i)
        act_norm(act, 0, 0, T)

    def dve_start(dve):
        dve.wait_ge(tokens_in, 16)
        for k in range(KT):
            dve_square(dve, k, T, KT - 1)
        dve_mean_square(dve, 0, T)
        dve.wait_ge(const_in, 16 * 4)
        dve_mod_bias(dve, 0)
        dve_mod_bias(dve, 1)
        dve.wait_ge(mod_ready, 2)
        step(dve_gain(dve, 0))
        dve_norm(dve, 0, 0, T)

    U_GROUP = [25, 26, 27, 28, 33, 34, 35, 36]
    POOL_GROUP = [29, 30, 31, 32, 37, 38, 39, 40]
    ZP_GROUP, ZD_GROUP = 41, 49
    conv_done = sem("conv_done")
    silu_done = sem("silu_done")
    tile_sq = sem("tile_sq")
    tile_used = sem("tile_used")
    vtok_done = sem("vtok_done")
    pads_clear = sem("pads_clear")
    sums_read = sem("sums_read")
    box_done = sem("box_done")
    u_hi_ready = sem("u_hi_ready")
    u_lo_ready = sem("u_lo_ready")
    y_done = sem("y_done")
    kq_ms = sem("kq_ms")
    kq_rstd = sem("kq_rstd")
    kq_bc = sem("kq_bc")
    kq_scaled = sem("kq_scaled")
    ab_sem = sem("ab_sem")
    ab_act = sem("ab_act")
    gb_ready = sem("gb_ready")
    gb_turned = sem("gb_turned")
    gb_tok_ready = sem("gb_tok_ready")
    cum_summed = sem("cum_summed")
    cum_ready = sem("cum_ready")
    cum_exp = sem("cum_exp")
    decay_ready = sem("decay_ready")

    def conv_width(ci):
        return T if ci < 16 else L

    def done_in(g):
        return GROUP_DONE["in"][g]

    def pe_in(pe):
        def before(g, k):
            if g == 0:
                pe.wait_ge(normed, k + 1)

        def post(ci):
            w = conv_width(ci)
            if 8 <= ci < 16:
                pe.wait_ge(silu_done, ci + 1)
                if ci == 8:
                    pe.wait_ge(sums_read, 1)
                else:
                    pe.wait_ge(vtok_done, ci - 8)
                for t in range(4):
                    last = nc.tensor.transpose(bank[MISC_BANK][:, t * P:(t + 1) * P],
                                               act_out[:, ci % 2, t * P:(t + 1) * P], C(Const.IDENT))
            else:
                hd = ci % 8
                pe.wait_ge(tile_sq, ci + 1 if ci < 8 else ci - 7)
                b = MISC_BANK if ci < 8 else MOD_BANK
                last = nc.tensor.matmul(bank[b][0:HEADS, 0:w], col(Cols.SEL + 7 - hd, HEADS),
                                        act_out[:, ci % 2, 0:w], start=(hd == 0), stop=(hd == 7))
            last.then_inc(tile_used, 1)

        def after(g):
            if 0 <= g - 3 < 24:
                post(g - 3)

        def full(g, k):
            return n_hi[:, k, :], n_lo[:, k, :]

        def x_only(g, k):
            return n_hi[:, k, 0:L], n_lo[:, k, 0:L]

        def pooled(g, k):
            d = 2 * (POOL_GROUP.index(g) % 4 // 2) + k
            return u_hi[:, d, :], u_lo[:, d, :]

        def wait_pooled(g, k):
            i = POOL_GROUP.index(g)
            pe.wait_ge(u_lo_ready, 4 * (i // 4) + 2 * (i % 4 // 2) + k + 1)

        linear(pe, "in", [8] * 17, CH_IN, full, T, before=before, after=after)
        linear(pe, "in", [8] * 12, CH_IN + 17, x_only, L, group0=17, after=after)
        linear(pe, "in", [2] * 4, CH_IN + 29, pooled, L, group0=29, before=wait_pooled)
        linear(pe, "in", [8] * 4, CH_IN + 30, x_only, L, group0=33)
        linear(pe, "in", [2] * 4, CH_IN + 34, pooled, L, group0=37, before=wait_pooled)
        linear(pe, "in", [8] * 16, CH_IN + 35, x_only, L, group0=41)
        pe.wait_ge(kq_rstd, 1)
        for j in range(2 * HEADS):
            hd, (src, w) = j % HEADS, ((rk, T), (rq, L))[j // HEADS]
            if j < BANKS:
                pe.wait_ge(groups_read, 57)
            else:
                pe.wait_ge(kq_scaled, j - BANKS + 1)
            nc.tensor.matmul(bank[j % BANKS][:, 0:w], C(Const.IDENT, HEADS)[:, hd:hd + 1].to_broadcast([HEADS, P]),
                             src[:, 0:w], start=True, stop=True).then_inc(kq_bc, 1)
        pe.wait_ge(gb_ready, 1)
        for t in range(4):
            last = nc.tensor.transpose(bank[MISC_BANK][:, t * 64:(t + 1) * 64], gb[:, t * P:(t + 1) * P],
                                       C(Const.IDENT, 64)[:, 0:64])
        last.then_inc(gb_turned, 1)
        pe.wait_ge(gb_tok_ready, 1)
        for d in (FWD, BWD):
            nc.tensor.matmul(bank[MOD_BANK][:, 32 * d:32 * d + 32], C(Const.INCL[d]),
                             gb_tok[:, :, 8 * d:8 * d + 8], start=True, stop=True)
        nc.tensor.matmul(bank[MOD_BANK][:, 64:128], C(Const.ONES), gb_tok[:, :, 0:16],
                         start=True, stop=True).then_inc(cum_summed, 1)

    IN_CHUNK_GROUPS = ([[g] for g in range(29)] + [[29, 30, 31, 32]] + [[g] for g in range(33, 37)]
                       + [[37, 38, 39, 40]] + [[g] for g in range(41, 57)])

    def act_in(act):
        def finish_conv(ci):
            w = conv_width(ci)
            act.wait_ge(conv_done, ci + 1)
            if ci < 8:
                dest = kT[:, ci, :]
            elif ci < 16:
                dest = act_out[:, ci % 2, :]
            else:
                dest = qT[:, ci - 16, :]
            if 8 <= ci < 16:
                act.wait_ge(tile_used, ci - 1)
            nc.scalar.activation(dest, conv[:, ci % 2, 0:w], ACT.Silu).then_inc(silu_done, 1)
            if not 8 <= ci < 16:
                if ci >= 2:
                    act.wait_ge(tile_used, ci - 1)
                act.wait_ge(silu_done, ci + 1)
                nc.scalar.activation(act_out[:, ci % 2, 0:w], dest, ACT.Square).then_inc(tile_sq, 1)

        def u_high(ui):
            act.wait_ge(box_done, ui + 1)
            nc.scalar.copy(u_hi[:, ui % 4, :], boxr[:, ui % 2].rearrange("p r c -> p (r c)")).then_inc(u_hi_ready, 1)

        for i, groups in enumerate(IN_CHUNK_GROUPS):
            split_ahead(act, i)
            for g in groups:
                act.wait_ge(linear_done, done_in(g))
                src = bank[g % BANKS]
                if g == 0:
                    nc.scalar.copy(gb[:], src[0:64, :]).then_inc(groups_read, 1)
                elif g <= 24:
                    ci = g - 1
                    segs = conv_width(ci) // L
                    if ci == 0:
                        act.wait_ge(pads_clear, 2)
                    if ci >= 2:
                        act.wait_ge(conv_done, ci - 1)
                    nc.scalar.copy(pad[:, ci % 2, 0:segs, CONV // 2:CONV // 2 + L],
                                   src[:, 0:segs * L].rearrange("p (a t) -> p a t", a=segs)).then_inc(groups_read, 1)
                    if ci:
                        finish_conv(ci - 1)
                elif g in U_GROUP:
                    ui = U_GROUP.index(g)
                    if ui == 0:
                        finish_conv(23)
                    if ui >= 2:
                        act.wait_ge(u_lo_ready, ui - 1)
                    nc.scalar.copy(upad[:, ui % 2, :, 8:8 + GRID_W],
                                   src[:, 0:L].rearrange("p (r c) -> p r c", r=ROWS)).then_inc(groups_read, 1)
                    if ui % 4:
                        u_high(ui - 1)
                    if ui % 4 == 3:
                        u_high(ui)
                elif g in POOL_GROUP:
                    e = POOL_GROUP.index(g)
                    nc.scalar.activation(y_pool[:, e, :], src[:, 0:L], ACT.Identity,
                                         scale=col(Cols.POOL_SCALE + e)).then_inc(groups_read, 1)
                elif g < ZD_GROUP:
                    z = g - ZP_GROUP
                    if z >= 2:
                        act.wait_ge(y_done, z - 1)
                    else:
                        act.wait_ge(tile_used, 24)
                    nc.scalar.activation(act_out[:, z % 2, 0:L], src[:, 0:L], ACT.Silu).then_inc(groups_read, 1)
                else:
                    nc.scalar.activation(z_dn[:, g - ZD_GROUP, :], src[:, 0:L], ACT.Silu).then_inc(groups_read, 1)
        act.wait_ge(kq_ms, 2)
        nc.scalar.activation(rk[:], rk[:], ACT.Sqrt)
        nc.scalar.activation(rq[:], rq[:], ACT.Sqrt).then_inc(kq_rstd, 1)
        act.wait_ge(ab_sem, 1)
        nc.scalar.activation(act_out[0:16, 0, :], conv[0:16, 0, :], ACT.Exp, scale=-1.0).then_inc(ab_act, 1)
        nc.scalar.activation(gb[32:48, :], gb[32:48, :], ACT.Exp, scale=-1.0).then_inc(ab_act, 1)
        nc.scalar.activation(log_a[:], cols[0:16, Cols.A_LOG:Cols.A_LOG + 1], ACT.Exp).then_inc(ab_act, 1)
        act.wait_ge(ab_act, 3)
        nc.scalar.activation(act_out[0:16, 0, :], act_out[0:16, 0, :], ACT.Ln, bias=1.0).then_inc(ab_act, 1)
        act.wait_ge(cum_ready, 1)
        nc.scalar.activation(e_cum[:], cum[:], ACT.Exp).then_inc(cum_exp, 1)
        nc.scalar.activation(e_tot[:], tot[:], ACT.Exp).then_inc(cum_exp, 1)
        nc.scalar.activation(e_tail[:], e_tail[:], ACT.Exp).then_inc(cum_exp, 1)

    def dve_in(dve):
        nc.vector.memset(pad[:], 0.0).then_inc(pads_clear, 1)
        nc.vector.memset(upad[:], 0.0).then_inc(pads_clear, 1)

        def v_rows(vi):
            dve.wait_ge(tile_used, 8 + vi + 1)
            nc.vector.tensor_copy(v_tok[:, :, vi, :],
                                  bank[MISC_BANK][:].rearrange("p (t d) -> p t d", t=4)).then_inc(vtok_done, 1)

        for ci in range(24):
            segs = conv_width(ci) // L
            dve.wait_ge(groups_read, ci + 2)
            if ci >= 2:
                dve.wait_ge(silu_done, ci - 1)
            acc = conv[:, ci % 2, 0:segs * L].rearrange("p (a t) -> p a t", a=segs)
            for j in range(CONV):
                src, w = pad[:, ci % 2, 0:segs, j:j + L], col(Cols.CONV + ci * CONV + j)
                if j == 0:
                    ins = nc.vector.tensor_scalar(acc, src, w, None, ALU.mult)
                else:
                    ins = nc.vector.scalar_tensor_tensor(acc, src, w, acc, ALU.mult, ALU.add)
                if j < CONV - 1:
                    step(ins)
            ins.then_inc(conv_done, 1)
            if ci == 9:
                dve.wait_ge(tile_used, 8)
                nc.vector.tensor_scalar(rk[:], bank[MISC_BANK][0:HEADS, :], EPS, None, ALU.add).then_inc(sums_read, 1)
            if 10 <= ci < 18:
                v_rows(ci - 10)

        def u_low(ui):
            dve.wait_ge(u_hi_ready, ui + 1)
            nc.vector.tensor_tensor(u_lo[:, ui % 4, :], boxr[:, ui % 2].rearrange("p r c -> p (r c)"),
                                    u_hi[:, ui % 4, :].bitcast(F32), ALU.subtract).then_inc(u_lo_ready, 1)

        def rows_of(w):
            return [(max(0, r - w // 2), min(ROWS, r - w // 2 + w)) for r in range(ROWS)]

        for ui in range(8):
            w = WINDOWS[ui // 2]
            u, a, b = upad[:, ui % 2], box[:, 0], box[:, 1]
            wide = GRID_W + 16
            dve.wait_ge(groups_read, U_GROUP[ui] + 1)
            if ui >= 2:
                dve.wait_ge(u_lo_ready, ui - 1)
            add = lambda o, x, y: step(nc.vector.tensor_tensor(o, x, y, ALU.add))
            add(a[:, :, 1:wide], u[:, :, 0:wide - 1], u[:, :, 1:wide])
            cur, other, lo = a, b, 1
            for reach in (1, 2, 4)[:ui // 2]:
                lo2 = lo + reach
                n = wide - 2 * lo2 + 1
                add(other[:, :, lo2:lo2 + n], cur[:, :, lo2 - reach:lo2 - reach + n],
                    cur[:, :, lo2 + reach:lo2 + reach + n])
                cur, other, lo = other, cur, lo2
            c = cur[:, :, 8:8 + GRID_W]
            r_ = boxr[:, ui % 2]
            if w == 2:
                add(r_[:, 1:4], c[:, 0:3], c[:, 1:4])
                step(nc.vector.tensor_copy(r_[:, 0:1], c[:, 0:1]))
            else:
                e = other[:, 0:3, 8:8 + GRID_W]
                add(e, c[:, 0:3], c[:, 1:4])
                if w == 4:
                    step(nc.vector.tensor_copy(r_[:, 0:1], e[:, 0:1]))
                    add(r_[:, 1:2], e[:, 0:1], c[:, 2:3])
                    add(r_[:, 2:3], e[:, 0:1], e[:, 2:3])
                    add(r_[:, 3:4], c[:, 1:2], e[:, 2:3])
                else:
                    add(r_[:, 0:1], e[:, 0:1], e[:, 2:3])
                    step(nc.vector.tensor_copy(r_[:, 1:4], r_[:, 0:1].to_broadcast([P, 3, GRID_W])))
            step(nc.vector.tensor_tensor(r_, r_, inv_cnt[:, ui // 2].unsqueeze(1).to_broadcast([P, ROWS, GRID_W]),
                                         ALU.mult))
            counts = [b_ - a_ for a_, b_ in rows_of(w)]
            for r in range(ROWS):
                ins = nc.vector.scalar_tensor_tensor(r_[:, r], r_[:, r], 1.0 / counts[r], u[:, r, 8:8 + GRID_W],
                                                     ALU.mult, ALU.subtract)
                if r == ROWS - 1:
                    ins.then_inc(box_done, 1)
                else:
                    step(ins)
            if ui == 0:
                dve.wait_ge(tile_used, 24)
                nc.vector.tensor_scalar(rq[:], bank[MOD_BANK][0:HEADS, 0:L], EPS, float(P), ALU.add, ALU.mult)\
                    .then_inc(sums_read, 1)
            if ui % 4:
                u_low(ui - 1)
            if ui % 4 == 3:
                u_low(ui)
        for z in range(8):
            dve.wait_ge(groups_read, ZP_GROUP + z + 1)
            nc.vector.tensor_tensor(y_pool[:, z, :], y_pool[:, z, :], act_out[:, z % 2, 0:L],
                                    ALU.mult).then_inc(y_done, 1)
        dve.wait_ge(sums_read, 2)
        nc.vector.reciprocal(rk[:], rk[:]).then_inc(kq_ms, 1)
        nc.vector.reciprocal(rq[:], rq[:]).then_inc(kq_ms, 1)
        step(nc.vector.tensor_scalar(gb[0:16, :], gb[0:16, :], cols[0:16, Cols.DT_BIAS:Cols.DT_BIAS + 1], None,
                                     ALU.add))
        nc.vector.scalar_tensor_tensor(conv[0:16, 0, :], gb[0:16, :], -1.0, gb[0:16, :],
                                       ALU.mult, ALU.max).then_inc(ab_sem, 1)
        for j in range(2 * HEADS):
            dest, w = (kT, T) if j < HEADS else (qT, L)
            dve.wait_ge(kq_bc, j + 1)
            nc.vector.tensor_tensor(dest[:, j % HEADS, :], dest[:, j % HEADS, :], bank[j % BANKS][:, 0:w],
                                    ALU.mult).then_inc(kq_scaled, 1)
        dve.wait_ge(ab_act, 4)
        step(nc.vector.scalar_tensor_tensor(gb[0:16, :], gb[0:16, :], 0.0, act_out[0:16, 0, :], ALU.max, ALU.add))
        step(nc.vector.tensor_scalar(gb[0:16, :], gb[0:16, :], log_a[:], -1.0, ALU.mult, ALU.mult))
        step(nc.vector.tensor_scalar(gb[32:48, :], gb[32:48, :], 1.0, None, ALU.add))
        nc.vector.reciprocal(gb[32:48, :], gb[32:48, :]).then_inc(gb_ready, 1)
        dve.wait_ge(gb_turned, 1)
        nc.vector.tensor_copy(gb_tok[:].rearrange("p t r -> p (t r)"), bank[MISC_BANK][:, 0:256]).then_inc(gb_tok_ready, 1)
        dve.wait_ge(cum_summed, 1)
        for d in (FWD, BWD):
            step(nc.vector.tensor_copy(cum[:, :, 8 * d:8 * d + 8],
                                       bank[MOD_BANK][:, 32 * d:32 * d + 32].rearrange("p (t g) -> p t g", t=4)))
        step(nc.vector.tensor_copy(tot[:], bank[MOD_BANK][:, 64:128].rearrange("p (t g) -> p t g", t=4)))
        nc.vector.tensor_tensor(e_tail[:], tot[:], cum[:], ALU.subtract).then_inc(cum_ready, 1)
        dve.wait_ge(cum_exp, 3)
        step(nc.vector.tensor_tensor(be_cum[:], e_cum[:], gb_tok[:, :, 32:48], ALU.mult))

    TILE_ORDER = ((2, 3, 0, 1), (3, 2, 1, 0))
    ROUNDS = [(step_, hg) for step_ in range(4) for hg in range(2)]
    g_cb, g_gram, g_kt, g_qk, g_at, g_p1, g_p2, g_p3, g_ks, g_vn, g_o, g_st = (
        sem(f"g_{n}") for n in ("cb", "gram", "kt", "qk", "at", "p1", "p2", "p3", "ks", "vn", "o", "st"))
    a_dec, a_pt, a_qd, a_kt, a_at, a_vn = (sem(f"a_{n}") for n in ("dec", "pt", "qd", "kt", "at", "vn"))
    d_diff, d_max, d_min, d_a, d_pt, d_qd, d_t1, d_xm, d_xt, d_rhs, d_vdec, d_state, d_o = (
        sem(f"d_{n}") for n in ("diff", "max", "min", "a", "pt", "qd", "t1", "xm", "xt", "rhs", "vdec",
                                "state", "o"))
    X_BATCH0 = 8

    def b4(b):
        return bank[b][:].rearrange("p (j c) -> p j c", j=4)

    def per_batch(r):
        step_, hg = ROUNDS[r]
        return [(2 * r + d, d, TILE_ORDER[d][step_], slice(4 * hg, 4 * hg + 4), 3 * d,
                 slice(8 * d + 4 * hg, 8 * d + 4 * hg + 4)) for d in (FWD, BWD)]

    def tok(t):
        return slice(t * P, (t + 1) * P)

    def nth(per, r, e, d):
        return 2 * per * r + 2 * e + d + 1

    def pe_recur(pe):
        parts = [MOD_EARLY]

        def some_mods(n):
            for _ in range(n):
                mod_part(pe, parts[0])
                parts[0] += 1

        def four(fn, s_):
            for j in range(4):
                last = fn(j)
            last.then_inc(s_, 1)

        pe.wait_ge(kq_scaled, 2 * HEADS)
        pe.wait_ge(cum_ready, 1)
        for r, (step_, hg) in enumerate(ROUNDS):
            batches = per_batch(r)
            with_x = step_ >= 2
            for n, d, t, hs, b0, gc in batches:
                w = W[d]
                if n >= 2:
                    pe.wait_ge(d_xt, nth(7, r - 1, 6, d))
                    if n - 2 >= X_BATCH0:
                        pe.wait_ge(d_o, n - 1 - X_BATCH0)
                    if ROUNDS[r - 1][0] < 3:
                        pe.wait_ge(d_state, n - 1)
                    if n - 2 >= X_BATCH0:
                        pe.wait_ge(a_vn, n - 1 - X_BATCH0)
                    pe.wait_ge(d_vdec, n - 1)
                four(lambda j: nc.tensor.matmul(
                    b4(b0)[:, j], gb_tok[:, t, gc][:, j:j + 1].to_broadcast([P, P]), C(Const.INCL[d]),
                    start=True, stop=True), g_cb)
                four(lambda j: nc.tensor.matmul(
                    b4(b0 + 1)[:, j], kT[:, hs, tok(t)][:, j], kT[:, hs, tok(t)][:, j],
                    start=True, stop=True), g_gram)
                four(lambda j: nc.tensor.transpose(b4(b0 + 2)[:, j], kT[:, hs, tok(t)][:, j],
                                                   C(Const.IDENT)), g_kt)
            if r:
                mod_turn(pe, r + 1)
            some_mods(2)
            for n, d, t, hs, b0, gc in batches:
                w = W[d]
                if with_x:
                    pe.wait_ge(a_kt, n + 1)
                    four(lambda j: nc.tensor.matmul(
                        b4(b0 + 2)[:, j], kT[:, hs, tok(t)][:, j], qT[:, hs, tok(t)][:, j],
                        start=True, stop=True), g_qk)
                pe.wait_ge(d_a, n + 1)
                if with_x:
                    pe.wait_ge(a_qd, n - X_BATCH0 + 1)
                four(lambda j: nc.tensor.transpose(b4(b0)[:, j], w["a"][:, j], C(Const.IDENT)), g_at)
            for li in range(1, 7):
                for n, d, t, hs, b0, gc in batches:
                    w = W[d]
                    if li == 1:
                        pe.wait_ge(a_at, n + 1)
                    pe.wait_ge(d_xm, nth(6, r, li - 1, d))
                    four(lambda j: nc.tensor.matmul(b4(b0 + 1)[:, j], w["at"][:, j], w["xm"][:, j],
                                                    start=True, stop=True), g_p1)
                some_mods(2)
                for n, d, t, hs, b0, gc in batches:
                    w = W[d]
                    pe.wait_ge(d_t1, nth(6, r, li - 1, d))
                    pe.wait_ge(d_xt, nth(7, r, li - 1, d))
                    if li == 1:
                        if with_x:
                            pe.wait_ge(d_pt, n - X_BATCH0 + 1)
                        else:
                            pe.wait_ge(a_kt, n + 1)
                    if li < 6:
                        four(lambda j: nc.tensor.matmul(b4(b0 + 2)[:, j], w["xt"][:, j], w["t1"][:, j],
                                                        start=True, stop=True), g_p2)
                    if li >= 5:
                        four(lambda j: nc.tensor.matmul(b4(b0)[:, j], w["t1"][:, j], w["xt"][:, j],
                                                        start=True, stop=True), g_p3)
            for n, d, t, hs, b0, gc in batches:
                if step_:
                    pe.wait_ge(d_state, n - 3)
                    four(lambda j: nc.tensor.matmul(b4(b0 + 1)[:, j], kT[:, hs, tok(t)][:, j],
                                                    state[:, d, hs][:, j], start=True, stop=True), g_ks)
            some_mods(2)
            for n, d, t, hs, b0, gc in batches:
                w = W[d]
                pe.wait_ge(d_rhs, n + 1)
                pe.wait_ge(d_xt, nth(7, r, 6, d))
                four(lambda j: nc.tensor.matmul(b4(b0 + 2)[:, j], w["xt"][:, j], w["rhs"][:, j],
                                                start=True, stop=True), g_vn)
            for n, d, t, hs, b0, gc in batches:
                w = W[d]
                if with_x:
                    pe.wait_ge(a_vn, n - X_BATCH0 + 1)
                    pe.wait_ge(d_qd, n - X_BATCH0 + 1)

                    def out_four(j):
                        nc.tensor.matmul(b4(b0)[:, j], state[:, d, hs][:, j], w["qdec"][:, j],
                                         start=True, stop=False)
                        return nc.tensor.matmul(b4(b0)[:, j], w["vnew"][:, j], w["pt"][:, j],
                                                start=False, stop=True)
                    four(out_four, g_o)
                if step_ < 3:
                    pe.wait_ge(d_vdec, n + 1)
                    four(lambda j: nc.tensor.matmul(b4(b0 + 1)[:, j], w["ktok"][:, j], w["rhs"][:, j],
                                                    start=True, stop=True), g_st)
        mod_turn(pe, 9)
        some_mods(MOD_PARTS)
        mod_turn(pe, 10)

    def act_recur(act):
        for r, (step_, hg) in enumerate(ROUNDS):
            batches = per_batch(r)
            with_x = step_ >= 2
            for n, d, t, hs, b0, gc in batches:
                w = W[d]
                if with_x:
                    act.wait_ge(d_diff, n + 1)
                    nc.scalar.activation(w["qdec"][:], b4(b0), ACT.Exp).then_inc(a_qd, 1)
                act.wait_ge(d_max, n + 1)
                nc.scalar.activation(w["dec"][:], w["dec"][:], ACT.Exp, scale=-1.0).then_inc(a_dec, 1)
                if with_x:
                    act.wait_ge(d_min, n - X_BATCH0 + 1)
                    nc.scalar.activation(w["pt"][:], w["pt"][:], ACT.Exp).then_inc(a_pt, 1)
                act.wait_ge(g_kt, n + 1)
                nc.scalar.copy(w["ktok"][:], b4(b0 + 2)).then_inc(a_kt, 1)
            for n, d, t, hs, b0, gc in batches:
                act.wait_ge(g_at, n + 1)
                nc.scalar.copy(W[d]["at"][:], b4(b0)).then_inc(a_at, 1)
            if with_x:
                for n, d, t, hs, b0, gc in batches:
                    act.wait_ge(d_vdec, n + 1)
                    nc.scalar.copy(W[d]["vnew"][:], b4(b0 + 2)).then_inc(a_vn, 1)
            act_mod_copy(act, 2 + r)
        act_mod_copy(act, 10)

    def dve_recur(dve):
        def bc(ap):
            return ap.unsqueeze(2).to_broadcast([P, 4, P])

        def mask(i):
            return C(i).unsqueeze(1).to_broadcast([P, 4, P])

        tt = nc.vector.tensor_tensor
        for r, (step_, hg) in enumerate(ROUNDS):
            batches = per_batch(r)
            with_x = step_ >= 2
            for n, d, t, hs, b0, gc in batches:
                w = W[d]
                m = n - X_BATCH0
                dve.wait_ge(g_cb, n + 1)
                tt(w["diff"][:], b4(b0), bc(cum[:, t, gc]), ALU.subtract).then_inc(d_diff, 1)
                dve.wait_ge(d_diff, n + 1)
                nc.vector.tensor_scalar(w["dec"][:], w["diff"][:], 0.0, None, ALU.max).then_inc(d_max, 1)
                if with_x:
                    nc.vector.tensor_scalar(w["pt"][:], w["diff"][:], 0.0, None, ALU.min).then_inc(d_min, 1)
                step(tt(w["rhs"][:], v_tok[:, t, hs], bc(gb_tok[:, t, 32 + gc.start:32 + gc.stop]), ALU.mult))
            if r:
                dve_mod_bias(dve, r + 1)
            for n, d, t, hs, b0, gc in batches:
                w = W[d]
                dve.wait_ge(a_dec, n + 1)
                step(tt(w["dec"][:], w["dec"][:], mask(Const.STRICT[d]), ALU.mult))
                dve.wait_ge(g_gram, n + 1)
                step(tt(w["dec"][:], w["dec"][:], b4(b0 + 1), ALU.mult))
                tt(w["a"][:], w["dec"][:], bc(gb_tok[:, t, 32 + gc.start:32 + gc.stop]), ALU.mult).then_inc(d_a, 1)
                dve.wait_ge(d_a, n + 1)
                step(tt(w["t1"][:], w["a"][:], mask(Const.LEVEL[d]), ALU.mult))
                tt(w["xm"][:], mask(Const.IDENT), w["t1"][:], ALU.subtract).then_inc(d_xm, 1)
                dve.wait_ge(d_xm, nth(6, r, 0, d))
                nc.vector.transpose(w["xt"][:], w["xm"][:]).then_inc(d_xt, 1)
            if with_x:
                for n, d, t, hs, b0, gc in batches:
                    w = W[d]
                    m = n - X_BATCH0
                    dve.wait_ge(a_pt, m + 1)
                    step(tt(w["pt"][:], w["pt"][:], mask(Const.INCL[d]), ALU.mult))
                    dve.wait_ge(g_qk, m + 1)
                    tt(w["pt"][:], w["pt"][:], b4(b0 + 2), ALU.mult).then_inc(d_pt, 1)
                    dve.wait_ge(a_qd, m + 1)
                    tt(w["qdec"][:], w["qdec"][:], qT[:, hs, tok(t)], ALU.mult).then_inc(d_qd, 1)
            for li in range(1, 7):
                for n, d, t, hs, b0, gc in batches:
                    w = W[d]
                    dve.wait_ge(g_p1, nth(6, r, li - 1, d))
                    tt(w["t1"][:], b4(b0 + 1), mask(Const.LEVEL[d] + li), ALU.mult).then_inc(d_t1, 1)
                for n, d, t, hs, b0, gc in batches:
                    w = W[d]
                    if li < 6:
                        dve.wait_ge(g_p2, nth(5, r, li - 1, d))
                        tt(w["xm"][:], w["xm"][:], b4(b0 + 2), ALU.subtract).then_inc(d_xm, 1)
                    if li < 5:
                        dve.wait_ge(d_xm, nth(6, r, li, d))
                        nc.vector.transpose(w["xt"][:], w["xm"][:]).then_inc(d_xt, 1)
                    else:
                        dve.wait_ge(g_p3, nth(2, r, li - 5, d))
                        tt(w["xt"][:], w["xt"][:], b4(b0), ALU.subtract).then_inc(d_xt, 1)
            for n, d, t, hs, b0, gc in batches:
                w = W[d]
                if step_:
                    dve.wait_ge(g_ks, n - 3)
                    step(tt(w["t1"][:], b4(b0 + 1), bc(be_cum[:, t, gc]), ALU.mult))
                    tt(w["rhs"][:], w["rhs"][:], w["t1"][:], ALU.subtract).then_inc(d_rhs, 1)
                else:
                    tt(w["rhs"][:], w["rhs"][:], w["rhs"][:], ALU.max).then_inc(d_rhs, 1)
            for n, d, t, hs, b0, gc in batches:
                w = W[d]
                dve.wait_ge(g_vn, n + 1)
                tt(w["rhs"][:], b4(b0 + 2), bc(e_tail[:, t, gc]), ALU.mult).then_inc(d_vdec, 1)
            for n, d, t, hs, b0, gc in batches:
                w = W[d]
                m = n - X_BATCH0
                st = state[:, d, hs]
                if with_x:
                    dve.wait_ge(g_o, m + 1)
                    if step_ == 2:
                        nc.vector.tensor_copy(o_sum[:, hs, tok(t)], b4(b0)).then_inc(d_o, 1)
                    else:
                        dve.wait_ge(d_o, m - 3)
                        tt(o_sum[:, hs, tok(t)], o_sum[:, hs, tok(t)], b4(b0), ALU.add).then_inc(d_o, 1)
                if step_ == 0:
                    dve.wait_ge(g_st, n + 1)
                    nc.vector.tensor_copy(st, b4(b0 + 1)).then_inc(d_state, 1)
                elif step_ < 3:
                    step(tt(st, st, bc(e_tot[:, t, gc]), ALU.mult))
                    dve.wait_ge(g_st, n + 1)
                    tt(st, st, b4(b0 + 1), ALU.add).then_inc(d_state, 1)
        dve_mod_bias(dve, 9)
        dve_mod_bias(dve, 10)

    o_sq, o_summed, o_ms, o_rs, o_n, y_hi_ready, y_lo_ready = (
        sem(n) for n in ("o_sq", "o_summed", "o_ms", "o_rs", "o_n", "y_hi_ready", "y_lo_ready"))
    y_hi = n_hi[:].rearrange("p k (a t) -> p (k a) t", a=2)
    y_lo = n_lo[:].rearrange("p k (a t) -> p (k a) t", a=2)
    o_pairs = [o_sum[:, 2 * i:2 * i + 2, :].rearrange("p a t -> p (a t)") for i in range(4)]

    def y_pair(v, i):
        return v[:, 2 * i:2 * i + 2, :].rearrange("p a t -> p (a t)")

    def pe_out(pe):
        for i in range(4):
            pe.wait_ge(o_sq, i + 1)
            if i == 0:
                pe.wait_ge(d_o, 8)
            nc.tensor.matmul(bank[MISC_BANK][:], C(Const.ONES), nt[:, 0, :], start=True, stop=True).then_inc(o_summed, 1)

        def before(g, k):
            if g == 0 and k % 2 == 0:
                pe.wait_ge(y_lo_ready, k // 2 + 1)

        linear(pe, "out", [16] * 8, CH_OUT, lambda g, k: (y_hi[:, k, :], y_lo[:, k, :]), L, before=before)
        norm_sum(pe, 1, L)

    def act_out_stage(act):
        for i in range(4):
            act.wait_ge(d_o, 8)
            nc.scalar.copy(y_pair(y_hi, i), y_pair(y_pool, i)).then_inc(y_hi_ready, 1)
        for i in range(4):
            act.wait_ge(o_ms, i + 1)
            nc.scalar.activation(rstd[:], rstd[:], ACT.Sqrt).then_inc(o_rs, 1)
            act.wait_ge(o_n, i + 1)
            nc.scalar.copy(y_pair(y_hi, 4 + i), o_pairs[i]).then_inc(y_hi_ready, 1)
        for i in range(N_OUT):
            split_ahead(act, CH_OUT + i)
        act_rstd(act, 1, L)

    def dve_out(dve):
        dve.wait_ge(d_o, 8)
        for i in range(4):
            o = o_pairs[i]
            if i:
                dve.wait_ge(o_summed, i)
            nc.vector.tensor_tensor(nt[:, 0, :], o, o, ALU.mult).then_inc(o_sq, 1)
            dve.wait_ge(y_hi_ready, i + 1)
            nc.vector.tensor_tensor(y_pair(y_lo, i), y_pair(y_pool, i), y_pair(y_hi, i).bitcast(F32),
                                    ALU.subtract).then_inc(y_lo_ready, 1)
            dve.wait_ge(o_summed, i + 1)
            step(nc.vector.tensor_scalar(rstd[:], bank[MISC_BANK][:], 1.0 / P, EPS, ALU.mult, ALU.add))
            nc.vector.reciprocal(rstd[:], rstd[:]).then_inc(o_ms, 1)
            dve.wait_ge(o_rs, i + 1)
            step(nc.vector.scalar_tensor_tensor(o, o, col(Cols.DN_GAIN), rstd[:], ALU.mult, ALU.mult))
            nc.vector.tensor_tensor(o, o, y_pair(z_dn, i), ALU.mult).then_inc(o_n, 1)
        for i in range(4):
            dve.wait_ge(y_hi_ready, 5 + i)
            nc.vector.tensor_tensor(y_pair(y_lo, 4 + i), o_pairs[i], y_pair(y_hi, 4 + i).bitcast(F32),
                                    ALU.subtract).then_inc(y_lo_ready, 1)
        for kt in range(KT):
            g = GROUPS_BEFORE["out"] + kt
            dve.wait_ge(linear_done, GROUP_DONE["out"][kt])
            nc.vector.scalar_tensor_tensor(h[:, kt, 0:L], bank[g % BANKS][:, 0:L], mods[:, M_GATE + kt, 0:1],
                                           h[:, kt, 0:L], ALU.mult, ALU.add).then_inc(groups_read, 1)
            dve.wait_ge(groups_read, g + 1)
            dve_square(dve, kt, L, KT - 1)
        for i in range(6):
            step(dve_gain(dve, i + 1))
            tile0, factor = GATES[i]
            step(nc.vector.tensor_scalar(gates[:, i], mods[:, tile0:tile0 + KT, :], factor, None, ALU.mult))
        dve_mean_square(dve, 1, L)
        dve.wait_ge(rstd_ready, 2)
        for kt in range(KT):
            last = nc.vector.scalar_tensor_tensor(h[:, kt, 0:L], h[:, kt, 0:L], col(Cols.FINAL_GAIN + kt),
                                                  rstd[:, 0:L], ALU.mult, ALU.mult)
        step(last)
        dve.wait_ge(ctx2_in, 16)
        for k in range(KT):
            dve_square(dve, k, T, KT - 1)

    SQ_COUNT.update({1: 2, 2: 3, 3: 5, 4: 6, 5: 8, 6: 10, 7: 11})

    FFNS = [(1, 2, 0, 0), (3, 4, 2, 30), (4, 5, 3, 52), (6, 7, 5, 74)]
    SC = (2, 3, 1, 22)
    MLA = (5, 6, 4, 0)
    MARKS = GROUP_DONE[("ffn", 0, 1)][-1] - GROUP_DONE[("ffn", 0, 0)][-1]
    HALF_CHUNKS, HALF_GROUPS = N_FFN // 2, 2 * HALF + KT

    def ffn_width(n):
        return T if n < 3 else L

    def pe_operands(pe, i):
        def before(g, k):
            if g == 0:
                pe.wait_ge(normed, KT * i + k + 1)
        return before

    def pe_ffn(pe, n):
        i, m, _, hid0 = FFNS[n]
        w, key, first = ffn_width(n), ("ffn", n, 0), CH_FFN[n]
        norm_sum(pe, m, w)
        with pe.Fori(0, 2) as half:
            linear(pe, key, [KT] * (2 * HALF), first, lambda g, k: (n_hi[:, k, 0:w], n_lo[:, k, 0:w]), w,
                   chunk_off=half * HALF_CHUNKS, group_off=half * HALF_GROUPS, before=pe_operands(pe, i))

            def before(g, k):
                if g == 2 * HALF:
                    pe.wait_ge(hid_lo, half * HALF + (hid0 + k + 1))

            linear(pe, key, [HALF] * KT, first + 2 * HALF, lambda g, k: (g_hi[:, k, 0:w], g_lo[:, k, 0:w]), w,
                   group0=2 * HALF, chunk_off=half * HALF_CHUNKS, group_off=half * HALF_GROUPS, before=before)

    def act_ffn(act, n):
        i, m, _, hid0 = FFNS[n]
        w, key = ffn_width(n), ("ffn", n, 0)
        g0 = GROUPS_BEFORE[key]
        act_norm(act, i, m, w)
        with act.Fori(0, 2) as half:
            def high(f):
                act.wait_ge(groups_read, half * HALF_GROUPS + (g0 + 2 * f + 2))
                nc.scalar.copy(g_hi[:, f, 0:w], prod[:, f % 2, 0:w]).then_inc(hid_hi, 1)

            for j in range(HALF_CHUNKS):
                split_ahead(act, CH_FFN[n] + j, mark_off=half * MARKS, turn_off=half * (16 * HALF_CHUNKS // RING))
                f = j // 2
                if j < 2 * HALF and j % 2 == 0:
                    act.wait_ge(linear_done, half * MARKS + GROUP_DONE[key][j])
                    if f >= 2:
                        act.wait_ge(groups_read, half * HALF_GROUPS + (g0 + 2 * f - 2))
                    nc.scalar.activation(silu[:, f % 2, 0:w], bank[(g0 + j) % BANKS][:, 0:w],
                                         ACT.Silu).then_inc(gate_ready, 1)
                    if f:
                        high(f - 1)
                if j == 2 * HALF:
                    high(HALF - 1)

    def dve_residual(dve, key, g_first, gate, w, d, mark_off=0, group_off=0, squares=True):
        g = GROUPS_BEFORE[key] + g_first + d
        dve.wait_ge(linear_done, mark_off + GROUP_DONE[key][g_first + d])
        for c, s_ in sides(w):
            last = nc.vector.scalar_tensor_tensor(h[:, d, s_], bank[g % BANKS][:, s_], gates[:, gate, d, c:c + 1],
                                                  h[:, d, s_], ALU.mult, ALU.add)
        last.then_inc(groups_read, 1)
        if squares:
            dve.wait_ge(groups_read, group_off + (g + 1))
            dve_square(dve, d, w, KT - 1)

    def dve_ffn(dve, n):
        i, m, gate, hid0 = FFNS[n]
        w, key = ffn_width(n), ("ffn", n, 0)
        g0 = GROUPS_BEFORE[key]
        dve_norm(dve, i, m, w)
        squares = n < 3
        steps = 2 * KT - 2 if squares else 0
        before = dve_count[0]
        with dve.Fori(0, 2) as half:
            dve_loop[0] = half * steps

            def low(f):
                dve.wait_ge(hid_hi, half * HALF + (hid0 + f + 1))
                nc.vector.tensor_tensor(g_lo[:, f, 0:w], prod[:, f % 2, 0:w], g_hi[:, f, 0:w].bitcast(F32),
                                        ALU.subtract).then_inc(hid_lo, 1)

            for f in range(HALF):
                g = g0 + 2 * f + 1
                dve.wait_ge(gate_ready, half * HALF + (hid0 + f + 1))
                dve.wait_ge(linear_done, half * MARKS + GROUP_DONE[key][2 * f + 1])
                if f >= 2:
                    dve.wait_ge(hid_lo, half * HALF + (hid0 + f - 1))
                nc.vector.tensor_tensor(prod[:, f % 2, 0:w], silu[:, f % 2, 0:w], bank[g % BANKS][:, 0:w],
                                        ALU.mult).then_inc(groups_read, 2)
                if f:
                    low(f - 1)
            low(HALF - 1)
            for d in range(KT):
                dve_residual(dve, key, 2 * HALF, gate, w, d, half * MARKS, half * HALF_GROUPS, squares)
        dve_loop[0] = 0
        assert dve_count[0] - before == steps
        dve_count[0] += steps

    def pe_sc(pe):
        i, m, _, hid0 = SC
        norm_sum(pe, m, T)
        linear(pe, "sc", [KT] * 24, CH_SC, lambda g, k: (n_hi[:, k, :], n_lo[:, k, :]), T,
               before=pe_operands(pe, i))

        def before(g, k):
            if g == 24:
                pe.wait_ge(hid_lo, hid0 + k + 1)

        linear(pe, "sc", [KT] * KT, CH_SC + 24, lambda g, k: (g_hi[:, k, :], g_lo[:, k, :]), T, group0=24,
               before=before)

    def act_sc(act):
        i, m, _, hid0 = SC
        g0 = GROUPS_BEFORE["sc"]
        act_norm(act, i, m, T)

        def high(ct):
            act.wait_ge(groups_read, g0 + 3 * ct + 3)
            nc.scalar.copy(g_hi[:, ct, :], prod[:, ct % 2, :]).then_inc(hid_hi, 1)

        for j in range(N_SC):
            split_ahead(act, CH_SC + j)
            ct, kind = j // 3, j % 3
            if j < 24 and kind == 0:
                act.wait_ge(linear_done, GROUP_DONE["sc"][j])
                if ct >= 2:
                    act.wait_ge(groups_read, g0 + 3 * ct - 4)
                nc.scalar.copy(silu[:, ct % 2, :], bank[(g0 + j) % BANKS][:]).then_inc(gate_ready, 1)
                if ct:
                    high(ct - 1)
            if j == 24:
                high(KT - 1)

    def dve_sc(dve):
        i, m, gate, hid0 = SC
        g0 = GROUPS_BEFORE["sc"]
        dve_norm(dve, i, m, T)
        step(nc.vector.memset(sc_pad[:], 0.0))
        conv_view = sc_conv[:].rearrange("p (a t) -> p a t", a=2)

        def low(ct):
            dve.wait_ge(hid_hi, hid0 + ct + 1)
            nc.vector.tensor_tensor(g_lo[:, ct, :], prod[:, ct % 2, :], g_hi[:, ct, :].bitcast(F32),
                                    ALU.subtract).then_inc(hid_lo, 1)

        for ct in range(KT):
            dve.wait_ge(gate_ready, hid0 + ct + 1)
            dve.wait_ge(linear_done, GROUP_DONE["sc"][3 * ct + 1])
            nc.vector.tensor_tensor(sc_pad[:, ct % 2, :, 1:1 + L],
                                    silu[:, ct % 2, :].rearrange("p (a t) -> p a t", a=2),
                                    bank[(g0 + 3 * ct + 1) % BANKS][:].rearrange("p (a t) -> p a t", a=2),
                                    ALU.mult).then_inc(groups_read, 2)
            dve.wait_ge(groups_read, g0 + 3 * ct + 2)
            for tap in range(3):
                src, wt = sc_pad[:, ct % 2, :, tap:tap + L], col(Cols.SC_CONV + 3 * ct + tap)
                if tap == 0:
                    step(nc.vector.tensor_scalar(conv_view, src, wt, None, ALU.mult))
                else:
                    step(nc.vector.scalar_tensor_tensor(conv_view, src, wt, conv_view, ALU.mult, ALU.add))
            dve.wait_ge(linear_done, GROUP_DONE["sc"][3 * ct + 2])
            if ct >= 2:
                dve.wait_ge(hid_lo, hid0 + ct - 1)
            nc.vector.tensor_tensor(prod[:, ct % 2, :], sc_conv[:], bank[(g0 + 3 * ct + 2) % BANKS][:],
                                    ALU.mult).then_inc(groups_read, 1)
            if ct:
                low(ct - 1)
        low(KT - 1)
        for d in range(KT):
            dve_residual(dve, "sc", 24, gate, T, d)

    l_sq, l_summed, l_ms, l_rs, l_scaled, l_hi, l_lo = (
        sem(f"lora_{n}") for n in ("sq", "summed", "ms", "rs", "scaled", "hi", "lo"))
    h_sq, h_sq_used, h_summed, h_ms, h_rs, h_scaled = (
        sem(f"head_{n}") for n in ("sq", "sq_used", "summed", "ms", "rs", "scaled"))
    rope_t, rope_turned, rope_done = (sem(f"rope_{n}") for n in ("t", "turned", "done"))
    s_ready, s_max, s_exp, s_norm, s_turned, s_copied, s_out, s_out_hi, s_out_lo = (
        sem(f"att_{n}") for n in ("scores", "max", "exp", "norm", "turned", "copied", "out", "out_hi", "out_lo"))
    q_raw = probs_t
    UQ, UK, UV, WO = 4, 16, 24, 32

    def tab(at, n=L):
        return rope[:, at:at + n]

    def mla_done(g):
        return GROUP_DONE["mla"][g]

    def pe_mla(pe):
        i, m, _, _ = MLA
        g0 = GROUPS_BEFORE["mla"]
        norm_sum(pe, m, T)
        before = pe_operands(pe, i)
        linear(pe, "mla", [KT] * 2, CH_MLA, lambda g, k: (n_hi[:, k, 0:L], n_lo[:, k, 0:L]), L, before=before)
        linear(pe, "mla", [KT] * 2, CH_MLA + 2, lambda g, k: (n_hi[:, k, :], n_lo[:, k, :]), T, group0=2)
        pe.wait_ge(l_sq, 2)
        for j in range(2):
            last = nc.tensor.matmul(bank[MISC_BANK][:, 0:L], C(Const.ONES), a_sq[:, j, 0:L],
                                    start=(j == 0), stop=(j == 1))
        last.then_inc(l_summed, 1)
        pe.wait_ge(l_sq, 3)
        nc.tensor.matmul(bank[MOD_BANK][:], C(Const.ONES), a_sq[:, 2, :], start=True, stop=True)\
            .then_inc(l_summed, 1)
        pe.wait_ge(rope_in_sem, 16)
        pe.wait_ge(rope_t, 1)
        pe.wait_ge(l_ms, 1)
        nc.tensor.matmul(bank[MISC_BANK][:, 0:L], tab(Rope.PERM, P), kr[:, 0:L], start=True, stop=True)\
            .then_inc(rope_turned, 1)

        def wait_lora(g, k):
            pe.wait_ge(l_lo, k + 1)

        def wait_kv(g, k):
            pe.wait_ge(l_lo, 3)

        linear(pe, "mla", [2] * 12, CH_MLA + 4, lambda g, k: (c_hi[:, k, 0:L], c_lo[:, k, 0:L]), L, group0=UQ,
               before=wait_lora)
        linear(pe, "mla", [1] * 8, CH_MLA + 7, lambda g, k: (c_hi[:, 2, :], c_lo[:, 2, :]), T, group0=UK,
               before=wait_kv)
        chunk = CH_MLA + 8
        pe.wait_ge(w_lo_ready, chunk + 1)
        for vi in range(8):
            g, half, t = g0 + UV + vi, vi // 4, vi % 4
            pe.wait_ge(groups_read, g - BANKS + 1)
            out_ap = bank[g % BANKS][:]
            c_h, c_l = c_hi[:, 2, tok(t)], c_lo[:, 2, tok(t)]
            w_h, w_l = (w[:, chunk % RING, half * 512:(half + 1) * 512] for w in (w_hi, w_lo))
            nc.tensor.matmul(out_ap, c_h, w_l, start=True, stop=False)
            nc.tensor.matmul(out_ap, c_l, w_h, start=False, stop=False)
            nc.tensor.matmul(out_ap, c_h, w_h, start=False, stop=True).then_inc(linear_done, 1)
        pe.wait_ge(groups_read, g0 + WO)
        for j in range(12):
            pe.wait_ge(h_sq, j + 1)
            b = bank[j % BANKS]
            if j >= BANKS:
                pe.wait_ge(h_ms, j - BANKS + 1)
            if j < 4:
                for e in range(2):
                    o = b[:, e * L:(e + 1) * L]
                    nc.tensor.matmul(o, C(Const.ONES), a_sq[:, j % 2, e * L:(e + 1) * L], start=True, stop=False)
                    last = nc.tensor.matmul(o, tab((Rope.ONES_LO, Rope.ONES_HI)[e], P), rot[:, j % 2, :],
                                            start=False, stop=True)
            else:
                nc.tensor.matmul(b[:], C(Const.ONES), a_sq[:, j % 2, :], start=True, stop=False)
                last = nc.tensor.matmul(b[:], tab(Rope.ONES_LO, P), a_sq[:, 2, :], start=False, stop=True)
            last.then_inc(h_summed, 1)
            if 1 <= j <= 4:
                p = j - 1
                pe.wait_ge(rope_t, p + 2)
                pe.wait_ge(rope_done, p + 1)
                nc.tensor.matmul(bank[MISC_BANK][:, 0:L], tab(Rope.PERM, P), q_raw[:, p, :],
                                 start=True, stop=True).then_inc(rope_turned, 1)
        pe.wait_ge(h_scaled, 12)
        pe.wait_ge(rope_done, 5)

        def scores(hd):
            for qt in range(2):
                b = bank[2 * (hd % 2) + qt]
                if hd >= 2:
                    pe.wait_ge(s_exp, 2 * (hd - 2) + qt + 1)
                nc.tensor.matmul(b[:], q_nope[:, hd, tok(qt)], k_nope[:, hd, :], start=True, stop=False)
                nc.tensor.matmul(b[:], q_rope[:, hd, tok(qt)], k_rope[:, hd // 2, :], start=False,
                                 stop=True).then_inc(s_ready, 1)

        scores(0)
        for hd in range(HEADS):
            if hd + 1 < HEADS:
                scores(hd + 1)
            for pair in range(2):
                if hd:
                    pe.wait_ge(s_copied, 2 * (hd - 1) + pair + 1)
                for e in range(2):
                    for qt in range(2):
                        if pair == 0 and e == 0:
                            pe.wait_ge(s_norm, 2 * hd + qt + 1)
                        last = nc.tensor.transpose(bank[4 + pair][:, e * L + qt * P:e * L + (qt + 1) * P],
                                                   probs[:, qt, tok(2 * pair + e)], C(Const.IDENT))
                last.then_inc(s_turned, 1)
            if hd >= 2:
                pe.wait_ge(s_out_lo, hd - 1)
            for t in range(4):
                if t % 2 == 0:
                    pe.wait_ge(s_copied, 2 * hd + t // 2 + 1)
                last = nc.tensor.matmul(bank[6 + hd % 2][:, 0:L], v_att[:, t, hd, :], probs_t[:, t, :],
                                        start=(t == 0), stop=(t == 3))
            last.then_inc(s_out, 1)

        def wait_out(g, k):
            if g == WO and k == 0:
                pe.wait_ge(s_out_lo, HEADS)

        linear(pe, "mla", [KT] * KT, CH_MLA + 9, lambda g, k: (n_hi[:, k, 0:L], n_lo[:, k, 0:L]), L, group0=WO,
               before=wait_out)

    def act_mla(act):
        i, m, _, _ = MLA
        g0 = GROUPS_BEFORE["mla"]
        act.wait_ge(groups_read, g0)
        act.dma_start(rope[:], rope_tab[:]).then_inc(rope_in_sem, 16)
        act_norm(act, i, m, T)

        def read(g, dest, w):
            act.wait_ge(linear_done, mla_done(g))
            nc.scalar.copy(dest, bank[(g0 + g) % BANKS][:, 0:w]).then_inc(groups_read, 1)

        for j in range(4):
            split_ahead(act, CH_MLA + j)
            read(j, (cq[:, 0, :], cq[:, 1, :], ckv[:], kr[:])[j], L if j < 2 else T)
        for j in range(2):
            act.wait_ge(l_ms, j + 1)
            w = (L, T)[j]
            nc.scalar.activation(a_rstd[:, j, 0:w], a_rstd[:, j, 0:w], ACT.Sqrt).then_inc(l_rs, 1)
        for j in range(3):
            act.wait_ge(l_scaled, j + 1)
            w = (L, L, T)[j]
            nc.scalar.copy(c_hi[:, j, 0:w], (cq[:, 0, :], cq[:, 1, :], ckv[:])[j]).then_inc(l_hi, 1)
        for j in range(3):
            split_ahead(act, CH_MLA + 4 + j)
            for g in range(4 * j, 4 * j + 4):
                read(UQ + g, q_nope[:, g, :] if g < HEADS else q_raw[:, g - HEADS, :], L)
        split_ahead(act, CH_MLA + 7)
        for g in range(8):
            read(UK + g, k_nope[:, g, :], T)
        split_ahead(act, CH_MLA + 8)
        for vi in range(8):
            read(UV + vi, v_att[:, vi % 4, 4 * (vi // 4):4 * (vi // 4) + 4, :].rearrange("p a d -> p (a d)"), T)
        for j in range(12):
            act.wait_ge(h_ms, j + 1)
            nc.scalar.activation(a_rstd[:, j % 2, :], a_rstd[:, j % 2, :], ACT.Sqrt).then_inc(h_rs, 1)
        scale = float(QK_HEAD) ** -0.5

        def softmax(hd):
            act.wait_ge(s_max, hd + 1)
            for qt in range(2):
                if hd:
                    act.wait_ge(s_turned, 2 * hd)
                nc.scalar.activation(probs[:, qt, :], bank[2 * (hd % 2) + qt][:], ACT.Exp, scale=scale,
                                     bias=smax[:, qt:qt + 1], accum_out=ssum[:, qt:qt + 1]).then_inc(s_exp, 1)

        def out_high(hd):
            act.wait_ge(s_out, hd + 1)
            nc.scalar.copy(n_hi[:, hd, 0:L], bank[6 + hd % 2][:, 0:L]).then_inc(s_out_hi, 1)

        for hd in range(HEADS):
            softmax(hd)
            if hd:
                out_high(hd - 1)
            act.wait_ge(s_turned, 2 * hd + 1)
            if hd:
                act.wait_ge(s_out, hd)
            nc.scalar.copy(probs_t[:, 0:2, :].rearrange("p a t -> p (a t)"), bank[4][:]).then_inc(s_copied, 1)
            act.wait_ge(s_turned, 2 * hd + 2)
            nc.scalar.copy(probs_t[:, 2:4, :].rearrange("p a t -> p (a t)"), bank[5][:]).then_inc(s_copied, 1)
        out_high(HEADS - 1)
        for j in range(8):
            split_ahead(act, CH_MLA + 9 + j)

    def dve_mla(dve):
        i, m, gate, _ = MLA
        g0 = GROUPS_BEFORE["mla"]
        dve_norm(dve, i, m, T)
        step(nc.vector.memset(q_rope[:], 0.0))
        lat = (cq[:, 0, :], cq[:, 1, :], ckv[:])
        for j in range(3):
            w = (L, L, T)[j]
            dve.wait_ge(groups_read, g0 + j + 1)
            nc.vector.tensor_tensor(a_sq[:, j, 0:w], lat[j], lat[j], ALU.mult).then_inc(l_sq, 1)
        for j in range(2):
            w, n, b = ((L, 2 * P, MISC_BANK), (T, P, MOD_BANK))[j]
            dve.wait_ge(l_summed, j + 1)
            step(nc.vector.tensor_scalar(a_rstd[:, j, 0:w], bank[b][:, 0:w], 1.0 / n, EPS, ALU.mult, ALU.add))
            nc.vector.reciprocal(a_rstd[:, j, 0:w], a_rstd[:, j, 0:w]).then_inc(l_ms, 1)
        dve.wait_ge(groups_read, g0 + 4)
        step(nc.vector.tensor_tensor(a_sq[:, 2, :], kr[:], kr[:], ALU.mult))
        nc.vector.tensor_scalar(kr[:], kr[:], col(Cols.G_K + 1), None, ALU.mult).then_inc(rope_t, 1)
        for j in range(3):
            w = (L, L, T)[j]
            dve.wait_ge(l_rs, (1, 1, 2)[j])
            nc.vector.scalar_tensor_tensor(lat[j], lat[j], col((Cols.G_QA, Cols.G_QA + 1, Cols.G_KVA)[j]),
                                           a_rstd[:, (0, 0, 1)[j], 0:w], ALU.mult, ALU.mult).then_inc(l_scaled, 1)
        for j in range(3):
            w = (L, L, T)[j]
            dve.wait_ge(l_hi, j + 1)
            nc.vector.tensor_tensor(c_lo[:, j, 0:w], lat[j], c_hi[:, j, 0:w].bitcast(F32),
                                    ALU.subtract).then_inc(l_lo, 1)
        dve.wait_ge(rope_in_sem, 16)
        dve.wait_ge(rope_turned, 1)
        step(nc.vector.tensor_tensor(kr_rot[:, 0:L], bank[MISC_BANK][:, 0:L], tab(Rope.SIN), ALU.mult))
        step(nc.vector.tensor_tensor(rot[:, 0, :], kr[:, 0:L], tab(Rope.COS), ALU.mult))
        step(nc.vector.tensor_tensor(kr_rot[:, 0:L], kr_rot[:, 0:L], rot[:, 0, :], ALU.add))
        nc.vector.tensor_copy(kr_rot[:, L:T], kr[:, L:T]).then_inc(rope_done, 1)
        dve.wait_ge(rope_done, 1)
        dve.wait_ge(groups_read, g0 + WO)

        def head_square(j):
            if j >= 2:
                dve.wait_ge(h_summed, j - 1)
            if j < 4:
                qn = q_nope[:, 2 * j:2 * j + 2, :].rearrange("p a t -> p (a t)")
                nc.vector.tensor_tensor(rot[:, j % 2, :], q_raw[:, j, :], q_raw[:, j, :], ALU.mult)
                nc.vector.tensor_tensor(a_sq[:, j % 2, :], qn, qn, ALU.mult).then_inc(h_sq, 1)
            else:
                kn = k_nope[:, j - 4, :]
                nc.vector.tensor_tensor(a_sq[:, j % 2, :], kn, kn, ALU.mult).then_inc(h_sq, 1)

        def head_mean(j):
            dve.wait_ge(h_summed, j + 1)
            if j >= 2:
                dve.wait_ge(h_scaled, j - 1)
            step(nc.vector.tensor_scalar(a_rstd[:, j % 2, :], bank[j % BANKS][:], 1.0 / QK_HEAD, EPS,
                                         ALU.mult, ALU.add))
            nc.vector.reciprocal(a_rstd[:, j % 2, :], a_rstd[:, j % 2, :]).then_inc(h_ms, 1)

        def head_scale(j):
            dve.wait_ge(h_rs, j + 1)
            r_ = a_rstd[:, j % 2, :]
            if j < 4:
                qn = q_nope[:, 2 * j:2 * j + 2, :].rearrange("p a t -> p (a t)")
                nc.vector.scalar_tensor_tensor(qn, qn, col(Cols.G_Q), r_, ALU.mult, ALU.mult)
                raw = q_raw[:, j, :]
                dve.wait_ge(h_sq, j + 1)
                nc.vector.tensor_scalar(raw, raw, col(Cols.G_Q + 1), None, ALU.mult).then_inc(rope_t, 1)
                dve.wait_ge(rope_turned, j + 2)
                step(nc.vector.tensor_tensor(rot[:, j % 2, :], bank[MISC_BANK][:, 0:L], tab(Rope.SIN), ALU.mult))
                step(nc.vector.tensor_tensor(raw, raw, tab(Rope.COS), ALU.mult))
                nc.vector.tensor_tensor(raw, raw, rot[:, j % 2, :], ALU.add).then_inc(rope_done, 1)
                dve.wait_ge(rope_done, j + 2)
                for e in range(2):
                    s_ = slice(e * ROPE, (e + 1) * ROPE)
                    last = nc.vector.tensor_tensor(q_rope[s_, 2 * j + e, :], q_raw[s_, j, :],
                                                   a_rstd[s_, j % 2, e * L:(e + 1) * L], ALU.mult)
            else:
                hd = j - 4
                kn = k_nope[:, hd, :]
                nc.vector.scalar_tensor_tensor(kn, kn, col(Cols.G_K), r_, ALU.mult, ALU.mult)
                s_ = slice(hd % 2 * ROPE, (hd % 2 + 1) * ROPE)
                last = nc.vector.tensor_tensor(k_rope[s_, hd // 2, :], kr_rot[s_, :], a_rstd[s_, j % 2, :], ALU.mult)
            last.then_inc(h_scaled, 1)

        head_square(0)
        for j in range(12):
            if j + 1 < 12:
                head_square(j + 1)
            head_mean(j)
            head_scale(j)
        scale = float(QK_HEAD) ** -0.5

        def find_max(hd):
            if hd:
                dve.wait_ge(s_exp, 2 * hd)
            for qt in range(2):
                dve.wait_ge(s_ready, 2 * hd + qt + 1)
                step(nc.vector.tensor_reduce(smax[:, qt:qt + 1], bank[2 * (hd % 2) + qt][:], AX_X, ALU.max))
            nc.vector.tensor_scalar(smax[:], smax[:], -scale, None, ALU.mult).then_inc(s_max, 1)

        def normalise(hd):
            dve.wait_ge(s_exp, 2 * hd + 2)
            step(nc.vector.reciprocal(ssum[:], ssum[:]))
            for qt in range(2):
                nc.vector.tensor_scalar(probs[:, qt, :], probs[:, qt, :], ssum[:, qt:qt + 1], None,
                                        ALU.mult).then_inc(s_norm, 1)

        def out_low(hd):
            dve.wait_ge(s_out_hi, hd + 1)
            nc.vector.tensor_tensor(n_lo[:, hd, 0:L], bank[6 + hd % 2][:, 0:L], n_hi[:, hd, 0:L].bitcast(F32),
                                    ALU.subtract).then_inc(s_out_lo, 1)

        for hd in range(HEADS):
            find_max(hd)
            normalise(hd)
            if hd:
                out_low(hd - 1)
        out_low(HEADS - 1)
        for d in range(KT):
            dve_residual(dve, "mla", WO, gate, L, d)

    def store(sp):
        sp.wait_ge(groups_read, GROUPS_BEFORE[("ffn", 3, 1)] + HALF_GROUPS)
        sp.dma_start(out[:], h[:, :, 0:L]).then_inc(out_done, 16)
        sp.wait_ge(out_done, 16)

    block = ctx.enter_context(nc.Block())

    @block.sync
    def _(sp):
        sp_program(sp)
        store(sp)

    @block.gpsimd
    def _(pool):
        pool_program(pool)

    @block.tensor
    def _(pe):
        pe_start(pe)
        pe_in(pe)
        pe_recur(pe)
        pe_out(pe)
        pe_ffn(pe, 0)
        pe_sc(pe)
        pe_ffn(pe, 1)
        pe_ffn(pe, 2)
        pe_mla(pe)
        pe_ffn(pe, 3)

    @block.scalar
    def _(act):
        act_start(act)
        act_in(act)
        act_recur(act)
        act_out_stage(act)
        act_ffn(act, 0)
        act_sc(act)
        act_ffn(act, 1)
        act_ffn(act, 2)
        act_mla(act)
        act_ffn(act, 3)

    @block.vector
    def _(dve):
        dve_start(dve)
        dve_in(dve)
        dve_recur(dve)
        dve_out(dve)
        dve_ffn(dve, 0)
        dve_sc(dve)
        dve_ffn(dve, 1)
        dve_ffn(dve, 2)
        dve_mla(dve)
        dve_ffn(dve, 3)

    ctx.close()


def _tiles(w):
    k, n = w.shape
    return w.reshape(k // P, P, n // P, P).transpose(2, 0, 1, 3)


def _chunks(tiles):
    t = np.concatenate([x.reshape(-1, P, P) for x in tiles])
    return t.reshape(-1, TILES_PER_CHUNK, P, P).transpose(0, 2, 1, 3).reshape(-1, P, CHUNK)


def lay_out(i):
    f = np.float32
    w_in = i["w_in"][0]
    o = np.cumsum([0, 3 * D, 32, D, D, D])
    wq, wk, wv = w_in[:, 0:D], w_in[:, D:2 * D], w_in[:, 2 * D:3 * D]
    wab, wz, wu, wzp = (w_in[:, o[n]:o[n + 1]] for n in range(1, 5))
    ab = np.zeros((D, P), f)
    ab[:, 0:16], ab[:, 32:48] = wab[:, 0:16], wab[:, 16:32]
    pool = np.stack([_tiles(i["pool_w"][0, g]) for g in range(4)])
    tu = _tiles(wu)
    seq = [_tiles(ab), _tiles(wk), _tiles(wv), _tiles(wq), tu[:4], pool[:2], tu[4:], pool[2:],
           _tiles(wzp), _tiles(wz), _tiles(i["w_out"][0])[:, OUT_ORDER]]

    def ffn(layer, n):
        t1, t3 = _tiles(i["ffn_w1_2"][layer, n]), _tiles(i["ffn_w3_2"][layer, n])
        t2 = _tiles(i["ffn_w2_2"][layer, n])
        for half in range(2):
            a = slice(half * HALF, (half + 1) * HALF)
            seq.append(np.stack([t1[a], t3[a]], axis=1))
            seq.append(t2[:, a])

    ffn(0, 0)
    t = _tiles(i["sc_w_in_2"][0])
    seq.append(np.stack([t[8:16], t[16:24], t[0:8]], axis=1))
    seq.append(_tiles(i["sc_w_out_2"][0]))
    ffn(0, 1)
    ffn(1, 0)
    wa = i["mla_w_a_2"][0]
    wa = np.concatenate([wa, wa[:, 384:448]], axis=1)
    uq = i["mla_w_uq_2"][0].reshape(256, HEADS, QK_HEAD)
    uq = np.concatenate([uq[:, :, :NOPE].reshape(256, -1), uq[:, :, NOPE:].reshape(256, -1)], axis=1)
    ukv = i["mla_w_ukv_2"][0].reshape(P, HEADS, 2, P)
    seq += [_tiles(wa), _tiles(uq), _tiles(ukv[:, :, 0].reshape(P, -1)), _tiles(ukv[:, :, 1].reshape(P, -1)),
            _tiles(i["mla_w_o_2"][0])]
    ffn(1, 1)
    seq.append(np.zeros((AHEAD * TILES_PER_CHUNK, P, P), f))
    stream = _chunks(seq)
    assert stream.shape[0] == N_STREAM

    wm = np.concatenate([i["w_mod"][0], i["w_mod_2"][0], i["w_mod_2"][1],
                         np.zeros((D, MOD_GROUPS * MOD_COLS - 21 * D), f)], axis=1)
    modstream = wm.reshape(KT, P, MOD_GROUPS, 2, CHUNK).transpose(2, 0, 3, 1, 4).reshape(-1, P, CHUNK)

    def feat(a):
        return a.T.reshape(KT, P, -1).transpose(1, 0, 2)

    tokens = np.concatenate([feat(i["x"][0]), feat(i["ctx"][0])], axis=2)
    ctx2 = feat(i["ctx_2"][0])
    conds = np.zeros((P, 2, KT, 32), f)
    for b, (c, cc) in enumerate(((i["c"][0], i["c_ctx"]), (i["c_2"][0], i["c_ctx_2"]))):
        conds[:, b, :, 0] = c.reshape(KT, P).T
        conds[:, b, :, 1] = cc.reshape(KT, P).T
    cols = np.zeros((P, Cols.N), f)

    def put(at, v):
        v = np.asarray(v).reshape(-1, P).T
        cols[:, at:at + v.shape[1]] = v

    put(Cols.NORM_GAIN, i["norm_gain"][0])
    put(Cols.FINAL_GAIN, i["final_gain"])
    put(Cols.G_NORM, i["g_norm_2"])
    put(Cols.POOL_SCALE, i["pool_scale"][0])
    put(Cols.DN_GAIN, i["dn_norm_gain"][0])
    cw = i["conv_w"][0].reshape(CONV, 3, KT, P)[:, [1, 2, 0]]
    put(Cols.CONV, cw.transpose(1, 2, 0, 3))
    put(Cols.SC_CONV, i["sc_conv_2"][0].reshape(3, KT, P).transpose(1, 0, 2))
    put(Cols.G_QA, i["mla_g_qa_2"][0])
    put(Cols.G_KVA, i["mla_g_kva_2"][0])
    for at, g in ((Cols.G_Q, i["mla_g_q_2"][0]), (Cols.G_K, i["mla_g_k_2"][0])):
        put(at, np.concatenate([g, g[NOPE:]]))
    cols[0:16, Cols.A_LOG] = i["a_log"][0].reshape(-1)
    cols[0:16, Cols.DT_BIAS] = i["dt_bias"][0].reshape(-1)
    put(Cols.BIAS, np.concatenate([i["b_mod"][0], i["b_mod_2"].reshape(-1),
                                   np.zeros(MOD_GROUPS * MOD_COLS - 21 * D, f)]))

    cols[:, Cols.SEL + 7] = 1
    consts = np.zeros((P, Const.N, P), f)
    r, c = np.arange(P)[:, None], np.arange(P)[None, :]
    consts[:, Const.IDENT] = r == c
    consts[:, Const.ONES] = 1
    for d in (FWD, BWD):
        lower = (c < r) if d == FWD else (c > r)
        consts[:, Const.STRICT[d]] = lower
        consts[:, Const.INCL[d]] = (r <= c) if d == FWD else (r >= c)
        for n, b in enumerate(LEVELS):
            consts[:, Const.LEVEL[d] + n] = lower & (r // (2 * b) == c // (2 * b)) & (r // b != c // b)
    n_freq = ROPE // 4
    inv = (f(10000.0) ** (-np.arange(n_freq, dtype=f) / n_freq)).astype(f)
    tok = np.arange(L)
    ang = np.stack([(tok // GRID_W).astype(f)[:, None] * inv, (tok % GRID_W).astype(f)[:, None] * inv], axis=1)
    ang = np.repeat(ang[:, :, None, :], 2, axis=2).reshape(L, ROPE).T
    ang = np.concatenate([ang, ang])
    rope = np.zeros((P, Rope.N), f)
    rope[:, Rope.COS:Rope.COS + L], rope[:, Rope.SIN:Rope.SIN + L] = np.cos(ang), np.sin(ang)
    rope[:ROPE, Rope.ONES_LO:Rope.ONES_LO + P] = 1
    rope[ROPE:, Rope.ONES_HI:Rope.ONES_HI + P] = 1
    partner = np.where(c % 32 < 16, c + 16, c - 16)
    rope[:, Rope.PERM:Rope.PERM + P] = np.where(r == partner, np.where(c % 32 < 16, -1.0, 1.0), 0.0)
    gc = np.arange(GRID_W)
    counts = np.zeros((P, 4, GRID_W), f)
    for n, w in enumerate(WINDOWS):
        counts[:, n] = 1.0 / (np.clip(gc - w // 2 + w, 0, GRID_W) - np.clip(gc - w // 2, 0, GRID_W))
    named = dict(stream=stream, modstream=modstream, tokens=tokens, ctx2=ctx2, conds=conds, cols=cols,
                 consts=consts, rope=rope, counts=counts)
    return {k: np.ascontiguousarray(v) for k, v in named.items()}


def kernel(**inputs):
    import concourse.bacc as bacc
    from concourse.bass_utils import run_bass_kernel_spmd

    arrays = lay_out({k: np.asarray(v) for k, v in inputs.items()})
    nc = bacc.Bacc("TRN2", target_bir_lowering=False, num_devices=1)
    args = [nc.dram_tensor("in_" + k, v.shape, F32, kind="ExternalInput").ap() for k, v in arrays.items()]
    out = nc.dram_tensor("out", (P, KT, L), F32, kind="ExternalOutput").ap()
    two_block_kernel(nc, *args, out)
    r = run_bass_kernel_spmd(nc, [{"in_" + k: v for k, v in arrays.items()}], core_ids=[0])
    return r.results[0]["out"].transpose(2, 1, 0).reshape(1, L, D)
```

```python
from contextlib import ExitStack

import numpy as np

import concourse.bass as bass
from concourse import mybir

F32 = mybir.dt.float32
F32R = mybir.dt.float32r
ACT = mybir.ActivationFunctionType
ALU = mybir.AluOpType
AX_X = mybir.AxisListType.X

P = 128
D = 1024
KT = D // P
L = 256
T = 2 * L
HEADS = 8
FF = 2816
FT = FF // P
HALF = FT // 2
EPS = 1e-6
CONV = 5
GRID_W = 64
ROWS = L // GRID_W
WINDOWS = (2, 4, 8, 16)
NOPE, ROPE = 128, 64
QK_HEAD = NOPE + ROPE
TILES_PER_CHUNK = 8
CHUNK = TILES_PER_CHUNK * P
RING = 3
BANKS = 6
MOD_BANK, MISC_BANK = 6, 7

CH_IN = 0
N_IN = 51
CH_OUT = CH_IN + N_IN
N_OUT = 16
N_FFN = 2 * (2 * HALF + HALF * KT // TILES_PER_CHUNK)
CH_FFN = [CH_OUT + N_OUT, 0, 0, 0]
CH_SC = CH_FFN[0] + N_FFN
N_SC = 32
CH_FFN[1] = CH_SC + N_SC
CH_FFN[2] = CH_FFN[1] + N_FFN
CH_MLA = CH_FFN[2] + N_FFN
N_MLA = 17
CH_FFN[3] = CH_MLA + N_MLA
N_CHUNKS = CH_FFN[3] + N_FFN
AHEAD = 2
N_STREAM = N_CHUNKS + AHEAD + 1

OUT_ORDER = list(range(8, 16)) + list(range(8))

MOD_COLS = 2048
MOD_GROUPS = 11
MOD_TILES = MOD_COLS // P
MOD_PARTS = 2 * KT
M_SHIFT, M_SCALE, M_GATE = 0, 8, 16


def mod2(layer, vector):
    return 24 + 72 * layer + 8 * vector


class Cols:
    NORM_GAIN = 0
    FINAL_GAIN = 8
    G_NORM = 16
    POOL_SCALE = 64
    DN_GAIN = 72
    CONV = 73
    SC_CONV = 193
    G_QA = 217
    G_KVA = 219
    G_Q = 220
    G_K = 222
    A_LOG = 224
    DT_BIAS = 225
    BIAS = 226
    SEL = 226 + MOD_GROUPS * MOD_TILES
    N = SEL + 15


class Const:
    IDENT, ONES = range(2)
    INCL = (2, 3)
    STRICT = (4, 5)
    LEVEL = (6, 13)
    N = 20


class Rope:
    COS, SIN, PERM = 0, L, 2 * L
    PAIR = PERM + P
    SHARED = PAIR + 14
    N = SHARED + HEADS


LEVELS = (1, 2, 4, 8, 16, 32, 64)
FWD, BWD = 0, 1


IN_TAIL = ([("u", 0), ("u", 1), ("z_dn", 0), ("u", 2), ("z_dn", 1), ("u", 3), ("z_dn", 2), ("u", 4), ("z_dn", 3),
            ("pool", 0), ("u", 5), ("z_dn", 4), ("u", 6), ("z_dn", 5), ("u", 7), ("z_dn", 6), ("z_dn", 7),
            ("z_pool", 0), ("z_pool", 1), ("pool", 1)] + [("z_pool", i) for i in range(2, 8)])
IN_TAIL_GROUPS = []
for kind_, i_ in IN_TAIL:
    IN_TAIL_GROUPS += [("pool", 4 * i_ + e_) for e_ in range(4)] if kind_ == "pool" else [(kind_, i_)]

MOVING_CHUNK = "moving"


class Together:

    def __init__(self, groups, k):
        self.groups, self.k = groups, k


FFN_FIRST, SC_FIRST, IN_FIRST, OUT_FIRST, MLA_FIRST = 4, 6, 4, 6, 4


def mark_plan():
    stages = {}
    before = [0] * (N_CHUNKS + 1)
    groups_before = {}
    count = groups = 0

    def stage(name, first_chunk, sizes):
        nonlocal count, groups
        groups_before[name] = groups
        done = []
        tile = first_chunk * TILES_PER_CHUNK
        for n in sizes:
            if n == MOVING_CHUNK:
                before[tile // TILES_PER_CHUNK] = count
                tile += TILES_PER_CHUNK
                for _ in range(8):
                    count += 1
                    done.append(count)
                groups += 8
                continue
            turn = n if isinstance(n, Together) else Together(1, n)
            for j in range(turn.k):
                for _ in range(turn.groups):
                    if tile % TILES_PER_CHUNK == 0:
                        before[tile // TILES_PER_CHUNK] = count
                    tile += 1
                    if tile % TILES_PER_CHUNK == 0 or j == turn.k - 1:
                        count += 1
                    if j == turn.k - 1:
                        done.append(count)
            groups += turn.groups
        stages[name] = done

    stage("in", CH_IN, [Together(IN_FIRST, 8)] + [8] * (25 - IN_FIRST)
          + [2 if kind == "pool" else 8 for kind, _ in IN_TAIL_GROUPS])
    stage("out", CH_OUT, [Together(OUT_FIRST, 16)] + [16] * (8 - OUT_FIRST))
    for n in range(4):
        if n == 1:
            stage("sc", CH_SC, [Together(SC_FIRST, 8)] + [8] * (32 - SC_FIRST))
        if n == 3:
            stage("mla", CH_MLA, [Together(MLA_FIRST, 8)] + [2] * 12 + [1] * 8 + [MOVING_CHUNK] + [8] * 8)
        for half in range(2):
            stage(("ffn", n, half), CH_FFN[n] + half * N_FFN // 2,
                  [Together(FFN_FIRST, 8)] + [8] * (2 * HALF - FFN_FIRST) + [HALF] * KT)
    before[N_CHUNKS] = count
    return before, stages, groups_before


CHUNK_BEFORE, GROUP_DONE, GROUPS_BEFORE = mark_plan()


def two_block_kernel(nc, stream, modstream, tokens, ctx2, conds, cols_in, consts_in, rope_tab, count_in, out):
    ctx = ExitStack()

    def sem(name):
        return ctx.enter_context(nc.semaphore(name))

    class Scope:

        def __enter__(self):
            self.stack = ExitStack()
            return self

        def __exit__(self, *_):
            self.stack.close()

        def __call__(self, name, shape, dt=F32):
            return self.stack.enter_context(nc.sbuf_tensor(name, shape, dt))

    def sb(name, shape, dt=F32):
        return ctx.enter_context(nc.sbuf_tensor(name, shape, dt))

    h = sb("h", [P, KT, T])
    w_raw = sb("w_raw", [P, RING, CHUNK])
    w_hi = sb("w_hi", [P, RING, CHUNK], F32R)
    w_lo = sb("w_lo", [P, RING, CHUNK], F32R)
    cols = sb("cols", [P, Cols.N])
    mods = sb("mods", [P, MOD_GROUPS * MOD_TILES, 2])
    consts = sb("consts", [P, Const.N, P])
    gains = sb("gains", [P, 7, KT, 2])
    gates = sb("gates", [P, 6, KT, 2])

    with Scope() as s:
        n_hi = s("n_hi", [P, KT, T], F32R)
        n_lo = s("n_lo", [P, KT, T], F32R)
    gdn_names = ["diff", "dec", "a", "at", "xm", "xt", "t1", "rhs", "vnew", "pt", "qdec", "ktok"]
    W = [{}, {}]
    with Scope() as s:
        for d in (FWD, BWD):
            for name in gdn_names[:8]:
                W[d][name] = s(f"gdn_{name}{d}", [P, 4, P])
    sb("n_space", [P, 2, KT, T])

    with Scope() as s:
        kT = s("kT", [P, HEADS, T])
        qT = s("qT", [P, HEADS, L])
        v_tok = s("v_tok", [P, 4, HEADS, P])
        z_dn = s("z_dn", [P, HEADS, L])
        y_pool = s("y_pool", [P, KT, L])
        mod_raw = s("mod_raw", [P, 3, CHUNK])
        mod_row = s("mod_row", [P, 512])
        cond = s("cond", [P, 2, KT, 32])
        gb = s("gb", [64, T])
        gb_tok = s("gb_tok", [P, 4, 64])
        cum = s("cum", [P, 4, 16])
        e_cum = s("e_cum", [P, 4, 16])
        be_cum = s("be_cum", [P, 4, 16])
        tot = s("tot", [P, 4, 16])
        e_tot = s("e_tot", [P, 4, 16])
        e_tail = s("e_tail", [P, 4, 16])
        log_a = s("log_a", [16, 1])
        with Scope() as s2:
            pad = s2("pad", [P, 2, 2, L + CONV - 1])
            conv = s2("conv", [P, 2, T])
            act_out = s2("act_out", [P, 2, T])
            upad = s2("upad", [P, 2, ROWS, GRID_W + 16])
            box = s2("box", [P, 2, ROWS, GRID_W + 16])
            boxr = s2("boxr", [P, 2, ROWS, GRID_W])
            u_hi = s2("u_hi", [P, 4, L], F32R)
            u_lo = s2("u_lo", [P, 4, L], F32R)
            inv_cnt = s2("inv_cnt", [P, 4, GRID_W])
            rk = s2("rk", [HEADS, T])
            rq = s2("rq", [HEADS, L])
        with Scope() as s2:
            for d in (FWD, BWD):
                for name in gdn_names[8:]:
                    W[d][name] = s2(f"gdn_{name}{d}", [P, 4, P])
            state = s2("state", [P, 2, HEADS, P])
            o_sum = s2("o_sum", [P, HEADS, L])
    with Scope() as s:
        nt = s("nt", [P, 2, T])
        sq_acc = s("sq_acc", [P, T])
        rstd = s("rstd", [P, T])
        with Scope() as s2:
            g_hi = s2("g_hi", [P, HALF, T], F32R)
            g_lo = s2("g_lo", [P, HALF, T], F32R)
            silu = s2("silu", [P, 2, T])
            prod = s2("prod", [P, 2, T])
            sc_pad = s2("sc_pad", [P, 2, 2, L + 2])
            sc_conv = s2("sc_conv", [P, T])
        with Scope() as s2:
            cq = s2("cq", [P, 2, L])
            ckv = s2("ckv", [P, T])
            kr = s2("kr", [P, T])
            kr_rot = s2("kr_rot", [P, T])
            a_sq = s2("a_sq", [P, 3, T])
            a_rstd = s2("a_rstd", [P, 2, T])
            c_hi = s2("c_hi", [P, 3, T], F32R)
            c_lo = s2("c_lo", [P, 3, T], F32R)
            q_nope = s2("q_nope", [P, HEADS, L])
            q_rope = s2("q_rope", [P, HEADS, L])
            k_nope = s2("k_nope", [P, HEADS, T])
            k_rope = s2("k_rope", [P, HEADS // 2, T])
            v_att = s2("v_att", [P, 4, HEADS, P])
            probs = s2("probs", [P, 2, T])
            probs_t = s2("probs_t", [P, 4, L])
            rot = s2("rot", [P, 2, L])
            smax = s2("smax", [P, 2])
            ssum = s2("ssum", [P, 2])
            rope = s2("rope", [P, Rope.N])

    bank = [ctx.enter_context(nc.psum_tensor(f"bank{b}", [P, 512], F32)) for b in range(8)]

    raw_full = [sem(f"raw_full{i}") for i in range(RING)]
    mod_full = [sem(f"mod_full{i}") for i in range(3)]
    cond_in = sem("cond_in")
    const_in = sem("const_in")
    masks_in = sem("masks_in")
    tokens_in = sem("tokens_in")
    ctx2_in = sem("ctx2_in")
    rope_in_sem = sem("rope_in")
    out_done = sem("out_done")
    w_hi_ready = sem("w_hi_ready")
    w_lo_ready = sem("w_lo_ready")
    linear_done = sem("linear_done")
    groups_read = sem("groups_read")
    cond_ready = sem("cond_ready")
    mod_used = sem("mod_used")
    mod_copied = sem("mod_copied")
    mod_turned = sem("mod_turned")
    mod_ready = sem("mod_ready")
    gains_ready = sem("gains_ready")
    sq_ready = sem("sq_ready")
    sum_ready = sem("sum_ready")
    ms_ready = sem("ms_ready")
    rstd_ready = sem("rstd_ready")
    rstd_spread = sem("rstd_spread")
    scaled = sem("scaled")
    norm_hi = sem("norm_hi")
    normed = sem("normed")
    gate_ready = sem("gate_ready")
    hid_hi = sem("hid_hi")
    hid_lo = sem("hid_lo")
    dve_step = sem("dve_step")
    dve_count = [0]
    dve_loop = [0]

    def C(i, rows=P):
        return consts[0:rows, i, :]

    def col(i, n=1):
        return cols[:, i:i + n]

    def step(ins):
        dve_count[0] += 1
        ins.then_inc(dve_step, 1)
        nc.vector.wait_ge(dve_step, dve_loop[0] + dve_count[0])

    def load_chunk(sp, i, slot):
        sp.dma_start(w_raw[:, slot, :], stream[i]).then_inc(raw_full[slot], 16)

    def load_mod(sp, m, slot):
        sp.dma_start(mod_raw[:, slot, :], modstream[m]).then_inc(mod_full[slot], 16)

    def stream_loads(sp, first, last):
        while first < last and first % RING:
            sp.wait_ge(w_lo_ready, first - RING + 1)
            load_chunk(sp, first, first % RING)
            first += 1
        rounds = (last - first) // RING
        if rounds > 0:
            with sp.Fori(0, rounds) as r:
                for s_ in range(RING):
                    sp.wait_ge(w_lo_ready, r * RING + (first + s_ - RING + 1))
                    load_chunk(sp, r * RING + (first + s_), s_)
            first += rounds * RING
        while first < last:
            sp.wait_ge(w_lo_ready, first - RING + 1)
            load_chunk(sp, first, first % RING)
            first += 1

    MOD_EARLY = MOD_PARTS
    MOD_ALL = MOD_GROUPS * MOD_PARTS
    AFTER_IN = N_IN + AHEAD + 1 + RING

    def sp_program(sp):
        sp.dma_start(cond[:], conds[:]).then_inc(cond_in, 16)
        for m in range(3):
            load_mod(sp, m, m)
        sp.dma_start(h[:], tokens[:]).then_inc(tokens_in, 16)
        sp.dma_start(cols[:], cols_in[:]).then_inc(const_in, 16)
        sp.dma_start(consts[:, 0:2, :], consts_in[:, 0:2, :]).then_inc(const_in, 16)
        for m in range(3, MOD_EARLY):
            sp.wait_ge(mod_used, m - 2)
            load_mod(sp, m, m % 3)
        for i in range(RING):
            load_chunk(sp, i, i)
        sp.dma_start(consts[:, 2:, :], consts_in[:, 2:, :]).then_inc(masks_in, 16)
        sp.dma_start(inv_cnt[:], count_in[:]).then_inc(masks_in, 16)
        stream_loads(sp, RING, AFTER_IN)
        sp.wait_ge(normed, KT)
        sp.dma_start(h[:, :, L:T], ctx2[:]).then_inc(ctx2_in, 16)
        late = MOD_ALL - MOD_EARLY
        with sp.Fori(0, late // 3) as r:
            for s_ in range(3):
                sp.wait_ge(mod_used, r * 3 + (MOD_EARLY + s_ - 2))
                load_mod(sp, r * 3 + (MOD_EARLY + s_), (MOD_EARLY + s_) % 3)
        for m in range(MOD_ALL - late % 3, MOD_ALL):
            sp.wait_ge(mod_used, m - 2)
            load_mod(sp, m, m % 3)
        stream_loads(sp, AFTER_IN, N_STREAM)

    def low_half(pool, i, slot):
        pool.wait_ge(w_hi_ready, i + 1)
        nc.gpsimd.tensor_tensor(w_lo[:, slot, :], w_raw[:, slot, :], w_hi[:, slot, :].bitcast(F32),
                                ALU.subtract).then_inc(w_lo_ready, 1)

    def low_halves(pool, first, last):
        with pool.Fori(0, (last - first) // RING) as r:
            for s_ in range(RING):
                low_half(pool, r * RING + (first + s_), s_)

    def pool_program(pool):
        before_recur = N_IN + AHEAD + 1
        assert before_recur % RING == 0
        low_halves(pool, 0, before_recur)
        pool_recur(pool)
        pool_out(pool)
        low_halves(pool, before_recur, N_STREAM)
        for i in range(N_STREAM - N_STREAM % RING, N_STREAM):
            low_half(pool, i, i % RING)

    def product3(pe, out_ap, tile, hi, lo, start, stop, before_low=None):
        slot, j = tile // TILES_PER_CHUNK % RING, tile % TILES_PER_CHUNK
        wh, wl = w_hi[:, slot, j * P:(j + 1) * P], w_lo[:, slot, j * P:(j + 1) * P]
        nc.tensor.matmul(out_ap, wl, hi, start=start, stop=False)
        nc.tensor.matmul(out_ap, wh, hi, start=False, stop=False)
        if before_low is not None:
            before_low()
        return nc.tensor.matmul(out_ap, wh, lo, start=False, stop=stop)

    def linear(pe, key, sizes, first_chunk, rhs, width, group0=0, chunk_off=0, group_off=0,
               before=None, after=None):
        tile = first_chunk * TILES_PER_CHUNK
        first = group0
        for n in sizes:
            turn = n if isinstance(n, Together) else Together(1, n)
            for k in range(turn.k):
                for e in range(first, first + turn.groups):
                    g = GROUPS_BEFORE[key] + e
                    if k == 0 and g >= BANKS:
                        pe.wait_ge(groups_read, g - BANKS + 1 + group_off)
                    if tile % TILES_PER_CHUNK == 0:
                        pe.wait_ge(w_lo_ready, tile // TILES_PER_CHUNK + 1 + chunk_off)
                    before_low = before(e, k) if before is not None else None
                    hi, lo = rhs(e, k)
                    w = width(e) if callable(width) else width
                    last = product3(pe, bank[g % BANKS][:, 0:w], tile, hi, lo, k == 0, k == turn.k - 1,
                                    before_low)
                    tile += 1
                    if tile % TILES_PER_CHUNK == 0 or k == turn.k - 1:
                        last.then_inc(linear_done, 1)
            first += turn.groups
            if after is not None:
                for e in range(first - turn.groups, first):
                    after(e)

    def mod_part(pe, m):
        g, q = m // MOD_PARTS, m % MOD_PARTS
        k, half = q // 2, q % 2
        pe.wait_ge(mod_full[m % 3], 16 * (m // 3 + 1))
        if q == 0 and g:
            pe.wait_ge(mod_copied, g)
        for jj in range(2):
            j = 2 * half + jj
            which = 0 if g * MOD_COLS + j * 512 < 3 * D else 1
            last = nc.tensor.matmul(bank[MOD_BANK][32 * j:32 * j + 32, :], cond[:, which, k, :],
                                    mod_raw[:, m % 3, jj * 512:(jj + 1) * 512],
                                    start=(k == 0), stop=(k == KT - 1))
        last.then_inc(mod_used, 1)

    def mod_turn(pe, g, free=None):
        pe.wait_ge(mod_copied, g + 1)
        if g:
            pe.wait_ge(mod_ready, g)
        for b in range(4):
            last = nc.tensor.transpose(bank[MISC_BANK][:, b * P:(b + 1) * P], mod_row[:, b * P:(b + 1) * P],
                                       C(Const.IDENT))
        last.then_inc(mod_turned, 1)

    def act_mod_copy(act, g):
        act.wait_ge(mod_used, MOD_PARTS * (g + 1))
        if g:
            act.wait_ge(mod_turned, g)
        nc.scalar.copy(mod_row[:], bank[MOD_BANK][:]).then_inc(mod_copied, 1)

    def dve_mod_bias(dve, g):
        dve.wait_ge(mod_turned, g + 1)
        turned = bank[MISC_BANK][:].rearrange("p (b j c) -> p j b c", b=4, j=4)[:, :, :, 0:2]
        t0 = g * MOD_TILES
        bias = col(Cols.BIAS + t0, MOD_TILES).rearrange("p (j b) -> p j b", j=4)
        for c in range(2):
            ins = nc.vector.tensor_tensor(
                mods[:, t0:t0 + MOD_TILES, c].rearrange("p (j b) -> p j b", j=4),
                turned[:, :, :, c], bias, ALU.add)
            if c:
                ins.then_inc(mod_ready, 1)

    NORMS = [(Cols.NORM_GAIN, M_SHIFT, M_SCALE)]
    for layer in range(2):
        for v in range(3):
            NORMS.append((Cols.G_NORM + 24 * layer + 8 * v, mod2(layer, 3 * v), mod2(layer, 3 * v + 1)))
    GATES = [(mod2(0, 2), 0.5), (mod2(0, 5), 1.0), (mod2(0, 8), 0.5),
             (mod2(1, 2), 0.5), (mod2(1, 5), 1.0), (mod2(1, 8), 0.5)]

    def dve_gain(dve, i):
        gain, _, scale = NORMS[i]
        for c in range(2):
            last = nc.vector.scalar_tensor_tensor(gains[:, i, :, c], mods[:, scale:scale + KT, c], 1.0,
                                                  col(gain, KT), ALU.add, ALU.mult)
        return last

    def norm_rows(width):
        return rstd[0:width // P, 0:P]

    def sum_bank(m):
        return MOD_BANK if m else MISC_BANK

    def norm_sum(pe, m, width):
        tiles = width // P
        for last_tile, src in enumerate((sq_acc, nt[:, 1, :])):
            pe.wait_ge(sq_ready, 2 * SQ_ROUND[m] + last_tile + 1)
            for t in range(tiles):
                last = nc.tensor.matmul(bank[sum_bank(m)][0:tiles, 0:P], col(Cols.SEL + 7 - t, tiles),
                                        src[:, t * P:(t + 1) * P], start=(last_tile == t == 0),
                                        stop=(last_tile == 1 and t == tiles - 1))
        last.then_inc(sum_ready, 1)

    def norm_spread(pe, m, width):
        tiles = width // P
        pe.wait_ge(rstd_ready, m + 1)
        for t in range(tiles):
            last = nc.tensor.matmul(bank[MISC_BANK][:, t * P:(t + 1) * P],
                                    C(Const.IDENT, tiles)[:, t:t + 1].to_broadcast([tiles, P]), norm_rows(width),
                                    start=True, stop=True)
        last.then_inc(rstd_spread, 1)

    def dve_mean_square(dve, m, width):
        rows = norm_rows(width)
        dve.wait_ge(sum_ready, m + 1)
        step(nc.vector.tensor_scalar(rows, bank[sum_bank(m)][0:width // P, 0:P], 1.0 / D, EPS, ALU.mult, ALU.add))
        nc.vector.reciprocal(rows, rows).then_inc(ms_ready, 1)

    def act_rstd(act, m, width):
        act.wait_ge(ms_ready, m + 1)
        nc.scalar.activation(norm_rows(width), norm_rows(width), ACT.Sqrt).then_inc(rstd_ready, 1)

    def sides(width):
        return [(0, slice(0, L)), (1, slice(L, T))][:width // L]

    def dve_norm(dve, i, m, width):
        if m:
            dve_mean_square(dve, m, width)
        dve.wait_ge(rstd_spread, m + 1)

        def low(k):
            dve.wait_ge(norm_hi, KT * i + k + 1)
            shift = NORMS[i][1]
            for c, s_ in sides(width):
                last = nc.vector.scalar_tensor_tensor(n_lo[:, k, s_], nt[:, k % 2, s_],
                                                      mods[:, shift + k, c:c + 1],
                                                      n_hi[:, k, s_].bitcast(F32), ALU.add, ALU.subtract)
            last.then_inc(normed, 1)

        for k in range(KT):
            if k >= 2:
                dve.wait_ge(normed, KT * i + k - 1)
            for c, s_ in sides(width):
                last = nc.vector.scalar_tensor_tensor(nt[:, k % 2, s_], h[:, k, s_],
                                                      gains[:, i, k, c:c + 1], bank[MISC_BANK][:, s_],
                                                      ALU.mult, ALU.mult)
            last.then_inc(scaled, 1)
            if k:
                low(k - 1)
        low(KT - 1)

    def act_norm(act, i, m, width):
        if m:
            act_rstd(act, m, width)
        shift = NORMS[i][1]
        for k in range(KT):
            act.wait_ge(scaled, KT * i + k + 1)
            for c, s_ in sides(width):
                last = nc.scalar.activation(n_hi[:, k, s_], nt[:, k % 2, s_], ACT.Identity,
                                            bias=mods[:, shift + k, c:c + 1])
            last.then_inc(norm_hi, 1)

    def dve_square(dve, k, s_):
        if k == 0:
            step(nc.vector.tensor_tensor(sq_acc[:, s_], h[:, 0, s_], h[:, 0, s_], ALU.mult))
            return
        square = nc.vector.tensor_tensor(nt[:, k % 2, s_], h[:, k, s_], h[:, k, s_], ALU.mult)
        if k == KT - 1:
            square.then_inc(sq_ready, 1)
            return
        step(square)
        ins = nc.vector.tensor_tensor(sq_acc[:, s_], sq_acc[:, s_], nt[:, k % 2, s_], ALU.add)
        if k == KT - 2:
            ins.then_inc(sq_ready, 1)
        else:
            step(ins)

    SQUARE_STEPS = 2 * (KT - 2)
    SQ_ROUND = {0: 0}

    def split_ahead(act, i, chunk_off=0, mark_off=0, turn_off=0):
        c = i + AHEAD
        act.wait_ge(raw_full[c % RING], 16 * (c // RING + 1) + turn_off)
        if i >= 1:
            act.wait_ge(linear_done, CHUNK_BEFORE[i] + mark_off)
        nc.scalar.copy(w_hi[:, c % RING, :], w_raw[:, c % RING, :]).then_inc(w_hi_ready, 1)

    def pe_start(pe):
        pe.wait_ge(cond_ready, 1)
        for q in range(MOD_PARTS):
            mod_part(pe, q)
            if q == MOD_PARTS - 4:
                pe.wait_ge(const_in, 16 * 2)
                norm_sum(pe, 0, T)
        pe.wait_ge(ms_ready, 1)
        mod_turn(pe, 0)
        pe.wait_ge(mod_ready, 1)
        norm_spread(pe, 0, T)

    def act_start(act):
        act.wait_ge(cond_in, 16)
        nc.scalar.activation(cond[:], cond[:], ACT.Silu).then_inc(cond_ready, 1)
        act_rstd(act, 0, T)
        act_mod_copy(act, 0)
        act.wait_ge(const_in, 16 * 2)
        for i in (-2, -1):
            split_ahead(act, i)
        act_norm(act, 0, 0, T)

    def dve_start(dve):
        dve.wait_ge(tokens_in, 16)
        for k in range(KT):
            dve_square(dve, k, slice(0, T))
        dve_mean_square(dve, 0, T)
        dve.wait_ge(const_in, 16 * 2)
        dve_mod_bias(dve, 0)
        dve.wait_ge(mod_ready, 1)
        step(dve_gain(dve, 0))
        dve_norm(dve, 0, 0, T)

    TAIL = 1 + 3 * HEADS
    group_of = {what: TAIL + n for n, what in enumerate(IN_TAIL_GROUPS)}
    conv_done = sem("conv_done")
    silu_done = sem("silu_done")
    tile_sq = sem("tile_sq")
    tile_used = sem("tile_used")
    vtok_done = sem("vtok_done")
    pads_clear = sem("pads_clear")
    sums_read = sem("sums_read")
    box_done = sem("box_done")
    u_hi_ready = sem("u_hi_ready")
    u_lo_ready = sem("u_lo_ready")
    y_done = sem("y_done")
    kq_ms = sem("kq_ms")
    kq_rstd = sem("kq_rstd")
    kq_bc = sem("kq_bc")
    kq_scaled = sem("kq_scaled")
    ab_sem = sem("ab_sem")
    ab_act = sem("ab_act")
    gb_ready = sem("gb_ready")
    gb_turned = sem("gb_turned")
    gb_tok_ready = sem("gb_tok_ready")
    cum_summed = sem("cum_summed")
    cum_ready = sem("cum_ready")
    cum_exp = sem("cum_exp")
    decay_ready = sem("decay_ready")

    POST_LAG = 4

    def conv_width(ci):
        return T if ci < 16 else L

    def done_in(g):
        return GROUP_DONE["in"][g]

    def running_sums(pe):
        pe.wait_ge(gb_ready, 1)
        for t in range(4):
            last = nc.tensor.transpose(bank[MISC_BANK][:, t * 64:(t + 1) * 64], gb[:, t * P:(t + 1) * P],
                                       C(Const.IDENT, 64)[:, 0:64])
        last.then_inc(gb_turned, 1)
        pe.wait_ge(gb_tok_ready, 1)
        pe.wait_ge(masks_in, 16 * 2)
        for d in (FWD, BWD):
            nc.tensor.matmul(bank[MOD_BANK][:, 32 * d:32 * d + 32], C(Const.INCL[d]),
                             gb_tok[:, :, 8 * d:8 * d + 8], start=True, stop=True)
        nc.tensor.matmul(bank[MOD_BANK][:, 64:128], C(Const.ONES), gb_tok[:, :, 0:16],
                         start=True, stop=True).then_inc(cum_summed, 1)

    def pe_in(pe):
        before = pe_operands(pe, 0)

        def post(ci):
            w = conv_width(ci)
            if 8 <= ci < 16:
                pe.wait_ge(silu_done, ci + 1)
                if ci == 8:
                    pe.wait_ge(sums_read, 1)
                else:
                    pe.wait_ge(vtok_done, ci - 8)
                for t in range(4):
                    last = nc.tensor.transpose(bank[MISC_BANK][:, t * P:(t + 1) * P],
                                               act_out[:, ci % 2, t * P:(t + 1) * P], C(Const.IDENT))
            else:
                hd = ci % 8
                pe.wait_ge(tile_sq, ci + 1 if ci < 8 else ci - 7)
                b = MISC_BANK if ci < 8 else MOD_BANK
                last = nc.tensor.matmul(bank[b][0:HEADS, 0:w], col(Cols.SEL + 7 - hd, HEADS),
                                        act_out[:, ci % 2, 0:w], start=(hd == 0), stop=(hd == 7))
            last.then_inc(tile_used, 1)

        def after(g):
            if 0 <= g - POST_LAG < 24:
                post(g - POST_LAG)

        def full(g, k):
            return n_hi[:, k, :], n_lo[:, k, :]

        def x_only(g, k):
            return n_hi[:, k, 0:L], n_lo[:, k, 0:L]

        def pooled(g, k):
            d = 2 * (IN_TAIL_GROUPS[g - TAIL][1] % 4 // 2) + k
            return u_hi[:, d, :], u_lo[:, d, :]

        def wait_pooled(g, k):
            e = IN_TAIL_GROUPS[g - TAIL][1]
            pe.wait_ge(u_lo_ready, 4 * (e // 4) + 2 * (e % 4 // 2) + k + 1)

        linear(pe, "in", [Together(IN_FIRST, 8)] + [8] * (17 - IN_FIRST), CH_IN, full, T, before=before, after=after)
        linear(pe, "in", [8] * 8, CH_IN + 17, x_only, L, group0=17, after=after)
        for n, (kind, e) in enumerate(IN_TAIL):
            if kind == "pool":
                linear(pe, "in", [2] * 4, CH_IN + TAIL + n, pooled, L, group0=group_of["pool", 4 * e],
                       before=wait_pooled)
                continue
            linear(pe, "in", [8], CH_IN + TAIL + n, x_only, L, group0=group_of[kind, e],
                   after=after if n < 3 else None)
            if (kind, e) == ("z_pool", 6):
                running_sums(pe)
        pe.wait_ge(kq_rstd, 1)
        for j in range(2 * HEADS):
            hd, (src, w) = j % HEADS, ((rk, T), (rq, L))[j // HEADS]
            if j < BANKS:
                pe.wait_ge(groups_read, 57)
            else:
                pe.wait_ge(kq_scaled, j - BANKS + 1)
            nc.tensor.matmul(bank[j % BANKS][:, 0:w], C(Const.IDENT, HEADS)[:, hd:hd + 1].to_broadcast([HEADS, P]),
                             src[:, 0:w], start=True, stop=True).then_inc(kq_bc, 1)

    IN_CHUNK_GROUPS = ([[]] * (IN_FIRST - 1) + [list(range(IN_FIRST))] + [[g] for g in range(IN_FIRST, TAIL)]
                       + [[group_of[kind, 4 * e + j] for j in range(4)] if kind == "pool" else [group_of[kind, e]]
                          for kind, e in IN_TAIL])

    def act_in(act):
        def finish_conv(ci):
            w = conv_width(ci)
            act.wait_ge(conv_done, ci + 1)
            if ci < 8:
                dest = kT[:, ci, :]
            elif ci < 16:
                dest = act_out[:, ci % 2, :]
            else:
                dest = qT[:, ci - 16, :]
            if 8 <= ci < 16:
                act.wait_ge(tile_used, ci - 1)
            nc.scalar.activation(dest, conv[:, ci % 2, 0:w], ACT.Silu).then_inc(silu_done, 1)
            if not 8 <= ci < 16:
                if ci >= 2:
                    act.wait_ge(tile_used, ci - 1)
                act.wait_ge(silu_done, ci + 1)
                nc.scalar.activation(act_out[:, ci % 2, 0:w], dest, ACT.Square).then_inc(tile_sq, 1)

        def u_high(ui):
            act.wait_ge(box_done, ui + 1)
            nc.scalar.copy(u_hi[:, ui % 4, :], boxr[:, ui % 2].rearrange("p r c -> p (r c)")).then_inc(u_hi_ready, 1)

        def unit_length():
            act.wait_ge(kq_ms, 2)
            nc.scalar.activation(rk[:], rk[:], ACT.Sqrt)
            nc.scalar.activation(rq[:], rq[:], ACT.Sqrt).then_inc(kq_rstd, 1)

        def decay_and_beta():
            act.wait_ge(ab_sem, 1)
            nc.scalar.activation(conv[0:16, 1, :], conv[0:16, 0, :], ACT.Exp, scale=-1.0).then_inc(ab_act, 1)
            nc.scalar.activation(gb[32:48, :], gb[32:48, :], ACT.Exp, scale=-1.0).then_inc(ab_act, 1)
            nc.scalar.activation(log_a[:], cols[0:16, Cols.A_LOG:Cols.A_LOG + 1], ACT.Exp).then_inc(ab_act, 1)
            act.wait_ge(ab_act, 3)
            nc.scalar.activation(conv[0:16, 1, :], conv[0:16, 1, :], ACT.Ln, bias=1.0).then_inc(ab_act, 1)

        for i, groups in enumerate(IN_CHUNK_GROUPS):
            split_ahead(act, i)
            for g in groups:
                act.wait_ge(linear_done, done_in(g))
                src = bank[g % BANKS]
                if g == 0:
                    nc.scalar.copy(gb[:], src[0:64, :]).then_inc(groups_read, 1)
                elif g <= 24:
                    ci = g - 1
                    segs = conv_width(ci) // L
                    if ci == 0:
                        act.wait_ge(pads_clear, 2)
                    if ci >= 2:
                        act.wait_ge(conv_done, ci - 1)
                    nc.scalar.copy(pad[:, ci % 2, 0:segs, CONV // 2:CONV // 2 + L],
                                   src[:, 0:segs * L].rearrange("p (a t) -> p a t", a=segs)).then_inc(groups_read, 1)
                    if ci:
                        finish_conv(ci - 1)
                    continue
                if g < TAIL:
                    continue
                kind, e = IN_TAIL_GROUPS[g - TAIL]
                if kind == "u":
                    ui = e
                    if ui == 0:
                        finish_conv(23)
                    if ui >= 2:
                        act.wait_ge(u_lo_ready, ui - 1)
                    nc.scalar.copy(upad[:, ui % 2, :, 8:8 + GRID_W],
                                   src[:, 0:L].rearrange("p (r c) -> p r c", r=ROWS)).then_inc(groups_read, 1)
                    if ui % 4:
                        u_high(ui - 1)
                elif kind == "pool":
                    nc.scalar.activation(y_pool[:, e, :], src[:, 0:L], ACT.Identity,
                                         scale=col(Cols.POOL_SCALE + e)).then_inc(groups_read, 1)
                elif kind == "z_pool":
                    z = e
                    if z >= 2:
                        act.wait_ge(y_done, z - 1)
                    else:
                        act.wait_ge(tile_used, 24)
                    nc.scalar.activation(act_out[:, z % 2, 0:L], src[:, 0:L], ACT.Silu).then_inc(groups_read, 1)
                else:
                    nc.scalar.activation(z_dn[:, e, :], src[:, 0:L], ACT.Silu).then_inc(groups_read, 1)
                if (kind, e) in (("u", 4), ("z_dn", 7)):
                    u_high(3 if kind == "u" else 7)
                if (kind, e) == ("z_pool", 2):
                    decay_and_beta()
        split_ahead(act, CH_OUT)
        unit_length()
        act.wait_ge(cum_ready, 1)
        nc.scalar.activation(e_cum[:], cum[:], ACT.Exp).then_inc(cum_exp, 1)
        nc.scalar.activation(e_tot[:], tot[:], ACT.Exp).then_inc(cum_exp, 1)
        nc.scalar.activation(e_tail[:], e_tail[:], ACT.Exp).then_inc(cum_exp, 1)

    def dve_in(dve):
        nc.vector.memset(pad[:], 0.0).then_inc(pads_clear, 1)
        nc.vector.memset(upad[:], 0.0).then_inc(pads_clear, 1)

        def v_rows(vi):
            dve.wait_ge(tile_used, 8 + vi + 1)
            nc.vector.tensor_copy(v_tok[:, :, vi, :],
                                  bank[MISC_BANK][:].rearrange("p (t d) -> p t d", t=4)).then_inc(vtok_done, 1)

        for ci in range(24):
            segs = conv_width(ci) // L
            dve.wait_ge(groups_read, ci + 2)
            if ci >= 2:
                dve.wait_ge(silu_done, ci - 1)
            acc = conv[:, ci % 2, 0:segs * L].rearrange("p (a t) -> p a t", a=segs)
            for j in range(CONV):
                src, w = pad[:, ci % 2, 0:segs, j:j + L], col(Cols.CONV + ci * CONV + j)
                if j == 0:
                    ins = nc.vector.tensor_scalar(acc, src, w, None, ALU.mult)
                else:
                    ins = nc.vector.scalar_tensor_tensor(acc, src, w, acc, ALU.mult, ALU.add)
                if j < CONV - 1:
                    step(ins)
            ins.then_inc(conv_done, 1)
            if ci == 10:
                dve.wait_ge(tile_used, 8)
                nc.vector.tensor_scalar(rk[:], bank[MISC_BANK][0:HEADS, :], EPS, None, ALU.add).then_inc(sums_read, 1)
            if 11 <= ci < 19:
                v_rows(ci - 11)

        def u_low(ui):
            dve.wait_ge(u_hi_ready, ui + 1)
            nc.vector.tensor_tensor(u_lo[:, ui % 4, :], boxr[:, ui % 2].rearrange("p r c -> p (r c)"),
                                    u_hi[:, ui % 4, :].bitcast(F32), ALU.subtract).then_inc(u_lo_ready, 1)

        def rows_of(w):
            return [(max(0, r - w // 2), min(ROWS, r - w // 2 + w)) for r in range(ROWS)]

        dve.wait_ge(masks_in, 16 * 2)
        for ui in range(8):
            w = WINDOWS[ui // 2]
            u, a, b = upad[:, ui % 2], box[:, 0], box[:, 1]
            wide = GRID_W + 16
            dve.wait_ge(groups_read, group_of["u", ui] + 1)
            if ui >= 2:
                dve.wait_ge(u_lo_ready, ui - 1)
            add = lambda o, x, y: step(nc.vector.tensor_tensor(o, x, y, ALU.add))
            add(a[:, :, 1:wide], u[:, :, 0:wide - 1], u[:, :, 1:wide])
            cur, other, lo = a, b, 1
            for reach in (1, 2, 4)[:ui // 2]:
                lo2 = lo + reach
                n = wide - 2 * lo2 + 1
                add(other[:, :, lo2:lo2 + n], cur[:, :, lo2 - reach:lo2 - reach + n],
                    cur[:, :, lo2 + reach:lo2 + reach + n])
                cur, other, lo = other, cur, lo2
            c = cur[:, :, 8:8 + GRID_W]
            r_ = boxr[:, ui % 2]
            if w == 2:
                add(r_[:, 1:4], c[:, 0:3], c[:, 1:4])
                step(nc.vector.tensor_copy(r_[:, 0:1], c[:, 0:1]))
            else:
                e = other[:, 0:3, 8:8 + GRID_W]
                add(e, c[:, 0:3], c[:, 1:4])
                if w == 4:
                    step(nc.vector.tensor_copy(r_[:, 0:1], e[:, 0:1]))
                    add(r_[:, 1:2], e[:, 0:1], c[:, 2:3])
                    add(r_[:, 2:3], e[:, 0:1], e[:, 2:3])
                    add(r_[:, 3:4], c[:, 1:2], e[:, 2:3])
                else:
                    add(r_[:, 0:1], e[:, 0:1], e[:, 2:3])
                    step(nc.vector.tensor_copy(r_[:, 1:4], r_[:, 0:1].to_broadcast([P, 3, GRID_W])))
            step(nc.vector.tensor_tensor(r_, r_, inv_cnt[:, ui // 2].unsqueeze(1).to_broadcast([P, ROWS, GRID_W]),
                                         ALU.mult))
            counts = [b_ - a_ for a_, b_ in rows_of(w)]
            for r in range(ROWS):
                ins = nc.vector.scalar_tensor_tensor(r_[:, r], r_[:, r], 1.0 / counts[r], u[:, r, 8:8 + GRID_W],
                                                     ALU.mult, ALU.subtract)
                if r == ROWS - 1:
                    ins.then_inc(box_done, 1)
                else:
                    step(ins)
            if ui == 0:
                dve.wait_ge(tile_used, 24)
                nc.vector.tensor_scalar(rq[:], bank[MOD_BANK][0:HEADS, 0:L], EPS, float(P), ALU.add, ALU.mult)\
                    .then_inc(sums_read, 1)
            if ui % 4:
                u_low(ui - 1)
            if ui % 4 == 3:
                u_low(ui)
        dve.wait_ge(silu_done, 24)
        step(nc.vector.tensor_scalar(gb[0:16, :], gb[0:16, :], cols[0:16, Cols.DT_BIAS:Cols.DT_BIAS + 1], None,
                                     ALU.add))
        nc.vector.scalar_tensor_tensor(conv[0:16, 0, :], gb[0:16, :], -1.0, gb[0:16, :],
                                       ALU.mult, ALU.max).then_inc(ab_sem, 1)
        for z in range(8):
            dve.wait_ge(groups_read, group_of["z_pool", z] + 1)
            nc.vector.tensor_tensor(y_pool[:, z, :], y_pool[:, z, :], act_out[:, z % 2, 0:L],
                                    ALU.mult).then_inc(y_done, 1)
            if z == 3:
                dve.wait_ge(ab_act, 4)
                step(nc.vector.scalar_tensor_tensor(gb[0:16, :], gb[0:16, :], 0.0, conv[0:16, 1, :],
                                                    ALU.max, ALU.add))
                step(nc.vector.tensor_scalar(gb[0:16, :], gb[0:16, :], log_a[:], -1.0, ALU.mult, ALU.mult))
                step(nc.vector.tensor_scalar(gb[32:48, :], gb[32:48, :], 1.0, None, ALU.add))
                nc.vector.reciprocal(gb[32:48, :], gb[32:48, :]).then_inc(gb_ready, 1)
            if z == 1:
                dve.wait_ge(sums_read, 2)
                nc.vector.reciprocal(rk[:], rk[:]).then_inc(kq_ms, 1)
                nc.vector.reciprocal(rq[:], rq[:]).then_inc(kq_ms, 1)
            if z == 6:
                dve.wait_ge(gb_turned, 1)
                nc.vector.tensor_copy(gb_tok[:].rearrange("p t r -> p (t r)"),
                                      bank[MISC_BANK][:, 0:256]).then_inc(gb_tok_ready, 1)
                dve.wait_ge(cum_summed, 1)
                for d in (FWD, BWD):
                    step(nc.vector.tensor_copy(cum[:, :, 8 * d:8 * d + 8],
                                               bank[MOD_BANK][:, 32 * d:32 * d + 32]
                                               .rearrange("p (t g) -> p t g", t=4)))
                step(nc.vector.tensor_copy(tot[:], bank[MOD_BANK][:, 64:128].rearrange("p (t g) -> p t g", t=4)))
                nc.vector.tensor_tensor(e_tail[:], tot[:], cum[:], ALU.subtract).then_inc(cum_ready, 1)
        dve.wait_ge(cum_exp, 3)
        step(nc.vector.tensor_tensor(be_cum[:], e_cum[:], gb_tok[:, :, 32:48], ALU.mult))
        for j in range(2 * HEADS):
            dest, w = (kT, T) if j < HEADS else (qT, L)
            dve.wait_ge(kq_bc, j + 1)
            nc.vector.tensor_tensor(dest[:, j % HEADS, :], dest[:, j % HEADS, :], bank[j % BANKS][:, 0:w],
                                    ALU.mult).then_inc(kq_scaled, 1)

    TILE_ORDER = ((2, 3, 0, 1), (3, 2, 1, 0))
    ROUNDS = [(step_, hg) for step_ in range(4) for hg in range(2)]
    g_cb, g_gram, g_kt, g_qk, g_at, g_p1, g_p2, g_p3, g_ks, g_vn, g_o, g_st = (
        sem(f"g_{n}") for n in ("cb", "gram", "kt", "qk", "at", "p1", "p2", "p3", "ks", "vn", "o", "st"))
    a_dec, a_pt, a_qd, a_kt, a_at, a_t1, a_vn = (sem(f"a_{n}") for n in ("dec", "pt", "qd", "kt", "at", "t1", "vn"))
    d_diff, d_max, d_min, d_a, d_at, d_pt, d_xm, d_xt, d_rhs, d_vdec, d_state, d_o = (
        sem(f"d_{n}") for n in ("diff", "max", "min", "a", "at", "pt", "xm", "xt", "rhs", "vdec", "state", "o"))
    p_mask, p_rhs, p_pt, p_qd, p_at = (sem(f"p_{n}") for n in ("mask", "rhs", "pt", "qd", "at"))
    X_BATCH0 = 8


    MOD_SLOTS = {"gram": 2, "at": 2, "level1": 2, "level2": 2, "level3": 2, "level4": 2, "level5": 2, "level6": 2,
                 "state": 2, "out": 2}
    mod_copies, mod_turns = {}, {}
    m = MOD_EARLY
    for r_ in range(len(ROUNDS)):
        for slot, n_parts in MOD_SLOTS.items():
            for m in range(m, m + n_parts):
                if m % MOD_PARTS == 2 and m >= 2 * MOD_PARTS:
                    mod_turns[r_, slot] = m // MOD_PARTS - 1
                if m % MOD_PARTS == MOD_PARTS - 1:
                    mod_copies[r_, slot] = m // MOD_PARTS
            m += 1
    assert m == MOD_ALL

    def b4(b):
        return bank[b][:].rearrange("p (j c) -> p j c", j=4)

    def per_batch(r):
        step_, hg = ROUNDS[r]
        return [(2 * r + d, d, TILE_ORDER[d][step_], slice(4 * hg, 4 * hg + 4), 3 * d,
                 slice(8 * d + 4 * hg, 8 * d + 4 * hg + 4)) for d in (FWD, BWD)]

    def tok(t):
        return slice(t * P, (t + 1) * P)

    def level_at(w, li):
        return w[("diff", "dec")[(li - 1) % 2]]

    def nth(per, r, e, d):
        return 2 * per * r + 2 * e + d + 1

    def pe_recur(pe):
        parts = [MOD_EARLY]

        def some_mods(r, slot):
            for _ in range(MOD_SLOTS[slot]):
                if parts[0] % MOD_PARTS == 2 and (r, slot) in mod_turns:
                    mod_turn(pe, mod_turns[r, slot])
                mod_part(pe, parts[0])
                parts[0] += 1

        def four(fn, s_):
            for j in range(4):
                last = fn(j)
            last.then_inc(s_, 1)

        pe.wait_ge(kq_scaled, 2 * HEADS)
        pe.wait_ge(cum_ready, 1)
        for r, (step_, hg) in enumerate(ROUNDS):
            batches = per_batch(r)
            with_x = step_ >= 2
            for n, d, t, hs, b0, gc in batches:
                if r:
                    pe.wait_ge(d_xt, nth(7, r - 1, 6, d))
                    if n - 2 >= X_BATCH0:
                        pe.wait_ge(d_o, n - 1 - X_BATCH0)
                four(lambda j: nc.tensor.matmul(
                    b4(b0)[:, j], gb_tok[:, t, gc][:, j:j + 1].to_broadcast([P, P]), C(Const.INCL[d]),
                    start=True, stop=True), g_cb)
            for n, d, t, hs, b0, gc in batches:
                if r:
                    pe.wait_ge(d_vdec, n - 1)
                    if ROUNDS[r - 1][0] < 3:
                        pe.wait_ge(d_state, n - 1)
                four(lambda j: nc.tensor.matmul(
                    b4(b0 + 1)[:, j], kT[:, hs, tok(t)][:, j], kT[:, hs, tok(t)][:, j],
                    start=True, stop=True), g_gram)
            for n, d, t, hs, b0, gc in batches:
                if n - 2 >= X_BATCH0:
                    pe.wait_ge(a_vn, n - 1 - X_BATCH0)
                if step_ == 3:
                    continue
                four(lambda j: nc.tensor.transpose(b4(b0 + 2)[:, j], kT[:, hs, tok(t)][:, j],
                                                   C(Const.IDENT)), g_kt)
            some_mods(r, "gram")
            for n, d, t, hs, b0, gc in batches:
                w = W[d]
                if with_x:
                    if step_ < 3:
                        pe.wait_ge(a_kt, n + 1)
                    four(lambda j: nc.tensor.matmul(
                        b4(b0 + 2)[:, j], kT[:, hs, tok(t)][:, j], qT[:, hs, tok(t)][:, j],
                        start=True, stop=True), g_qk)
                pe.wait_ge(d_a, n + 1)
                if with_x:
                    pe.wait_ge(a_qd, n - X_BATCH0 + 1)
                four(lambda j: nc.tensor.transpose(b4(b0)[:, j], w["a"][:, j], C(Const.IDENT)), g_at)
            some_mods(r, "at")
            for li in range(1, 7):
                for n, d, t, hs, b0, gc in batches:
                    w = W[d]
                    if li == 1:
                        pe.wait_ge(d_at, n + 1)
                    else:
                        pe.wait_ge(p_at, nth(5, r, li - 2, d))
                    pe.wait_ge(d_xm, nth(6, r, li - 1, d))
                    at_li = level_at(w, li)
                    four(lambda j: nc.tensor.matmul(b4(b0 + 1)[:, j], at_li[:, j], w["xm"][:, j],
                                                    start=True, stop=True), g_p1)
                some_mods(r, f"level{li}")
                for n, d, t, hs, b0, gc in batches:
                    w = W[d]
                    pe.wait_ge(a_t1, nth(6, r, li - 1, d))
                    pe.wait_ge(d_xt, nth(7, r, li - 1, d))
                    if li == 1:
                        if with_x:
                            pe.wait_ge(d_pt, n - X_BATCH0 + 1)
                        else:
                            pe.wait_ge(a_kt, n + 1)
                    if li < 6:
                        four(lambda j: nc.tensor.matmul(b4(b0 + 2)[:, j], w["xt"][:, j], w["t1"][:, j],
                                                        start=True, stop=True), g_p2)
                    if li >= 5:
                        four(lambda j: nc.tensor.matmul(b4(b0)[:, j], w["t1"][:, j], w["xt"][:, j],
                                                        start=True, stop=True), g_p3)
            for n, d, t, hs, b0, gc in batches:
                if step_:
                    pe.wait_ge(d_state, n - 3)
                    four(lambda j: nc.tensor.matmul(b4(b0 + 1)[:, j], kT[:, hs, tok(t)][:, j],
                                                    state[:, d, hs][:, j], start=True, stop=True), g_ks)
            some_mods(r, "state")
            for n, d, t, hs, b0, gc in batches:
                w = W[d]
                pe.wait_ge(d_rhs, n + 1)
                pe.wait_ge(d_xt, nth(7, r, 6, d))
                four(lambda j: nc.tensor.matmul(b4(b0 + 2)[:, j], w["xt"][:, j], w["rhs"][:, j],
                                                start=True, stop=True), g_vn)
            some_mods(r, "out")
            for n, d, t, hs, b0, gc in batches:
                w = W[d]
                if with_x:
                    pe.wait_ge(a_vn, n - X_BATCH0 + 1)
                    pe.wait_ge(p_qd, n - X_BATCH0 + 1)

                    def out_four(j):
                        nc.tensor.matmul(b4(b0)[:, j], state[:, d, hs][:, j], w["qdec"][:, j],
                                         start=True, stop=False)
                        return nc.tensor.matmul(b4(b0)[:, j], w["vnew"][:, j], w["pt"][:, j],
                                                start=False, stop=True)
                    four(out_four, g_o)
                if step_ < 3:
                    pe.wait_ge(d_vdec, n + 1)
                    four(lambda j: nc.tensor.matmul(b4(b0 + 1)[:, j], w["ktok"][:, j], w["rhs"][:, j],
                                                    start=True, stop=True), g_st)
        mod_turn(pe, MOD_GROUPS - 1)

    def act_recur(act):
        for r, (step_, hg) in enumerate(ROUNDS):
            batches = per_batch(r)
            with_x = step_ >= 2
            for n, d, t, hs, b0, gc in batches:
                w = W[d]
                if with_x:
                    act.wait_ge(d_diff, n + 1)
                    nc.scalar.activation(w["qdec"][:], b4(b0), ACT.Exp).then_inc(a_qd, 1)
                act.wait_ge(d_max, n + 1)
                nc.scalar.activation(w["dec"][:], w["dec"][:], ACT.Exp, scale=-1.0).then_inc(a_dec, 1)
                if with_x:
                    act.wait_ge(d_min, n - X_BATCH0 + 1)
                    nc.scalar.activation(w["pt"][:], w["pt"][:], ACT.Exp).then_inc(a_pt, 1)
                if step_ < 3:
                    act.wait_ge(g_kt, n + 1)
                    nc.scalar.copy(w["ktok"][:], b4(b0 + 2)).then_inc(a_kt, 1)
            if (r, "gram") in mod_copies:
                act_mod_copy(act, mod_copies[r, "gram"])
            for n, d, t, hs, b0, gc in batches:
                act.wait_ge(d_at, n + 1)
                nc.scalar.copy(W[d]["at"][:], b4(b0)).then_inc(a_at, 1)
            if (r, "at") in mod_copies:
                act_mod_copy(act, mod_copies[r, "at"])
            for li in range(1, 7):
                for n, d, t, hs, b0, gc in batches:
                    act.wait_ge(g_p1, nth(6, r, li - 1, d))
                    nc.scalar.copy(W[d]["t1"][:], b4(b0 + 1)).then_inc(a_t1, 1)
                if (r, f"level{li}") in mod_copies:
                    act_mod_copy(act, mod_copies[r, f"level{li}"])
            if (r, "state") in mod_copies:
                act_mod_copy(act, mod_copies[r, "state"])
            if with_x:
                for n, d, t, hs, b0, gc in batches:
                    act.wait_ge(d_vdec, n + 1)
                    nc.scalar.activation(W[d]["vnew"][:], b4(b0 + 2), ACT.Identity, scale=-1.0).then_inc(a_vn, 1)
            if (r, "out") in mod_copies:
                act_mod_copy(act, mod_copies[r, "out"])

    def pool_recur(pool):
        def mask(i):
            return C(i).unsqueeze(1).to_broadcast([P, 4, P])

        tt = nc.gpsimd.tensor_tensor
        pool.wait_ge(cum_ready, 1)
        for r, (step_, hg) in enumerate(ROUNDS):
            batches = per_batch(r)
            with_x = step_ >= 2
            for n, d, t, hs, b0, gc in batches:
                w = W[d]
                if r:
                    pool.wait_ge(d_xt, nth(7, r - 1, 6, d))
                beta = gb_tok[:, t, 32 + gc.start:32 + gc.stop].unsqueeze(2).to_broadcast([P, 4, P])
                tt(w["t1"][:], mask(Const.STRICT[d]), beta, ALU.mult).then_inc(p_mask, 1)
            for n, d, t, hs, b0, gc in batches:
                w = W[d]
                if r:
                    pool.wait_ge(d_vdec, n - 1)
                    if ROUNDS[r - 1][0] < 3:
                        pool.wait_ge(g_st, n - 1)
                beta = gb_tok[:, t, 32 + gc.start:32 + gc.stop].unsqueeze(2).to_broadcast([P, 4, P])
                tt(w["rhs"][:], v_tok[:, t, hs], beta, ALU.mult).then_inc(p_rhs, 1)
            if with_x:
                for n, d, t, hs, b0, gc in batches:
                    w = W[d]
                    pool.wait_ge(a_pt, n - X_BATCH0 + 1)
                    tt(w["pt"][:], w["pt"][:], mask(Const.INCL[d]), ALU.mult).then_inc(p_pt, 1)
            for li in range(2, 7):
                for n, d, t, hs, b0, gc in batches:
                    w = W[d]
                    if li == 2:
                        pool.wait_ge(a_at, n + 1)
                        pool.wait_ge(d_a, n + 1)
                    else:
                        pool.wait_ge(g_p1, nth(6, r, li - 3, d))
                    tt(level_at(w, li)[:], w["at"][:], mask(Const.LEVEL[1 - d] + li), ALU.mult).then_inc(p_at, 1)
                if li == 2 and with_x:
                    for n, d, t, hs, b0, gc in batches:
                        w = W[d]
                        pool.wait_ge(a_qd, n - X_BATCH0 + 1)
                        tt(w["qdec"][:], w["qdec"][:], qT[:, hs, tok(t)], ALU.mult).then_inc(p_qd, 1)

    def dve_recur(dve):
        def bc(ap):
            return ap.unsqueeze(2).to_broadcast([P, 4, P])

        def mask(i):
            return C(i).unsqueeze(1).to_broadcast([P, 4, P])

        def turned_groups(r, slot):
            if (r, slot) in mod_turns:
                dve_mod_bias(dve, mod_turns[r, slot])

        tt = nc.vector.tensor_tensor
        for r, (step_, hg) in enumerate(ROUNDS):
            batches = per_batch(r)
            with_x = step_ >= 2
            for n, d, t, hs, b0, gc in batches:
                w = W[d]
                m = n - X_BATCH0
                dve.wait_ge(g_cb, n + 1)
                tt(w["diff"][:], b4(b0), bc(cum[:, t, gc]), ALU.subtract).then_inc(d_diff, 1)
                dve.wait_ge(d_diff, n + 1)
                nc.vector.tensor_scalar(w["dec"][:], w["diff"][:], 0.0, None, ALU.max).then_inc(d_max, 1)
                if with_x:
                    nc.vector.tensor_scalar(w["pt"][:], w["diff"][:], 0.0, None, ALU.min).then_inc(d_min, 1)
            turned_groups(r, "gram")
            for n, d, t, hs, b0, gc in batches:
                w = W[d]
                dve.wait_ge(a_dec, n + 1)
                dve.wait_ge(p_mask, n + 1)
                step(tt(w["dec"][:], w["dec"][:], w["t1"][:], ALU.mult))
                dve.wait_ge(g_gram, n + 1)
                tt(w["a"][:], w["dec"][:], b4(b0 + 1), ALU.mult).then_inc(d_a, 1)
                dve.wait_ge(d_a, n + 1)
                step(tt(w["t1"][:], w["a"][:], mask(Const.LEVEL[d]), ALU.mult))
                tt(w["xm"][:], mask(Const.IDENT), w["t1"][:], ALU.subtract).then_inc(d_xm, 1)
                dve.wait_ge(d_xm, nth(6, r, 0, d))
                nc.vector.transpose(w["xt"][:], w["xm"][:]).then_inc(d_xt, 1)
                dve.wait_ge(g_at, n + 1)
                tt(level_at(w, 1)[:], b4(b0), mask(Const.LEVEL[1 - d] + 1), ALU.mult).then_inc(d_at, 1)
            if with_x:
                for n, d, t, hs, b0, gc in batches:
                    w = W[d]
                    m = n - X_BATCH0
                    dve.wait_ge(p_pt, m + 1)
                    dve.wait_ge(g_qk, m + 1)
                    tt(w["pt"][:], w["pt"][:], b4(b0 + 2), ALU.mult).then_inc(d_pt, 1)
            turned_groups(r, "at")
            for li in range(1, 7):
                for n, d, t, hs, b0, gc in batches:
                    w = W[d]
                    if li < 6:
                        dve.wait_ge(g_p2, nth(5, r, li - 1, d))
                        tt(w["xm"][:], w["xm"][:], b4(b0 + 2), ALU.subtract).then_inc(d_xm, 1)
                    if li < 5:
                        dve.wait_ge(d_xm, nth(6, r, li, d))
                        nc.vector.transpose(w["xt"][:], w["xm"][:]).then_inc(d_xt, 1)
                    else:
                        dve.wait_ge(g_p3, nth(2, r, li - 5, d))
                        tt(w["xt"][:], w["xt"][:], b4(b0), ALU.subtract).then_inc(d_xt, 1)
                turned_groups(r, f"level{li}")
            for n, d, t, hs, b0, gc in batches:
                w = W[d]
                dve.wait_ge(p_rhs, n + 1)
                if step_:
                    dve.wait_ge(g_ks, n - 3)
                    for j in range(4):
                        last = nc.vector.scalar_tensor_tensor(
                            w["rhs"][:, j], b4(b0 + 1)[:, j], be_cum[:, t, gc.start + j:gc.start + j + 1],
                            w["rhs"][:, j], ALU.mult, ALU.subtract)
                    last.then_inc(d_rhs, 1)
                else:
                    nc.vector.tensor_scalar(w["rhs"][:], w["rhs"][:], -1.0, None, ALU.mult).then_inc(d_rhs, 1)
            for n, d, t, hs, b0, gc in batches:
                w = W[d]
                dve.wait_ge(g_vn, n + 1)
                tt(w["rhs"][:], b4(b0 + 2), bc(e_tail[:, t, gc]), ALU.mult).then_inc(d_vdec, 1)
            turned_groups(r, "state")
            turned_groups(r, "out")
            for n, d, t, hs, b0, gc in batches:
                w = W[d]
                m = n - X_BATCH0
                st = state[:, d, hs]
                if with_x:
                    dve.wait_ge(g_o, m + 1)
                    if step_ == 2:
                        nc.vector.tensor_copy(o_sum[:, hs, tok(t)], b4(b0)).then_inc(d_o, 1)
                    else:
                        dve.wait_ge(d_o, m - 3)
                        tt(o_sum[:, hs, tok(t)], o_sum[:, hs, tok(t)], b4(b0), ALU.add).then_inc(d_o, 1)
                if step_ == 0:
                    dve.wait_ge(g_st, n + 1)
                    nc.vector.tensor_scalar(st, b4(b0 + 1), -1.0, None, ALU.mult).then_inc(d_state, 1)
                elif step_ < 3:
                    dve.wait_ge(g_st, n + 1)
                    for j in range(4):
                        last = nc.vector.scalar_tensor_tensor(
                            st[:, j], st[:, j], e_tot[:, t, gc.start + j:gc.start + j + 1], b4(b0 + 1)[:, j],
                            ALU.mult, ALU.subtract)
                    last.then_inc(d_state, 1)
        dve_mod_bias(dve, MOD_GROUPS - 1)
        dve.wait_ge(mod_ready, MOD_GROUPS)

    o_sq, o_summed, o_ms, o_rs, o_n, y_hi_ready, y_lo_ready = (
        sem(n) for n in ("o_sq", "o_summed", "o_ms", "o_rs", "o_n", "y_hi_ready", "y_lo_ready"))
    y_hi = n_hi[:].rearrange("p k (a t) -> p (k a) t", a=2)
    y_lo = n_lo[:].rearrange("p k (a t) -> p (k a) t", a=2)
    o_bc, o_gated, x_final, x_squared = (sem(n) for n in ("o_bc", "o_gated", "x_final", "x_squared"))
    o_pairs = [o_sum[:, 2 * i:2 * i + 2, :].rearrange("p a t -> p (a t)") for i in range(4)]

    def y_pair(v, i):
        return v[:, 2 * i:2 * i + 2, :].rearrange("p a t -> p (a t)")

    o_rows = rstd[0:HEADS, 0:L]
    o_squares = qT
    x_sq = [(silu, prod)[k // 4].rearrange("p a (b t) -> p (a b) t", b=2)[:, k % 4, :] for k in range(KT)]

    def pe_out(pe):
        def before(g, k):
            if g == 0 and k % 2 == 0:
                pe.wait_ge(y_lo_ready, k // 2 + 1)
            if g:
                return
            if k == 2:
                for hd in range(HEADS):
                    pe.wait_ge(o_sq, hd // 2 + 1)
                    last = nc.tensor.matmul(bank[MISC_BANK][0:HEADS, 0:L], col(Cols.SEL + 7 - hd, HEADS),
                                            o_squares[:, hd, :], start=(hd == 0), stop=(hd == HEADS - 1))
                last.then_inc(o_summed, 1)
            if 5 <= k <= 6:
                for i in (2 * k - 10, 2 * k - 9):
                    pe.wait_ge(o_rs, 1)
                    if i >= 2:
                        pe.wait_ge(o_n, i - 1)
                    for hd in (2 * i, 2 * i + 1):
                        last = nc.tensor.matmul(bank[(MOD_BANK, MISC_BANK)[i % 2]][:, hd % 2 * L:(hd % 2 + 1) * L],
                                                C(Const.IDENT, HEADS)[:, hd:hd + 1].to_broadcast([HEADS, P]),
                                                o_rows, start=True, stop=True)
                    last.then_inc(o_bc, 1)

        pe.wait_ge(d_o, 8)
        linear(pe, "out", [Together(OUT_FIRST, 16)] + [16] * (8 - OUT_FIRST), CH_OUT,
               lambda g, k: (y_hi[:, k, :], y_lo[:, k, :]), L, before=before)
        norm_sum(pe, 1, L)
        norm_spread(pe, 1, L)
        pe.wait_ge(ms_ready, 2)
        pe.wait_ge(sq_ready, 4)
        rows = bank[sum_bank(2)][0:4, 0:P]
        for t in (2, 3):
            nc.tensor.matmul(rows, col(Cols.SEL + 7 - t, 4), sq_acc[:, tok(t)], start=(t == 2), stop=False)
            nc.tensor.matmul(rows, col(Cols.SEL + 7 - t, 4), nt[:, 1, tok(t)], start=False, stop=False)
        for k in range(KT):
            pe.wait_ge(x_squared, k + 1)
            for t in (0, 1):
                last = nc.tensor.matmul(rows, col(Cols.SEL + 7 - t, 4), x_sq[k][:, tok(t)], start=False,
                                        stop=(k == KT - 1 and t == 1))
        last.then_inc(sum_ready, 1)

    def pool_out(pool):
        pool.wait_ge(d_o, 8)
        for i in range(4):
            nc.gpsimd.tensor_tensor(y_pair(z_dn, i), y_pair(z_dn, i), o_pairs[i], ALU.mult).then_inc(o_gated, 1)

    def act_out_stage(act):
        act.wait_ge(d_o, 8)
        for i in range(4):
            nc.scalar.copy(y_pair(y_hi, i), y_pair(y_pool, i)).then_inc(y_hi_ready, 1)
        split_ahead(act, CH_OUT + 1)
        split_ahead(act, CH_OUT + 2)
        act.wait_ge(o_ms, 1)
        nc.scalar.activation(o_rows, o_rows, ACT.Sqrt).then_inc(o_rs, 1)
        for i in range(4):
            split_ahead(act, CH_OUT + i + 3)
            act.wait_ge(o_n, i + 1)
            nc.scalar.copy(y_pair(y_hi, 4 + i), o_pairs[i]).then_inc(y_hi_ready, 1)
        for i in range(7, N_OUT + 1):
            split_ahead(act, CH_OUT + i)
        act_rstd(act, 1, L)
        for k in range(KT):
            act.wait_ge(x_final, k + 1)
            nc.scalar.activation(x_sq[k], h[:, k, 0:L], ACT.Square).then_inc(x_squared, 1)

    def dve_out(dve):
        dve.wait_ge(d_o, 8)
        for i in range(4):
            nc.vector.tensor_tensor(y_pair(o_squares, i), o_pairs[i], o_pairs[i], ALU.mult).then_inc(o_sq, 1)
        for i in range(4):
            dve.wait_ge(y_hi_ready, i + 1)
            nc.vector.tensor_tensor(y_pair(y_lo, i), y_pair(y_pool, i), y_pair(y_hi, i).bitcast(F32),
                                    ALU.subtract).then_inc(y_lo_ready, 1)
        dve.wait_ge(o_summed, 1)
        step(nc.vector.tensor_scalar(o_rows, bank[MISC_BANK][0:HEADS, 0:L], 1.0 / P, EPS, ALU.mult, ALU.add))
        nc.vector.reciprocal(o_rows, o_rows).then_inc(o_ms, 1)

        def out_low(i):
            dve.wait_ge(y_hi_ready, 5 + i)
            nc.vector.tensor_tensor(y_pair(y_lo, 4 + i), o_pairs[i], y_pair(y_hi, 4 + i).bitcast(F32),
                                    ALU.subtract).then_inc(y_lo_ready, 1)

        for i in range(4):
            dve.wait_ge(o_gated, i + 1)
            dve.wait_ge(o_bc, i + 1)
            nc.vector.scalar_tensor_tensor(o_pairs[i], y_pair(z_dn, i), col(Cols.DN_GAIN),
                                           bank[(MOD_BANK, MISC_BANK)[i % 2]][:], ALU.mult, ALU.mult).then_inc(o_n, 1)
            if i:
                out_low(i - 1)
        out_low(3)
        for i in range(6):
            step(dve_gain(dve, i + 1))
            tile0, factor = GATES[i]
            step(nc.vector.tensor_scalar(gates[:, i], mods[:, tile0:tile0 + KT, :], factor, None, ALU.mult))
        dve.wait_ge(ctx2_in, 16)
        for k in range(KT):
            dve_square(dve, k, slice(L, T))
        for kt in range(KT):
            g = GROUPS_BEFORE["out"] + kt
            dve.wait_ge(linear_done, GROUP_DONE["out"][kt])
            nc.vector.scalar_tensor_tensor(h[:, kt, 0:L], bank[g % BANKS][:, 0:L], mods[:, M_GATE + kt, 0:1],
                                           h[:, kt, 0:L], ALU.mult, ALU.add).then_inc(groups_read, 1)
            dve.wait_ge(groups_read, g + 1)
            dve_square(dve, kt, slice(0, L))
        dve_mean_square(dve, 1, L)
        dve.wait_ge(rstd_spread, 2)
        for kt in range(KT):
            nc.vector.scalar_tensor_tensor(h[:, kt, 0:L], h[:, kt, 0:L], col(Cols.FINAL_GAIN + kt),
                                           bank[MISC_BANK][:, 0:L], ALU.mult, ALU.mult).then_inc(x_final, 1)

    SQ_ROUND.update({1: 2, 3: 4, 4: 5, 5: 7, 6: 9, 7: 10})

    FFNS = [(1, 2, 0, 0), (3, 4, 2, 30), (4, 5, 3, 52), (6, 7, 5, 74)]
    SC = (2, 3, 1, 22)
    MLA = (5, 6, 4, 0)
    MARKS = GROUP_DONE[("ffn", 0, 1)][-1] - GROUP_DONE[("ffn", 0, 0)][-1]
    HALF_CHUNKS, HALF_GROUPS = N_FFN // 2, 2 * HALF + KT

    def ffn_width(n):
        return T if n < 3 else L

    def pe_operands(pe, i):
        def before(g, k):
            if g:
                return None
            pe.wait_ge(norm_hi, KT * i + k + 1)
            return lambda: pe.wait_ge(normed, KT * i + k + 1)
        return before

    def pe_ffn(pe, n):
        i, m, _, hid0 = FFNS[n]
        w, key, first = ffn_width(n), ("ffn", n, 0), CH_FFN[n]
        if n:
            norm_sum(pe, m, w)
        norm_spread(pe, m, w)
        with pe.Fori(0, 2) as half:
            linear(pe, key, [Together(FFN_FIRST, KT)] + [KT] * (2 * HALF - FFN_FIRST), first,
                   lambda g, k: (n_hi[:, k, 0:w], n_lo[:, k, 0:w]), w,
                   chunk_off=half * HALF_CHUNKS, group_off=half * HALF_GROUPS, before=pe_operands(pe, i))

            def before(g, k):
                if g == 2 * HALF:
                    pe.wait_ge(hid_lo, half * HALF + (hid0 + k + 1))

            linear(pe, key, [HALF] * KT, first + 2 * HALF, lambda g, k: (g_hi[:, k, 0:w], g_lo[:, k, 0:w]), w,
                   group0=2 * HALF, chunk_off=half * HALF_CHUNKS, group_off=half * HALF_GROUPS, before=before)

    def finished(chunk, together):
        return [] if chunk < together - 1 else list(range(together)) if chunk == together - 1 else [chunk]

    def act_ffn(act, n):
        i, m, _, hid0 = FFNS[n]
        w, key = ffn_width(n), ("ffn", n, 0)
        g0 = GROUPS_BEFORE[key]
        act_norm(act, i, m, w)
        with act.Fori(0, 2) as half:
            def high(f):
                act.wait_ge(groups_read, half * HALF_GROUPS + (g0 + 2 * f + 2))
                nc.scalar.copy(g_hi[:, f, 0:w], prod[:, f % 2, 0:w]).then_inc(hid_hi, 1)

            for j in range(HALF_CHUNKS):
                for g in finished(j, FFN_FIRST):
                    f = g // 2
                    if g >= 2 * HALF or g % 2:
                        continue
                    act.wait_ge(linear_done, half * MARKS + GROUP_DONE[key][g])
                    if f >= 2:
                        act.wait_ge(groups_read, half * HALF_GROUPS + (g0 + 2 * f - 2))
                    nc.scalar.activation(silu[:, f % 2, 0:w], bank[(g0 + g) % BANKS][:, 0:w],
                                         ACT.Silu).then_inc(gate_ready, 1)
                    if f:
                        high(f - 1)
                split_ahead(act, CH_FFN[n] + j + 1, mark_off=half * MARKS,
                            turn_off=half * (16 * HALF_CHUNKS // RING))
                if j == 2 * HALF - 1:
                    high(HALF - 1)

    def dve_residual(dve, key, g_first, gate, w, d, mark_off=0, group_off=0, squares=True):
        g = GROUPS_BEFORE[key] + g_first + d
        dve.wait_ge(linear_done, mark_off + GROUP_DONE[key][g_first + d])
        for c, s_ in sides(w):
            last = nc.vector.scalar_tensor_tensor(h[:, d, s_], bank[g % BANKS][:, s_], gates[:, gate, d, c:c + 1],
                                                  h[:, d, s_], ALU.mult, ALU.add)
        last.then_inc(groups_read, 1)
        if squares:
            dve.wait_ge(groups_read, group_off + (g + 1))
            dve_square(dve, d, slice(0, w))

    def dve_ffn(dve, n):
        i, m, gate, hid0 = FFNS[n]
        w, key = ffn_width(n), ("ffn", n, 0)
        g0 = GROUPS_BEFORE[key]
        dve_norm(dve, i, m, w)
        squares = n < 3
        steps = SQUARE_STEPS if squares else 0
        before = dve_count[0]
        with dve.Fori(0, 2) as half:
            dve_loop[0] = half * steps

            def low(f):
                dve.wait_ge(hid_hi, half * HALF + (hid0 + f + 1))
                nc.vector.tensor_tensor(g_lo[:, f, 0:w], prod[:, f % 2, 0:w], g_hi[:, f, 0:w].bitcast(F32),
                                        ALU.subtract).then_inc(hid_lo, 1)

            for f in range(HALF):
                g = g0 + 2 * f + 1
                dve.wait_ge(gate_ready, half * HALF + (hid0 + f + 1))
                dve.wait_ge(linear_done, half * MARKS + GROUP_DONE[key][2 * f + 1])
                if f >= 2:
                    dve.wait_ge(hid_lo, half * HALF + (hid0 + f - 1))
                nc.vector.tensor_tensor(prod[:, f % 2, 0:w], silu[:, f % 2, 0:w], bank[g % BANKS][:, 0:w],
                                        ALU.mult).then_inc(groups_read, 2)
                if f:
                    low(f - 1)
            low(HALF - 1)
            for d in range(KT):
                dve_residual(dve, key, 2 * HALF, gate, w, d, half * MARKS, half * HALF_GROUPS, squares)
        dve_loop[0] = 0
        assert dve_count[0] - before == steps
        dve_count[0] += steps

    def pe_sc(pe):
        i, m, _, hid0 = SC
        norm_sum(pe, m, T)
        norm_spread(pe, m, T)
        linear(pe, "sc", [Together(SC_FIRST, KT)] + [KT] * (24 - SC_FIRST), CH_SC,
               lambda g, k: (n_hi[:, k, :], n_lo[:, k, :]), T,
               before=pe_operands(pe, i))

        def before(g, k):
            if g == 24:
                pe.wait_ge(hid_lo, hid0 + k + 1)

        linear(pe, "sc", [KT] * KT, CH_SC + 24, lambda g, k: (g_hi[:, k, :], g_lo[:, k, :]), T, group0=24,
               before=before)

    def act_sc(act):
        i, m, _, hid0 = SC
        g0 = GROUPS_BEFORE["sc"]
        act_norm(act, i, m, T)

        def high(ct):
            act.wait_ge(groups_read, g0 + 3 * ct + 3)
            nc.scalar.copy(g_hi[:, ct, :], prod[:, ct % 2, :]).then_inc(hid_hi, 1)

        for j in range(N_SC):
            for g in finished(j, SC_FIRST):
                ct = g // 3
                if g >= 24 or g % 3:
                    continue
                act.wait_ge(linear_done, GROUP_DONE["sc"][g])
                if ct >= 2:
                    act.wait_ge(groups_read, g0 + 3 * ct - 4)
                nc.scalar.copy(silu[:, ct % 2, :], bank[(g0 + g) % BANKS][:]).then_inc(gate_ready, 1)
                if ct:
                    high(ct - 1)
            split_ahead(act, CH_SC + j + 1)
            if j == 23:
                high(KT - 1)

    def dve_sc(dve):
        i, m, gate, hid0 = SC
        g0 = GROUPS_BEFORE["sc"]
        dve_norm(dve, i, m, T)
        step(nc.vector.memset(sc_pad[:], 0.0))
        conv_view = sc_conv[:].rearrange("p (a t) -> p a t", a=2)

        def low(ct):
            dve.wait_ge(hid_hi, hid0 + ct + 1)
            nc.vector.tensor_tensor(g_lo[:, ct, :], prod[:, ct % 2, :], g_hi[:, ct, :].bitcast(F32),
                                    ALU.subtract).then_inc(hid_lo, 1)

        for ct in range(KT):
            dve.wait_ge(gate_ready, hid0 + ct + 1)
            dve.wait_ge(linear_done, GROUP_DONE["sc"][3 * ct + 1])
            nc.vector.tensor_tensor(sc_pad[:, ct % 2, :, 1:1 + L],
                                    silu[:, ct % 2, :].rearrange("p (a t) -> p a t", a=2),
                                    bank[(g0 + 3 * ct + 1) % BANKS][:].rearrange("p (a t) -> p a t", a=2),
                                    ALU.mult).then_inc(groups_read, 2)
            dve.wait_ge(groups_read, g0 + 3 * ct + 2)
            for tap in range(3):
                src, wt = sc_pad[:, ct % 2, :, tap:tap + L], col(Cols.SC_CONV + 3 * ct + tap)
                if tap == 0:
                    step(nc.vector.tensor_scalar(conv_view, src, wt, None, ALU.mult))
                else:
                    step(nc.vector.scalar_tensor_tensor(conv_view, src, wt, conv_view, ALU.mult, ALU.add))
            dve.wait_ge(linear_done, GROUP_DONE["sc"][3 * ct + 2])
            if ct >= 2:
                dve.wait_ge(hid_lo, hid0 + ct - 1)
            nc.vector.tensor_tensor(prod[:, ct % 2, :], sc_conv[:], bank[(g0 + 3 * ct + 2) % BANKS][:],
                                    ALU.mult).then_inc(groups_read, 1)
            if ct:
                low(ct - 1)
        low(KT - 1)
        for d in range(KT):
            dve_residual(dve, "sc", 24, gate, T, d)

    l_sq, l_summed, l_ms, l_rs, l_scaled, l_hi, l_lo = (
        sem(f"lora_{n}") for n in ("sq", "summed", "ms", "rs", "scaled", "hi", "lo"))
    h_sq, h_sq_used, h_summed, h_ms, h_rs, h_scaled = (
        sem(f"head_{n}") for n in ("sq", "sq_used", "summed", "ms", "rs", "scaled"))
    rope_t, rope_turned, rope_done = (sem(f"rope_{n}") for n in ("t", "turned", "done"))
    s_ready, s_max, s_exp, s_norm, s_turned, s_copied, s_out, s_out_hi, s_out_lo = (
        sem(f"att_{n}") for n in ("scores", "max", "exp", "norm", "turned", "copied", "out", "out_hi", "out_lo"))
    h_bc = sem("head_bc")
    q_raw = probs_t
    rope_sq = nt[:].rearrange("p a (b t) -> p (a b) t", b=2)
    rk_rows, rq_rows = a_rstd[0:HEADS, 0, :], a_rstd[0:HEADS, 1, 0:L]
    UQ, UK, UV, WO = 4, 16, 24, 32

    def tab(at, n=L):
        return rope[:, at:at + n]

    def mla_done(g):
        return GROUP_DONE["mla"][g]

    def pe_mla(pe):
        i, m, _, _ = MLA
        g0 = GROUPS_BEFORE["mla"]
        norm_sum(pe, m, T)
        norm_spread(pe, m, T)

        def latent_width(g):
            return L if g < 2 else T

        linear(pe, "mla", [Together(MLA_FIRST, KT)], CH_MLA,
               lambda g, k: (n_hi[:, k, 0:latent_width(g)], n_lo[:, k, 0:latent_width(g)]), latent_width,
               before=pe_operands(pe, i))
        pe.wait_ge(l_sq, 2)
        for j in range(2):
            last = nc.tensor.matmul(bank[MISC_BANK][:, 0:L], C(Const.ONES), a_sq[:, j, 0:L],
                                    start=(j == 0), stop=(j == 1))
        last.then_inc(l_summed, 1)
        pe.wait_ge(l_sq, 3)
        nc.tensor.matmul(bank[MOD_BANK][:], C(Const.ONES), a_sq[:, 2, :], start=True, stop=True)\
            .then_inc(l_summed, 1)
        def wait_lora(g, k):
            pe.wait_ge(l_lo, k + 1)

        def wait_kv(g, k):
            pe.wait_ge(l_lo, 3)

        linear(pe, "mla", [2] * 12, CH_MLA + 4, lambda g, k: (c_hi[:, k, 0:L], c_lo[:, k, 0:L]), L, group0=UQ,
               before=wait_lora)
        pe.wait_ge(rope_in_sem, 16)
        pe.wait_ge(rope_t, 1)
        pe.wait_ge(l_ms, 1)
        nc.tensor.matmul(bank[MISC_BANK][:, 0:L], tab(Rope.PERM, P), kr[:, 0:L], start=True, stop=True)\
            .then_inc(rope_turned, 1)

        linear(pe, "mla", [1] * 8, CH_MLA + 7, lambda g, k: (c_hi[:, 2, :], c_lo[:, 2, :]), T, group0=UK,
               before=wait_kv)
        pe.wait_ge(l_ms, 2)
        for j in range(4):
            pe.wait_ge(h_sq, j + 1)
            for e in range(2):
                hd = 2 * j + e
                last = nc.tensor.matmul(bank[MOD_BANK][0:HEADS, 0:L], col(Cols.SEL + 7 - hd, HEADS),
                                        a_sq[:, j % 2, e * L:(e + 1) * L], start=(hd == 0), stop=False)
            last.then_inc(h_summed, 1)
        pe.wait_ge(h_sq, 5)
        for j in range(4):
            last = nc.tensor.matmul(bank[MOD_BANK][0:HEADS, 0:L], tab(Rope.PAIR + 6 - 2 * j, HEADS), rope_sq[:, j, :],
                                    start=False, stop=(j == 3))
        last.then_inc(h_summed, 1)
        pe.wait_ge(rope_t, 2)
        for p in range(2):
            pe.wait_ge(rope_done, p + 1)
            nc.tensor.matmul(bank[MISC_BANK][:], tab(Rope.PERM, P), q_raw[:, 2 * p:2 * p + 2, :],
                             start=True, stop=True).then_inc(rope_turned, 1)
        chunk = CH_MLA + 8
        pe.wait_ge(w_lo_ready, chunk + 1)
        for vi in range(8):
            g, half, t = g0 + UV + vi, vi // 4, vi % 4
            pe.wait_ge(groups_read, g - BANKS + 1)
            out_ap = bank[g % BANKS][:]
            c_h, c_l = c_hi[:, 2, tok(t)], c_lo[:, 2, tok(t)]
            w_h, w_l = (w[:, chunk % RING, half * 512:(half + 1) * 512] for w in (w_hi, w_lo))
            nc.tensor.matmul(out_ap, c_h, w_l, start=True, stop=False)
            nc.tensor.matmul(out_ap, c_l, w_h, start=False, stop=False)
            nc.tensor.matmul(out_ap, c_h, w_h, start=False, stop=True).then_inc(linear_done, 1)
        pe.wait_ge(rope_done, 3)
        for hd in range(HEADS):
            pe.wait_ge(h_sq, 6 + hd)
            last = nc.tensor.matmul(bank[MISC_BANK][0:HEADS, :], col(Cols.SEL + 7 - hd, HEADS), a_sq[:, hd % 2, :],
                                    start=(hd == 0), stop=False)
            if hd < HEADS - 1:
                last.then_inc(h_summed, 1)
        nc.tensor.matmul(bank[MISC_BANK][0:HEADS, :], tab(Rope.SHARED, HEADS), a_sq[:, 2, :],
                         start=False, stop=True).then_inc(h_summed, 1)
        def scores(hd):
            for qt in range(2):
                b = bank[2 * (hd % 2) + qt]
                if hd >= 2:
                    pe.wait_ge(s_exp, 2 * (hd - 2) + qt + 1)
                nc.tensor.matmul(b[:], q_nope[:, hd, tok(qt)], k_nope[:, hd, :], start=True, stop=False)
                nc.tensor.matmul(b[:], q_rope[:, hd, tok(qt)], k_rope[:, hd // 2, :], start=False,
                                 stop=True).then_inc(s_ready, 1)

        pe.wait_ge(groups_read, g0 + WO)
        pe.wait_ge(h_rs, 1)
        for j in range(4):
            for e in range(2):
                hd = 2 * j + e
                last = nc.tensor.matmul(bank[j][:, e * L:(e + 1) * L],
                                        C(Const.IDENT, HEADS)[:, hd:hd + 1].to_broadcast([HEADS, P]),
                                        rq_rows, start=True, stop=True)
            last.then_inc(h_bc, 1)
        pe.wait_ge(h_rs, 2)
        for hd in range(HEADS):
            if hd >= 4:
                pe.wait_ge(h_scaled, 4 + hd - 3)
            nc.tensor.matmul(bank[4 + hd % 4][:], C(Const.IDENT, HEADS)[:, hd:hd + 1].to_broadcast([HEADS, P]),
                             rk_rows, start=True, stop=True).then_inc(h_bc, 1)
            if hd == 5:
                scores(0)
        pe.wait_ge(h_scaled, 12)
        for hd in range(HEADS):
            if hd + 1 < HEADS:
                scores(hd + 1)
            for pair in range(2):
                if hd:
                    pe.wait_ge(s_copied, 2 * (hd - 1) + pair + 1)
                for e in range(2):
                    for qt in range(2):
                        if pair == 0 and e == 0:
                            pe.wait_ge(s_norm, 2 * hd + qt + 1)
                        last = nc.tensor.transpose(bank[4 + pair][:, e * L + qt * P:e * L + (qt + 1) * P],
                                                   probs[:, qt, tok(2 * pair + e)], C(Const.IDENT))
                last.then_inc(s_turned, 1)
            if hd >= 2:
                pe.wait_ge(s_out_lo, hd - 1)
            for t in range(4):
                if t % 2 == 0:
                    pe.wait_ge(s_copied, 2 * hd + t // 2 + 1)
                last = nc.tensor.matmul(bank[6 + hd % 2][:, 0:L], v_att[:, t, hd, :], probs_t[:, t, :],
                                        start=(t == 0), stop=(t == 3))
            last.then_inc(s_out, 1)

        def wait_out(g, k):
            if g == WO:
                if k == 0:
                    pe.wait_ge(s_exp, 2 * HEADS)
                    pe.wait_ge(s_copied, 2 * HEADS)
                pe.wait_ge(s_out_lo, k + 1)

        linear(pe, "mla", [KT] * KT, CH_MLA + 9, lambda g, k: (n_hi[:, k, 0:L], n_lo[:, k, 0:L]), L, group0=WO,
               before=wait_out)

    def act_mla(act):
        i, m, _, _ = MLA
        g0 = GROUPS_BEFORE["mla"]
        act.wait_ge(groups_read, g0)
        act.dma_start(rope[:], rope_tab[:]).then_inc(rope_in_sem, 16)
        act_norm(act, i, m, T)

        def read(g, dest, w):
            act.wait_ge(linear_done, mla_done(g))
            nc.scalar.copy(dest, bank[(g0 + g) % BANKS][:, 0:w]).then_inc(groups_read, 1)

        for j in range(3):
            split_ahead(act, CH_MLA + j + 1)
        for j in range(4):
            read(j, (cq[:, 0, :], cq[:, 1, :], ckv[:], kr[:])[j], L if j < 2 else T)
        def latent(n, w, parts):
            act.wait_ge(l_ms, n + 1)
            nc.scalar.activation(a_rstd[:, n, 0:w], a_rstd[:, n, 0:w], ACT.Sqrt).then_inc(l_rs, 1)
            for j in parts:
                act.wait_ge(l_scaled, j + 1)
                nc.scalar.copy(c_hi[:, j, 0:w], (cq[:, 0, :], cq[:, 1, :], ckv[:])[j]).then_inc(l_hi, 1)

        latent(0, L, (0, 1))
        for j in range(3):
            split_ahead(act, CH_MLA + 4 + j)
            for g in range(4 * j, 4 * j + 4):
                read(UQ + g, q_nope[:, g, :] if g < HEADS else q_raw[:, g - HEADS, :], L)
            if j == 0:
                latent(1, T, (2,))
        split_ahead(act, CH_MLA + 7)
        for g in range(8):
            read(UK + g, k_nope[:, g, :], T)
        split_ahead(act, CH_MLA + 8)
        for vi in range(8):
            read(UV + vi, v_att[:, vi % 4, 4 * (vi // 4):4 * (vi // 4) + 4, :].rearrange("p a d -> p (a d)"), T)
        for j, rows in enumerate((rq_rows, rk_rows)):
            act.wait_ge(h_ms, j + 1)
            nc.scalar.activation(rows, rows, ACT.Sqrt).then_inc(h_rs, 1)
        scale = float(QK_HEAD) ** -0.5

        def softmax(hd):
            act.wait_ge(s_max, hd + 1)
            for qt in range(2):
                if hd:
                    act.wait_ge(s_turned, 2 * hd)
                nc.scalar.activation(probs[:, qt, :], bank[2 * (hd % 2) + qt][:], ACT.Exp, scale=scale,
                                     bias=smax[:, qt:qt + 1], accum_out=ssum[:, qt:qt + 1]).then_inc(s_exp, 1)

        def out_high(hd):
            act.wait_ge(s_out, hd + 1)
            nc.scalar.copy(n_hi[:, hd, 0:L], bank[6 + hd % 2][:, 0:L]).then_inc(s_out_hi, 1)

        for hd in range(HEADS):
            softmax(hd)
            if hd:
                out_high(hd - 1)
            act.wait_ge(s_turned, 2 * hd + 1)
            if hd:
                act.wait_ge(s_out, hd)
            nc.scalar.copy(probs_t[:, 0:2, :].rearrange("p a t -> p (a t)"), bank[4][:]).then_inc(s_copied, 1)
            act.wait_ge(s_turned, 2 * hd + 2)
            nc.scalar.copy(probs_t[:, 2:4, :].rearrange("p a t -> p (a t)"), bank[5][:]).then_inc(s_copied, 1)
        out_high(HEADS - 1)
        for j in range(9):
            split_ahead(act, CH_MLA + 9 + j)

    def dve_mla(dve):
        i, m, gate, _ = MLA
        g0 = GROUPS_BEFORE["mla"]
        dve_norm(dve, i, m, T)
        step(nc.vector.memset(q_rope[:], 0.0))
        lat = (cq[:, 0, :], cq[:, 1, :], ckv[:])
        for j in range(3):
            w = (L, L, T)[j]
            dve.wait_ge(groups_read, g0 + j + 1)
            nc.vector.tensor_tensor(a_sq[:, j, 0:w], lat[j], lat[j], ALU.mult).then_inc(l_sq, 1)

        def latent_mean(j):
            w, n, b = ((L, 2 * P, MISC_BANK), (T, P, MOD_BANK))[j]
            dve.wait_ge(l_summed, j + 1)
            step(nc.vector.tensor_scalar(a_rstd[:, j, 0:w], bank[b][:, 0:w], 1.0 / n, EPS, ALU.mult, ALU.add))
            nc.vector.reciprocal(a_rstd[:, j, 0:w], a_rstd[:, j, 0:w]).then_inc(l_ms, 1)

        def latent_scale(n, w, parts):
            dve.wait_ge(l_rs, n + 1)
            for j in parts:
                nc.vector.scalar_tensor_tensor(lat[j], lat[j], col((Cols.G_QA, Cols.G_QA + 1, Cols.G_KVA)[j]),
                                               a_rstd[:, n, 0:w], ALU.mult, ALU.mult).then_inc(l_scaled, 1)
            for j in parts:
                dve.wait_ge(l_hi, j + 1)
                nc.vector.tensor_tensor(c_lo[:, j, 0:w], lat[j], c_hi[:, j, 0:w].bitcast(F32),
                                        ALU.subtract).then_inc(l_lo, 1)

        latent_mean(0)
        latent_scale(0, L, (0, 1))
        latent_mean(1)
        latent_scale(1, T, (2,))
        dve.wait_ge(groups_read, g0 + 4)
        step(nc.vector.tensor_tensor(a_sq[:, 2, :], kr[:], kr[:], ALU.mult))
        nc.vector.tensor_scalar(kr[:], kr[:], col(Cols.G_K + 1), None, ALU.mult).then_inc(rope_t, 1)
        dve.wait_ge(rope_in_sem, 16)
        dve.wait_ge(rope_turned, 1)
        step(nc.vector.tensor_tensor(kr_rot[:, 0:L], bank[MISC_BANK][:, 0:L], tab(Rope.SIN), ALU.mult))
        step(nc.vector.tensor_tensor(rot[:, 0, :], kr[:, 0:L], tab(Rope.COS), ALU.mult))
        step(nc.vector.tensor_tensor(kr_rot[:, 0:L], kr_rot[:, 0:L], rot[:, 0, :], ALU.add))
        nc.vector.tensor_copy(kr_rot[:, L:T], kr[:, L:T]).then_inc(rope_done, 1)
        dve.wait_ge(rope_done, 1)
        for j in range(4):
            dve.wait_ge(groups_read, g0 + UQ + 2 * j + 2)
            if j >= 2:
                dve.wait_ge(h_summed, j - 1)
            qn = q_nope[:, 2 * j:2 * j + 2, :]
            nc.vector.tensor_tensor(a_sq[:, j % 2, :].rearrange("p (a t) -> p a t", a=2), qn, qn,
                                    ALU.mult).then_inc(h_sq, 1)
        dve.wait_ge(groups_read, g0 + UK)
        nc.vector.tensor_tensor(rope_sq, q_raw[:], q_raw[:], ALU.mult).then_inc(h_sq, 1)
        dve.wait_ge(h_sq, 5)
        nc.vector.tensor_scalar(q_raw[:], q_raw[:], col(Cols.G_Q + 1), None, ALU.mult).then_inc(rope_t, 1)
        for p in range(2):
            part = q_raw[:, 2 * p:2 * p + 2, :]
            turned = probs[:, p, :].rearrange("p (a t) -> p a t", a=2)
            dve.wait_ge(rope_turned, p + 2)
            nc.vector.tensor_tensor(turned, bank[MISC_BANK][:].rearrange("p (a t) -> p a t", a=2),
                                    tab(Rope.SIN).unsqueeze(1).to_broadcast([P, 2, L]), ALU.mult).then_inc(rope_done, 1)
            step(nc.vector.tensor_tensor(part, part, tab(Rope.COS).unsqueeze(1).to_broadcast([P, 2, L]), ALU.mult))
            dve.wait_ge(rope_done, p + 2)
            step(nc.vector.tensor_tensor(part, part, turned, ALU.add))

        def head_mean(rows, b, w, summed):
            dve.wait_ge(h_summed, summed)
            step(nc.vector.tensor_scalar(rows, bank[b][0:HEADS, 0:w], 1.0 / QK_HEAD, EPS, ALU.mult, ALU.add))
            nc.vector.reciprocal(rows, rows).then_inc(h_ms, 1)

        head_mean(rq_rows, MOD_BANK, L, 5)
        for hd in range(HEADS):
            dve.wait_ge(groups_read, g0 + UK + hd + 1)
            if hd >= 2:
                dve.wait_ge(h_summed, 5 + hd - 1)
            nc.vector.tensor_tensor(a_sq[:, hd % 2, :], k_nope[:, hd, :], k_nope[:, hd, :], ALU.mult).then_inc(h_sq, 1)
        head_mean(rk_rows, MISC_BANK, T, 13)
        for j in range(4):
            dve.wait_ge(h_bc, j + 1)
            qn, r_ = q_nope[:, 2 * j:2 * j + 2, :], bank[j]
            nc.vector.scalar_tensor_tensor(qn, qn, col(Cols.G_Q), r_[:].rearrange("p (a t) -> p a t", a=2),
                                           ALU.mult, ALU.mult)
            for e in range(2):
                s_ = slice(e * ROPE, (e + 1) * ROPE)
                last = nc.vector.tensor_tensor(q_rope[s_, 2 * j + e, :], q_raw[s_, j, :],
                                               r_[s_, e * L:(e + 1) * L], ALU.mult)
            last.then_inc(h_scaled, 1)
        for hd in range(HEADS):
            dve.wait_ge(h_bc, 4 + hd + 1)
            kn, r_ = k_nope[:, hd, :], bank[4 + hd % 4]
            nc.vector.scalar_tensor_tensor(kn, kn, col(Cols.G_K), r_[:], ALU.mult, ALU.mult)
            s_ = slice(hd % 2 * ROPE, (hd % 2 + 1) * ROPE)
            nc.vector.tensor_tensor(k_rope[s_, hd // 2, :], kr_rot[s_, :], r_[s_, :], ALU.mult).then_inc(h_scaled, 1)
        scale = float(QK_HEAD) ** -0.5

        def find_max(hd):
            if hd:
                dve.wait_ge(s_exp, 2 * hd)
            for qt in range(2):
                dve.wait_ge(s_ready, 2 * hd + qt + 1)
                step(nc.vector.tensor_reduce(smax[:, qt:qt + 1], bank[2 * (hd % 2) + qt][:], AX_X, ALU.max))
            nc.vector.tensor_scalar(smax[:], smax[:], -scale, None, ALU.mult).then_inc(s_max, 1)

        def normalise(hd):
            dve.wait_ge(s_exp, 2 * hd + 2)
            step(nc.vector.reciprocal(ssum[:], ssum[:]))
            for qt in range(2):
                nc.vector.tensor_scalar(probs[:, qt, :], probs[:, qt, :], ssum[:, qt:qt + 1], None,
                                        ALU.mult).then_inc(s_norm, 1)

        def out_low(hd):
            dve.wait_ge(s_out_hi, hd + 1)
            nc.vector.tensor_tensor(n_lo[:, hd, 0:L], bank[6 + hd % 2][:, 0:L], n_hi[:, hd, 0:L].bitcast(F32),
                                    ALU.subtract).then_inc(s_out_lo, 1)

        for hd in range(HEADS):
            find_max(hd)
            normalise(hd)
            if hd:
                out_low(hd - 1)
        out_low(HEADS - 1)
        for d in range(KT):
            dve_residual(dve, "mla", WO, gate, L, d)

    def store(sp):
        for d in range(KT):
            sp.wait_ge(groups_read, GROUPS_BEFORE[("ffn", 3, 1)] + 2 * HALF + d + 1)
            sp.dma_start(out[:, d, :], h[:, d, 0:L]).then_inc(out_done, 16)
        sp.wait_ge(out_done, 16 * KT)

    block = ctx.enter_context(nc.Block())

    @block.sync
    def _(sp):
        sp_program(sp)
        store(sp)

    @block.gpsimd
    def _(pool):
        pool_program(pool)

    @block.tensor
    def _(pe):
        pe_start(pe)
        pe_in(pe)
        pe_recur(pe)
        pe_out(pe)
        pe_ffn(pe, 0)
        pe_sc(pe)
        pe_ffn(pe, 1)
        pe_ffn(pe, 2)
        pe_mla(pe)
        pe_ffn(pe, 3)

    @block.scalar
    def _(act):
        act_start(act)
        act_in(act)
        act_recur(act)
        act_out_stage(act)
        act_ffn(act, 0)
        act_sc(act)
        act_ffn(act, 1)
        act_ffn(act, 2)
        act_mla(act)
        act_ffn(act, 3)

    @block.vector
    def _(dve):
        dve_start(dve)
        dve_in(dve)
        dve_recur(dve)
        dve_out(dve)
        dve_ffn(dve, 0)
        dve_sc(dve)
        dve_ffn(dve, 1)
        dve_ffn(dve, 2)
        dve_mla(dve)
        dve_ffn(dve, 3)

    ctx.close()


def _tiles(w):
    k, n = w.shape
    return w.reshape(k // P, P, n // P, P).transpose(2, 0, 1, 3)


def _chunks(tiles):
    t = np.concatenate([x.reshape(-1, P, P) for x in tiles])
    return t.reshape(-1, TILES_PER_CHUNK, P, P).transpose(0, 2, 1, 3).reshape(-1, P, CHUNK)


def _together(tiles, n):
    return np.concatenate([x.reshape(-1, P, P) for x in (tiles[:n].swapaxes(0, 1), tiles[n:])])


def lay_out(i):
    f = np.float32
    w_in = i["w_in"][0]
    o = np.cumsum([0, 3 * D, 32, D, D, D])
    wq, wk, wv = w_in[:, 0:D], w_in[:, D:2 * D], w_in[:, 2 * D:3 * D]
    wab, wz, wu, wzp = (w_in[:, o[n]:o[n + 1]] for n in range(1, 5))
    ab = np.zeros((D, P), f)
    ab[:, 0:16], ab[:, 32:48] = wab[:, 0:16], wab[:, 16:32]
    pool = np.stack([_tiles(i["pool_w"][0, g]) for g in range(4)])
    first = np.concatenate([_tiles(ab), _tiles(wk)])
    tail = {"u": _tiles(wu), "z_dn": _tiles(wz), "z_pool": _tiles(wzp), "pool": pool.reshape(2, 8, P, P)}
    seq = [_together(first, IN_FIRST), _tiles(wv), _tiles(wq)] + [tail[kind][n] for kind, n in IN_TAIL]
    seq.append(_together(_tiles(i["w_out"][0])[:, OUT_ORDER], OUT_FIRST))

    def ffn(layer, n):
        t1, t3 = _tiles(i["ffn_w1_2"][layer, n]), _tiles(i["ffn_w3_2"][layer, n])
        t2 = _tiles(i["ffn_w2_2"][layer, n])
        for half in range(2):
            a = slice(half * HALF, (half + 1) * HALF)
            seq.append(_together(np.stack([t1[a], t3[a]], axis=1).reshape(2 * HALF, KT, P, P), FFN_FIRST))
            seq.append(t2[:, a])

    ffn(0, 0)
    t = _tiles(i["sc_w_in_2"][0])
    seq.append(_together(np.stack([t[8:16], t[16:24], t[0:8]], axis=1).reshape(24, KT, P, P), SC_FIRST))
    seq.append(_tiles(i["sc_w_out_2"][0]))
    ffn(0, 1)
    ffn(1, 0)
    wa = i["mla_w_a_2"][0]
    wa = np.concatenate([wa, wa[:, 384:448]], axis=1)
    uq = i["mla_w_uq_2"][0].reshape(256, HEADS, QK_HEAD)
    uq = np.concatenate([uq[:, :, :NOPE].reshape(256, -1), uq[:, :, NOPE:].reshape(256, -1)], axis=1)
    ukv = i["mla_w_ukv_2"][0].reshape(P, HEADS, 2, P)
    seq += [_together(_tiles(wa), MLA_FIRST), _tiles(uq), _tiles(ukv[:, :, 0].reshape(P, -1)),
            _tiles(ukv[:, :, 1].reshape(P, -1)), _tiles(i["mla_w_o_2"][0])]
    ffn(1, 1)
    seq.append(np.zeros(((N_STREAM - N_CHUNKS) * TILES_PER_CHUNK, P, P), f))
    stream = _chunks(seq)
    assert stream.shape[0] == N_STREAM

    wm = np.concatenate([i["w_mod"][0], i["w_mod_2"][0], i["w_mod_2"][1],
                         np.zeros((D, MOD_GROUPS * MOD_COLS - 21 * D), f)], axis=1)
    modstream = wm.reshape(KT, P, MOD_GROUPS, 2, CHUNK).transpose(2, 0, 3, 1, 4).reshape(-1, P, CHUNK)

    def feat(a):
        return a.T.reshape(KT, P, -1).transpose(1, 0, 2)

    tokens = np.concatenate([feat(i["x"][0]), feat(i["ctx"][0])], axis=2)
    ctx2 = feat(i["ctx_2"][0])
    conds = np.zeros((P, 2, KT, 32), f)
    for b, (c, cc) in enumerate(((i["c"][0], i["c_ctx"]), (i["c_2"][0], i["c_ctx_2"]))):
        conds[:, b, :, 0] = c.reshape(KT, P).T
        conds[:, b, :, 1] = cc.reshape(KT, P).T
    cols = np.zeros((P, Cols.N), f)

    def put(at, v):
        v = np.asarray(v).reshape(-1, P).T
        cols[:, at:at + v.shape[1]] = v

    put(Cols.NORM_GAIN, i["norm_gain"][0])
    put(Cols.FINAL_GAIN, i["final_gain"])
    put(Cols.G_NORM, i["g_norm_2"])
    put(Cols.POOL_SCALE, i["pool_scale"][0])
    put(Cols.DN_GAIN, i["dn_norm_gain"][0])
    cw = i["conv_w"][0].reshape(CONV, 3, KT, P)[:, [1, 2, 0]]
    put(Cols.CONV, cw.transpose(1, 2, 0, 3))
    put(Cols.SC_CONV, i["sc_conv_2"][0].reshape(3, KT, P).transpose(1, 0, 2))
    put(Cols.G_QA, i["mla_g_qa_2"][0])
    put(Cols.G_KVA, i["mla_g_kva_2"][0])
    for at, g in ((Cols.G_Q, i["mla_g_q_2"][0]), (Cols.G_K, i["mla_g_k_2"][0])):
        put(at, np.concatenate([g, g[NOPE:]]))
    cols[0:16, Cols.A_LOG] = i["a_log"][0].reshape(-1)
    cols[0:16, Cols.DT_BIAS] = i["dt_bias"][0].reshape(-1)
    put(Cols.BIAS, np.concatenate([i["b_mod"][0], i["b_mod_2"].reshape(-1),
                                   np.zeros(MOD_GROUPS * MOD_COLS - 21 * D, f)]))

    cols[:, Cols.SEL + 7] = 1
    consts = np.zeros((P, Const.N, P), f)
    r, c = np.arange(P)[:, None], np.arange(P)[None, :]
    consts[:, Const.IDENT] = r == c
    consts[:, Const.ONES] = 1
    for d in (FWD, BWD):
        lower = (c < r) if d == FWD else (c > r)
        consts[:, Const.STRICT[d]] = lower
        consts[:, Const.INCL[d]] = (r <= c) if d == FWD else (r >= c)
        for n, b in enumerate(LEVELS):
            consts[:, Const.LEVEL[d] + n] = lower & (r // (2 * b) == c // (2 * b)) & (r // b != c // b)
    n_freq = ROPE // 4
    inv = (f(10000.0) ** (-np.arange(n_freq, dtype=f) / n_freq)).astype(f)
    tok = np.arange(L)
    ang = np.stack([(tok // GRID_W).astype(f)[:, None] * inv, (tok % GRID_W).astype(f)[:, None] * inv], axis=1)
    ang = np.repeat(ang[:, :, None, :], 2, axis=2).reshape(L, ROPE).T
    ang = np.concatenate([ang, ang])
    rope = np.zeros((P, Rope.N), f)
    rope[:, Rope.COS:Rope.COS + L], rope[:, Rope.SIN:Rope.SIN + L] = np.cos(ang), np.sin(ang)
    rope[:ROPE, Rope.PAIR + 6] = rope[ROPE:, Rope.PAIR + 7] = 1
    rope[:ROPE, Rope.SHARED:Rope.SHARED + HEADS] = 1
    partner = np.where(c % 32 < 16, c + 16, c - 16)
    rope[:, Rope.PERM:Rope.PERM + P] = np.where(r == partner, np.where(c % 32 < 16, -1.0, 1.0), 0.0)
    gc = np.arange(GRID_W)
    counts = np.zeros((P, 4, GRID_W), f)
    for n, w in enumerate(WINDOWS):
        counts[:, n] = 1.0 / (np.clip(gc - w // 2 + w, 0, GRID_W) - np.clip(gc - w // 2, 0, GRID_W))
    named = dict(stream=stream, modstream=modstream, tokens=tokens, ctx2=ctx2, conds=conds, cols=cols,
                 consts=consts, rope=rope, counts=counts)
    return {k: np.ascontiguousarray(v) for k, v in named.items()}


def kernel(**inputs):
    import concourse.bacc as bacc
    from concourse.bass_utils import run_bass_kernel_spmd

    arrays = lay_out({k: np.asarray(v) for k, v in inputs.items()})
    nc = bacc.Bacc("TRN2", target_bir_lowering=False, num_devices=1)
    args = [nc.dram_tensor("in_" + k, v.shape, F32, kind="ExternalInput").ap() for k, v in arrays.items()]
    out = nc.dram_tensor("out", (P, KT, L), F32, kind="ExternalOutput").ap()
    two_block_kernel(nc, *args, out)
    r = run_bass_kernel_spmd(nc, [{"in_" + k: v for k, v in arrays.items()}], core_ids=[0])
    return r.results[0]["out"].transpose(2, 1, 0).reshape(1, L, D)
```
